# Optimizing a Trainium2 kernel written in Bass

```python
import jax, jax.numpy as jnp
from jax import lax
import numpy as np

D_MODEL = 1024
BATCH = 1
SEQ = 256
DEPTH = 2

N_MIXERS = 2
N_CONV_LAYERS = (DEPTH + 1) // 2
N_LRU_LAYERS = DEPTH // 2
CONF_KERNEL = 31
D_RNN = D_MODEL
LRU_HEADS = 4
LRU_HEAD_DIM = D_RNN // LRU_HEADS
LRU_CONV = 4
LRU_C = 8.0
N_GROUPS = 4
EXPERTS_PER_GROUP = 8
N_EXPERTS = N_GROUPS * EXPERTS_PER_GROUP
TOP_K = 2
D_EXPERT = 512
ROW_BLOCK = 256
EPS = 1e-6

kernel_name = "hybrid_conformer_rglru_hmoe_adaln"

def rmsnorm(x, g):
    x32 = x.astype(jnp.float32)
    y = x32 * lax.rsqrt(jnp.mean(x32 * x32, axis=-1, keepdims=True) + EPS)
    return (y * g.astype(jnp.float32)).astype(x.dtype)

def modulate(h, shift, scale):
    return h * (1 + scale[:, None, :]) + shift[:, None, :]

def causal_depthwise_conv(x, w, b):
    k = w.shape[0]
    y = lax.conv_general_dilated(
        x, w[:, None, :].astype(x.dtype), window_strides=(1,),
        padding=[(k - 1, 0)], dimension_numbers=("NWC", "WIO", "NWC"),
        feature_group_count=x.shape[-1])
    return y + b

def conformer_conv(h, w1, b1, dw, dwb, ln_g, ln_b, w2, b2):
    u = h @ w1 + b1
    a, g = jnp.split(u, 2, axis=-1)
    v = a * jax.nn.sigmoid(g)
    v = causal_depthwise_conv(v, dw, dwb)
    v32 = v.astype(jnp.float32)
    mu = jnp.mean(v32, axis=-1, keepdims=True)
    var = jnp.mean(jnp.square(v32 - mu), axis=-1, keepdims=True)
    v = ((v32 - mu) * lax.rsqrt(var + EPS) * ln_g.astype(jnp.float32)
         + ln_b.astype(jnp.float32)).astype(h.dtype)
    v = jax.nn.silu(v)
    return v @ w2 + b2

def _lin_combine(left, right):
    a_l, b_l = left
    a_r, b_r = right
    return a_l * a_r, a_r * b_l + b_r

def rglru_block(h, wy, by, wx, bx, cw, cb, wa, ba, wi, bi, lam, wo, bo):
    bsz, s, _ = h.shape
    y = jax.nn.gelu(h @ wy + by)
    u = causal_depthwise_conv(h @ wx + bx, cw, cb)
    uh = u.reshape(bsz, s, LRU_HEADS, LRU_HEAD_DIM)
    r = jax.nn.sigmoid(jnp.einsum("bshi,hij->bshj", uh, wa) + ba).reshape(bsz, s, D_RNN)
    ig = jax.nn.sigmoid(jnp.einsum("bshi,hij->bshj", uh, wi) + bi).reshape(bsz, s, D_RNN)
    log_a = -LRU_C * r.astype(jnp.float32) * jax.nn.softplus(-lam.astype(jnp.float32))
    a = jnp.exp(log_a)
    mult = jnp.sqrt(-jnp.expm1(2.0 * log_a))
    b_term = mult * (ig * u).astype(jnp.float32)
    _, hs = lax.associative_scan(_lin_combine, (a, b_term), axis=1)
    return (hs.astype(h.dtype) * y) @ wo + bo

def hier_moe(h, wg, bg, wr, br, w_gate, w_up, w_down):
    bsz, s, d = h.shape
    t = bsz * s
    ht = h.reshape(t, d)
    glog = (ht @ wg + bg).astype(jnp.float32)
    gprob = jax.nn.softmax(glog, axis=-1)
    g_sel = jnp.argmax(glog, axis=-1).astype(jnp.int32)
    p_g = jnp.take_along_axis(gprob, g_sel[:, None], axis=1)[:, 0]
    elog_all = (ht @ wr + br).astype(jnp.float32).reshape(t, N_GROUPS, EXPERTS_PER_GROUP)
    elog = jnp.take_along_axis(elog_all, g_sel[:, None, None], axis=1)[:, 0]
    top_v, top_i = lax.top_k(elog, TOP_K)
    gate_w = jax.nn.softmax(top_v, axis=-1) * p_g[:, None]
    eid = (g_sel[:, None] * EXPERTS_PER_GROUP + top_i).reshape(-1).astype(jnp.int32)
    gates = gate_w.reshape(-1)
    tok = jnp.repeat(jnp.arange(t, dtype=jnp.int32), TOP_K)
    n_assign = t * TOP_K
    order = jnp.argsort(eid)
    s_eid, s_tok, s_gate = eid[order], tok[order], gates[order]
    counts = jax.ops.segment_sum(jnp.ones_like(eid), eid, num_segments=N_EXPERTS)
    starts = jnp.cumsum(counts) - counts
    padded = ((counts + ROW_BLOCK - 1) // ROW_BLOCK) * ROW_BLOCK
    pends = jnp.cumsum(padded)
    pstarts = pends - padded
    dest = pstarts[s_eid] + (jnp.arange(n_assign, dtype=jnp.int32) - starts[s_eid])
    n_blocks = -(-n_assign // ROW_BLOCK) + N_EXPERTS
    n_rows = n_blocks * ROW_BLOCK
    row_tok = jnp.full((n_rows,), t, jnp.int32).at[dest].set(s_tok)
    row_gate = jnp.zeros((n_rows,), h.dtype).at[dest].set(s_gate.astype(h.dtype))
    block_eid = jnp.minimum(
        jnp.searchsorted(pends, jnp.arange(n_blocks, dtype=jnp.int32) * ROW_BLOCK, side="right"),
        N_EXPERTS - 1).astype(jnp.int32)
    ht_pad = jnp.concatenate([ht, jnp.zeros((1, d), ht.dtype)], axis=0)

    def run_block(args):
        idx, e = args
        xb = ht_pad[idx]
        hid = jax.nn.silu(xb @ w_gate[e]) * (xb @ w_up[e])
        return hid @ w_down[e]

    y_rows = lax.map(run_block, (row_tok.reshape(n_blocks, ROW_BLOCK), block_eid))
    y_rows = y_rows.reshape(n_rows, d) * row_gate[:, None]
    y = jnp.zeros((t + 1, d), h.dtype).at[row_tok].add(y_rows)[:t]
    return y.reshape(bsz, s, d)

def setup_inputs(seed: int = 0) -> dict:
    key = jax.random.key(seed)
    ks = iter(jax.random.split(key, 64))
    f32 = jnp.float32

    def nrm(shape, scale):
        return jax.random.normal(next(ks), shape, f32) * scale

    def gain(shape):
        return 1.0 + 0.02 * jax.random.normal(next(ks), shape, f32)

    D, DR, NA, NB = D_MODEL, D_RNN, N_CONV_LAYERS, N_LRU_LAYERS
    s_lam = jax.random.uniform(next(ks), (NB, DR), f32, 0.9, 0.999) ** (1.0 / LRU_C)
    return {
        "x": jax.random.normal(next(ks), (BATCH, SEQ, D), f32),
        "c": jax.random.normal(next(ks), (BATCH, D), f32),
        "ada_w": nrm((DEPTH, D, 6 * D), D ** -0.5),
        "ada_b": nrm((DEPTH, 6 * D), 0.01),
        "norm1_g": gain((DEPTH, D)),
        "norm2_g": gain((DEPTH, D)),
        "cm_w1": nrm((NA, D, 2 * D), D ** -0.5),
        "cm_b1": nrm((NA, 2 * D), 0.01),
        "cm_dw": nrm((NA, CONF_KERNEL, D), CONF_KERNEL ** -0.5),
        "cm_dwb": nrm((NA, D), 0.01),
        "cm_ln_g": gain((NA, D)),
        "cm_ln_b": nrm((NA, D), 0.01),
        "cm_w2": nrm((NA, D, D), D ** -0.5),
        "cm_b2": nrm((NA, D), 0.01),
        "rg_wy": nrm((NB, D, DR), D ** -0.5),
        "rg_by": nrm((NB, DR), 0.01),
        "rg_wx": nrm((NB, D, DR), D ** -0.5),
        "rg_bx": nrm((NB, DR), 0.01),
        "rg_cw": nrm((NB, LRU_CONV, DR), LRU_CONV ** -0.5),
        "rg_cb": nrm((NB, DR), 0.01),
        "rg_wa": nrm((NB, LRU_HEADS, LRU_HEAD_DIM, LRU_HEAD_DIM), LRU_HEAD_DIM ** -0.5),
        "rg_ba": nrm((NB, LRU_HEADS, LRU_HEAD_DIM), 0.01),
        "rg_wi": nrm((NB, LRU_HEADS, LRU_HEAD_DIM, LRU_HEAD_DIM), LRU_HEAD_DIM ** -0.5),
        "rg_bi": nrm((NB, LRU_HEADS, LRU_HEAD_DIM), 0.01),
        "rg_lambda": jnp.log(s_lam) - jnp.log1p(-s_lam),
        "rg_wo": nrm((NB, DR, D), DR ** -0.5),
        "rg_bo": nrm((NB, D), 0.01),
        "moe_wg": nrm((DEPTH, D, N_GROUPS), D ** -0.5),
        "moe_bg": nrm((DEPTH, N_GROUPS), 0.01),
        "moe_wr": nrm((DEPTH, D, N_EXPERTS), D ** -0.5),
        "moe_br": nrm((DEPTH, N_EXPERTS), 0.01),
        "moe_w_gate": nrm((DEPTH, N_EXPERTS, D, D_EXPERT), D ** -0.5),
        "moe_w_up": nrm((DEPTH, N_EXPERTS, D, D_EXPERT), D ** -0.5),
        "moe_w_down": nrm((DEPTH, N_EXPERTS, D_EXPERT, D), D_EXPERT ** -0.5),
        "fin_ada_w": nrm((D, 2 * D), D ** -0.5),
        "fin_ada_b": nrm((2 * D,), 0.01),
        "fin_g": gain((D,)),
    }

def reference(x, c, ada_w, ada_b, norm1_g, norm2_g,
              cm_w1, cm_b1, cm_dw, cm_dwb, cm_ln_g, cm_ln_b, cm_w2, cm_b2,
              rg_wy, rg_by, rg_wx, rg_bx, rg_cw, rg_cb, rg_wa, rg_ba, rg_wi, rg_bi,
              rg_lambda, rg_wo, rg_bo,
              moe_wg, moe_bg, moe_wr, moe_br, moe_w_gate, moe_w_up, moe_w_down,
              fin_ada_w, fin_ada_b, fin_g):
    c_act = jax.nn.silu(c)
    for i in range(DEPTH):
        mod = c_act @ ada_w[i] + ada_b[i]
        sh1, sc1, g1, sh2, sc2, g2 = jnp.split(mod, 6, axis=-1)
        h = modulate(rmsnorm(x, norm1_g[i]), sh1, sc1)
        j = i // N_MIXERS
        if i % N_MIXERS == 0:
            m = conformer_conv(h, cm_w1[j], cm_b1[j], cm_dw[j], cm_dwb[j],
                               cm_ln_g[j], cm_ln_b[j], cm_w2[j], cm_b2[j])
        else:
            m = rglru_block(h, rg_wy[j], rg_by[j], rg_wx[j], rg_bx[j], rg_cw[j], rg_cb[j],
                            rg_wa[j], rg_ba[j], rg_wi[j], rg_bi[j], rg_lambda[j],
                            rg_wo[j], rg_bo[j])
        x = x + g1[:, None, :] * m
        h = modulate(rmsnorm(x, norm2_g[i]), sh2, sc2)
        x = x + g2[:, None, :] * hier_moe(h, moe_wg[i], moe_bg[i], moe_wr[i], moe_br[i],
                                          moe_w_gate[i], moe_w_up[i], moe_w_down[i])
    fsh, fsc = jnp.split(c_act @ fin_ada_w + fin_ada_b, 2, axis=-1)
    return modulate(rmsnorm(x, fin_g), fsh, fsc)


_drawn_inputs = setup_inputs


def setup_inputs(seed=0):
    import zlib

    import numpy as np

    out = dict(_drawn_inputs(seed))
    spreads = {}
    factors = {'cm_b1': 7.818,
     'cm_dwb': 3.593,
     'cm_ln_b': 3.686,
     'cm_b2': 4.866,
     'rg_by': 8.0,
     'rg_bx': 3.752,
     'rg_cb': 3.079,
     'rg_ba': 8.0,
     'rg_bi': 8.0,
     'rg_bo': 8.0,
     'moe_bg': 4.451,
     'moe_br': 4.536,
     'fin_ada_b': 5.644,
     'fin_g': 2.974}
    for name, (base, spread) in spreads.items():
        noise = np.random.default_rng([zlib.crc32(name.encode()), seed]).standard_normal(out[name].shape)
        drawn = base * np.exp(spread * noise) if base else spread * noise
        out[name] = __import__('jax').numpy.asarray(drawn.astype(out[name].dtype))
    for name, factor in factors.items():
        out[name] = (out[name] * factor).astype(out[name].dtype)
    return out
```

```python
from contextlib import ExitStack

import concourse.bass as bass
from concourse import mybir

F32 = mybir.dt.float32
I32 = mybir.dt.int32
ALU = mybir.AluOpType
ACT = mybir.ActivationFunctionType
AX = mybir.AxisListType

P = 128
T = 256
TT = T // P
D = 1024
DC = D // P
EPS = 1e-6
TAPS = 31
LTAPS = 4
HEADS = 4
NG, NE = 4, 32
EPG = NE // NG
F = 512
FC = F // P
SLOTS = 64
NSUB = P // SLOTS
MAXB = NE + (2 * T - NE) // SLOTS
MAXP = -(-MAXB // NSUB)
BIG = 1e30
GELU_A, GELU_B = 0.044715, 1.5957691216057308

PAR_A = {"n1": 0, "n2": 16, "fin": 32, "b1": 40, "dwb": 56, "lng": 64, "lnb": 72, "b2": 80, "c": 88}
PAR_B = {"by": 128, "bx": 136, "cb": 144, "ba": 152, "bi": 160, "lam": 168, "bo": 176, "cw": 184}
PAR_ADA = 256
PAR_DW = 384
DW_ROWS = TAPS * DC // 2
PAR_TILES = [96, 88, 112, DW_ROWS, DW_ROWS]


def dw_col(k, c):
    r = k * DC + c
    return PAR_DW + (r if r < DW_ROWS else P + r - DW_ROWS)


class Link:

    def __init__(self, eng, sem, base=0):
        self.eng, self.sem, self.base, self.n = eng, sem, base, 0

    def __call__(self, ins):
        self.n += 1
        ins.then_inc(self.sem, 1)
        self.eng.wait_ge(self.sem, self.base + self.n)


def trunk(nc, x, c, ada_w, ada_b, norm1_g, norm2_g, cm_w1, cm_b1, cm_dw, cm_dwb, cm_ln_g, cm_ln_b,
          cm_w2, cm_b2, rg_wy, rg_by, rg_wx, rg_bx, rg_cw, rg_cb, rg_wa, rg_ba, rg_wi, rg_bi,
          rg_lambda, rg_wo, rg_bo, moe_wg, moe_bg, moe_wr, moe_br, moe_w_gate, moe_w_up,
          moe_w_down, fin_ada_w, fin_ada_b, fin_g, out):
    ctx = ExitStack()
    with ctx:
        def sb(name, shape, dt=F32):
            return ctx.enter_context(nc.sbuf_tensor(name, shape, dt))

        def sem(name):
            return ctx.enter_context(nc.semaphore(name))

        ps = ctx.enter_context(nc.psum_tensor("ps", [P, 8, 512], F32))

        wbuf = sb("wbuf", [P, 24 * 1024])
        adabuf = sb("adabuf", [P, 2, 4, D])
        wab = sb("wab", [P, 2, HEADS, 2, 256])
        X = sb("X", [P, DC, T])
        H = sb("H", [P, DC, T])
        B = sb("B", [P, DC, T])
        C = sb("C", [P, DC, T])
        Dd = sb("Dd", [P, DC, T])
        V = sb("V", [P, DC * (T + TAPS - 1)])
        sg = sb("sg", [P, 2, T])
        rowsum = wab[:, 0, 0:2, :, :].rearrange("p h i j -> p (h i j)")
        par = sb("par", [P, 5 * P])
        mod = sb("mod", [P, 14 * DC])
        wgr = sb("wgr", [P, 2, DC, NG + NE])
        brow = sb("brow", [1, 2, NG + NE])
        cb32 = sb("cb32", [P, DC, 32])
        rs = sb("rs", [P, T])
        gs = sb("gs", [P, DC])
        small = sb("small", [P, 8, DC])
        ident = sb("ident", [P, P])
        onesd = sb("onesd", [P, P])
        ones = sb("ones", [P, P])
        upper = sb("upper", [P, P])
        sel = sb("sel", [P, 1])
        iota0 = sb("iota0", [P, P])
        iota1 = sb("iota1", [P, P])
        rev = sb("rev", [P, NE])
        blk = sb("blk", [P, 2 * MAXP])
        thr = sb("thr", [P, T // SLOTS])
        lg = sb("lg", [P, TT, NG + NE])
        r4 = sb("r4", [P, 3, TT, NG])
        r1 = sb("r1", [P, 16, TT])
        cnt = sb("cnt", [P, 4, NE])
        cmp3 = C[:, 0:5, :].rearrange("p c t -> p (c t)").rearrange("p (b e) -> p b e", e=NE)
        dflat = Dd[:, :, :].rearrange("p c t -> p (c t)")
        r32 = dflat[:, 0:6 * TT * NE].rearrange("p (i a e) -> p i a e", i=6, a=TT)
        dfree = 6 * TT * NE
        tabf = sb("tabf", [P, 2 * MAXP + 1])
        tab = sb("tab", [1, 2 * MAXP + 4], I32)
        gslot = sb("gslot", [P, 2, TT])
        gw = sb("gw", [P, 2, TT])
        pick, gate1, gate2 = (dflat[:, dfree + i * TT * P:dfree + (i + 1) * TT * P].rearrange("p (a s) -> p a s", a=TT)
                              for i in range(3))
        scat = sg[:, 0, :]

        w1 = wbuf[:, 0:16384].rearrange("p (k n) -> p k n", k=DC)
        w2 = wbuf[:, 16384:24576].rearrange("p (k n) -> p k n", k=DC)
        rgw = [wbuf[:, i * 8192:(i + 1) * 8192].rearrange("p (k n) -> p k n", k=DC) for i in range(3)]
        vconf = V[:, :].rearrange("p (c t) -> p c t", c=DC)
        vlru = V[:, 0:DC * (T + LTAPS - 1)].rearrange("p (c t) -> p c t", c=DC)
        vflat = V[:, 0:DC * T].rearrange("p (c t) -> p c t", c=DC)
        htok = B[:, :, :].rearrange("p (a c) t -> p a (c t)", a=TT)
        xg = C[:, 0:4, :].rearrange("p c t -> p (c t)").rearrange("p (k s) -> p k s", k=DC)
        hid = V[:, 0:F]
        hidT = V[:, F:2 * F].rearrange("p (c s) -> p c s", c=FC)
        dn = V[:, 2 * F:2 * F + D]
        sigb = C[:, 4:6, :].rearrange("p c t -> p (c t)")
        xin = wbuf[:, 0:TT * D].rearrange("p (a d) -> p a d", a=TT)
        ptile = [adabuf[:, 0, i // 2, (i % 2) * P:(i % 2) * P + P] for i in range(4)] + [
            adabuf[:, 0, 2, 0:P]]
        ptile = [C[:, i, 0:P] for i in range(5)]

        s_x = sem("s_x")
        s_par = [sem(f"s_par{i}") for i in range(5)]
        s_router = sem("s_router")
        s_w1, s_w2 = sem("s_w1"), sem("s_w2")
        s_wx, s_wy, s_wo, s_wab = sem("s_wx"), sem("s_wy"), sem("s_wo"), sem("s_wab")
        ada_landed = [sem("ada_landed0"), sem("ada_landed1")]
        ada_used = sem("ada_used")
        consts = sem("consts")
        pool_link = sem("pool_link")
        act_link = sem("act_link")
        dve_link = sem("dve_link")
        sel_ready = sem("sel_ready")
        par_mm, par_ready = sem("par_mm"), sem("par_ready")
        x_mm, x_ready = sem("x_mm"), sem("x_ready")
        csig, cact = sem("csig"), sem("cact")
        rows_ready, cols_mm, mod_ready = sem("rows_ready"), sem("cols_mm"), sem("mod_ready")
        sq_ready, ms_mm, xn_ready, h_ready = sem("sq_ready"), sem("ms_mm"), sem("xn_ready"), sem("h_ready")
        gs_ready = sem("gs_ready")
        inv_ready, root_ready, ln_inv, ln_root = sem("inv_ready"), sem("root_ready"), sem("ln_inv"), sem("ln_root")
        b2_ready, b_ready = sem("b2_ready"), sem("b_ready")
        glu_mm, sg_ready, v_ready = sem("glu_mm"), sem("sg_ready"), sem("v_ready")
        pad_ready = sem("pad_ready")
        conv_dve = sem("conv_dve")
        mean_mm, cen_ready, csq_ready, var_mm, z_ready = sem("mean_mm"), sem("cen_ready"), sem("csq_ready"), sem("var_mm"), sem("z_ready")
        zs_ready, act_in = sem("zs_ready"), sem("act_in")
        o_mm, o_ready = sem("o_mm"), sem("o_ready")
        gb_ready = sem("gb_ready")
        mixer_read = sem("mixer_read")
        ux_mm, ux_ready, u_ready = sem("ux_mm"), sem("ux_ready"), sem("u_ready")
        q_mm, q_ready, g_in, g_sig, y_ready = sem("q_mm"), sem("q_ready"), sem("g_in"), sem("g_sig"), sem("y_ready")
        gate_mm, rg_ready, ta_ready, nk_in, nk_exp, nk_ln, nk_ready = (sem(n) for n in (
            "gate_mm", "rg_ready", "ta_ready", "nk_in", "nk_exp", "nk_ln", "nk_ready"))
        hs_ready = sem("hs_ready")
        lg_mm, ge_in, ge_ready, mask_ready, rank_mm, route_ready = (sem(n) for n in (
            "lg_mm", "ge_in", "ge_ready", "mask_ready", "rank_mm", "route_ready"))
        ht_mm, ht_dve, ht_act = sem("ht_mm"), sem("ht_dve"), sem("ht_act")
        moe_zero = sem("moe_zero")
        fin_mm, s_out = sem("fin_mm"), sem("s_out")

        class Moe:
            def __init__(self, l):
                def s(n):
                    return sem(f"moe{l}_{n}")
                self.landed = [s(f"landed{i}") for i in range(6 * NSUB)]
                self.used = [s(f"used{i}") for i in range(6)]
                self.pick, self.gate, self.link = s("pick"), s("gate"), s("link")
                self.gath, self.xga, self.xgd = s("gather"), s("xg_act"), s("xg_dve")
                self.sig, self.hid = s("sig"), s("hid")
                self.ht_mm, self.ht = s("hidT_mm"), s("hidT")
                self.sc_mm, self.sc = s("scat_mm"), s("scat")
                self.dna, self.dnd = s("dn_act"), s("dn_dve")
                self.y = s("y")

        moe = [Moe(0), Moe(1)]

        def pcol(off, n=1):
            return par[:, off:off + n]

        def mcol(part, ch):
            return mod[:, part * DC + ch:part * DC + ch + 1]

        def ada_src(part):
            if part < 12:
                return ada_w[part // 6, :, (part % 6) * D:(part % 6 + 1) * D]
            return fin_ada_w[:, (part - 12) * D:(part - 11) * D]

        def conv(g, link, ch, done):
            acc = B[:, ch, :]
            link(g.tensor_scalar(acc, vconf[:, ch, 0:T], pcol(dw_col(0, ch)), pcol(PAR_A["dwb"] + ch),
                                 ALU.mult, ALU.add))
            for k in range(1, TAPS):
                ins = g.scalar_tensor_tensor(out=acc, in0=vconf[:, ch, k:k + T], scalar=pcol(dw_col(k, ch)),
                                             in1=acc, op0=ALU.mult, op1=ALU.add)
                if k < TAPS - 1:
                    link(ins)
                else:
                    ins.then_inc(done, 1)

        block = ctx.enter_context(nc.Block())

        @block.sync
        def _(sp):
            def ada_load(part):
                src = ada_src(part).rearrange("(k p) n -> p k n", p=P)
                for h in range(2):
                    sp.wait_ge(ada_used, 2 * part + h + 1)
                    sp.dma_start(adabuf[:, h, :, :], src[:, 4 * h:4 * h + 4, :]).then_inc(ada_landed[h], 16)

            def rows(w):
                return w.rearrange("(k p) n -> p k n", p=P)

            sp.dma_start(xin, x[0].rearrange("(a p) d -> p a d", p=P)).then_inc(s_x, 16)
            for part in range(2):
                ada_load(part)
            sp.wait_ge(x_mm, 1)
            sp.dma_start(w1, rows(cm_w1[0])).then_inc(s_w1, 16)
            sp.dma_start(w2, rows(cm_w2[0])).then_inc(s_w2, 16)
            for part in range(2, 8):
                ada_load(part)

            def experts(l):
                m = moe[l]
                gsrc = moe_w_gate[l].rearrange("e (p k) f -> (e p) (k f)", p=P)
                usrc = moe_w_up[l].rearrange("e (p k) f -> (e p) (k f)", p=P)
                dsrc = moe_w_down[l].rearrange("e (p k) d -> (e p) (k d)", p=P)
                sp.wait_ge(route_ready, l + 1)
                passes = sp.value_load(tab[0:1, 0:1], min_val=1, max_val=MAXP)
                nblk = sp.value_load(tab[0:1, 1:2], min_val=1, max_val=MAXB)
                with sp.Fori(0, passes) as i:
                    ids = [sp.value_load(tab[0:1, bass.ds(i * NSUB + j + 2, 1)], min_val=0, max_val=NE - 1)
                           for j in range(NSUB)]
                    for ph in range(6):
                        src, h = (gsrc, usrc, dsrc)[ph // 2], ph % 2
                        sp.wait_ge(m.used[ph], i + 1)
                        for j in range(NSUB):
                            slot = ph * NSUB + j
                            dst = wbuf[:, slot * 2048:(slot + 1) * 2048]
                            sp.dma_start(dst, src[bass.ds(ids[j] * P, P), h * 2048:(h + 1) * 2048],
                                         cond=(i * NSUB + j < nblk)).then_inc(m.landed[slot], 16)

            experts(0)
            sp.wait_ge(moe[0].y, 1)
            for w, s, i in ((rg_wx, s_wx, 0), (rg_wy, s_wy, 1), (rg_wo, s_wo, 2)):
                sp.dma_start(rgw[i], rows(w[0])).then_inc(s, 16)
                if i == 1:
                    for n, g in enumerate((rg_wa, rg_wi)):
                        sp.dma_start(wab[:, n, :, :, :], g[0].rearrange("h (i p) j -> p h i j", p=P)).then_inc(s_wab, 16)
            for part in range(8, 14):
                ada_load(part)
            experts(1)
            for a in range(TT):
                sp.wait_ge((ht_dve, ht_act)[a], 3)
                sp.dma_start(out[0, a * P:(a + 1) * P, :], htok[:, a, :]).then_inc(s_out, 16)
            sp.wait_ge(s_out, 16 * TT)

        @block.gpsimd
        def _(pool):
            link = Link(pool, pool_link)
            g = nc.gpsimd
            link(g.memset(ident[:], 0.0))
            link(g.memset(ones[:], 1.0))
            g.affine_select(out=ident[:], in_=ident[:], compare_op=ALU.not_equal, fill=1.0, base=0,
                            pattern=[[-1, P]], channel_multiplier=1).then_inc(consts, 1)
            g.affine_select(out=upper[:], in_=ones[:], compare_op=ALU.is_gt, fill=0.0, base=0,
                            pattern=[[1, P]], channel_multiplier=-1).then_inc(consts, 1)
            g.memset(onesd[:], 1.0 / D).then_inc(consts, 1)
            kw = dict(allow_small_or_imprecise_dtypes=True)
            g.iota(iota0[:], [[1, P]], base=0, channel_multiplier=0, **kw).then_inc(consts, 1)
            g.iota(iota1[:], [[1, P]], base=P, channel_multiplier=0, **kw).then_inc(consts, 1)
            g.iota(rev[:], [[-1, NE]], base=NE, channel_multiplier=0, **kw).then_inc(consts, 1)
            g.iota(blk[:], [[1, 2 * MAXP]], base=0, channel_multiplier=0, **kw).then_inc(consts, 1)
            g.iota(thr[:], [[SLOTS, T // SLOTS]], base=0, channel_multiplier=0, **kw).then_inc(consts, 1)
            g.memset(vconf[:, :, 0:TAPS - 1], 0.0).then_inc(pad_ready, 1)

            for q in range(DC // 2):
                y = B[:, 2 * q:2 * q + 2, :]
                pool.wait_ge(q_ready, 2 * q + 2)
                link(g.tensor_tensor(sg[:, :, :], y, y, ALU.mult))
                link(g.tensor_scalar(sg[:, :, :], sg[:, :, :], GELU_A, 1.0, ALU.mult, ALU.add))
                g.tensor_tensor(sg[:, :, :], sg[:, :, :], y, ALU.mult).then_inc(g_in, 1)
                pool.wait_ge(g_sig, q + 1)
                g.tensor_tensor(y, y, sg[:, :, :], ALU.mult).then_inc(y_ready, 1)
                pool.wait_ge(y_ready, q + 1)

        @block.scalar
        def _(act):
            a = nc.scalar
            link = Link(act, act_link)

            def vec(tile, row, src, n):
                act.dma_start(ptile[tile][row:row + n, :], src).then_inc(s_par[tile], 16)

            def v8(t):
                return t.rearrange("l (c p) -> (l c) p", p=P)

            vec(0, PAR_A["c"], v8(c), 8)
            vec(0, PAR_A["n1"], v8(norm1_g), 16)
            vec(0, PAR_A["n2"], v8(norm2_g), 16)
            vec(0, PAR_A["fin"], fin_g.rearrange("(c p) -> c p", p=P), 8)
            vec(0, PAR_A["b1"], v8(cm_b1), 16)
            for n, t in (("dwb", cm_dwb), ("lng", cm_ln_g), ("lnb", cm_ln_b), ("b2", cm_b2)):
                vec(0, PAR_A[n], v8(t), 8)
            vec(2, 0, ada_b.rearrange("l (c p) -> (l c) p", p=P), 96)
            vec(2, 96, fin_ada_b.rearrange("(c p) -> c p", p=P), 16)
            for n, t in (("by", rg_by), ("bx", rg_bx), ("cb", rg_cb), ("lam", rg_lambda), ("bo", rg_bo)):
                vec(1, PAR_B[n] - P, v8(t), 8)
            vec(1, PAR_B["ba"] - P, rg_ba[0].rearrange("h (c p) -> (h c) p", p=P), 8)
            vec(1, PAR_B["bi"] - P, rg_bi[0].rearrange("h (c p) -> (h c) p", p=P), 8)
            vec(1, PAR_B["cw"] - P, rg_cw[0].rearrange("k (c p) -> (k c) p", p=P), 32)
            dwr = cm_dw[0].rearrange("k (c p) -> (k c) p", p=P)
            vec(3, 0, dwr[0:DW_ROWS, :], DW_ROWS)
            vec(4, 0, dwr[DW_ROWS:2 * DW_ROWS, :], DW_ROWS)
            for l in range(2):
                act.dma_start(wgr[:, l, :, 0:NG], moe_wg[l].rearrange("(k p) g -> p k g", p=P)).then_inc(s_router, 16)
                act.dma_start(wgr[:, l, :, NG:], moe_wr[l].rearrange("(k p) g -> p k g", p=P)).then_inc(s_router, 16)
            act.dma_start(brow[0:1, :, 0:NG], moe_bg.rearrange("(a l) g -> a l g", a=1)).then_inc(s_router, 16)
            act.dma_start(brow[0:1, :, NG:], moe_br.rearrange("(a l) g -> a l g", a=1)).then_inc(s_router, 16)

            act.wait_ge(par_ready, 1)
            a.activation(small[:, 0, :], pcol(PAR_A["c"], DC), ACT.Sigmoid).then_inc(csig, 1)

            def ada_rows(part):
                act.wait_ge(ada_used, 2 * part + 4)
                if part >= 1:
                    act.wait_ge(cols_mm, part)
                a.activation(rowsum[:, :], ps[:, 6:8, :].rearrange("p b n -> p (b n)"), ACT.Copy).then_inc(rows_ready, 1)

            def norm(k, src, sh_part):
                act.wait_ge(x_ready, k + 1)
                if k == 0:
                    act.wait_ge(x_ready, 1)
                a.activation(H[:, :, :], X[:, :, :], ACT.Square).then_inc(sq_ready, 1)
                act.wait_ge(inv_ready, k + 1)
                a.activation(rs[:, :], rs[:, :], ACT.Sqrt).then_inc(root_ready, 1)
                act.wait_ge(xn_ready, k + 1)
                act.wait_ge(gs_ready, k + 1)
                for ch in range(DC):
                    a.activation(H[:, ch, :], H[:, ch, :], ACT.Identity, bias=mcol(sh_part, ch),
                                 scale=gs[:, ch:ch + 1]).then_inc(h_ready, 1)

            def out_proj(k, g1_part):
                for n in range(DC):
                    act.wait_ge(o_mm, (k * DC + n) // 2 + 1)
                    if n == 0:
                        act.wait_ge(gb_ready, k + 1)
                    a.activation(C[:, n, :], ps[:, n // 2, (n % 2) * T:(n % 2 + 1) * T], ACT.Identity,
                                 bias=small[:, 1, n:n + 1], scale=mcol(g1_part, n)).then_inc(o_ready, 1)

            for part in range(2):
                ada_rows(part)
            norm(0, X, 0)

            act.wait_ge(par_ready, 5)
            act.wait_ge(nk_in, 1)
            a.activation(small[:, 3, :], small[:, 2, :], ACT.Exp, scale=-1.0).then_inc(nk_exp, 1)
            act.wait_ge(nk_exp, 2)
            a.activation(small[:, 5, :], small[:, 4, :], ACT.Ln).then_inc(nk_ln, 1)
            for m in range(DC):
                act.wait_ge(glu_mm, m + 1)
                if m >= 2:
                    act.wait_ge(v_ready, m - 1)
                a.activation(sg[:, m % 2, :], ps[:, m % 4, T:2 * T], ACT.Sigmoid,
                             bias=pcol(PAR_A["b1"] + DC + m)).then_inc(sg_ready, 1)
                for part in ADA_AFTER.get(m, ()):
                    ada_rows(part)
            act.wait_ge(cen_ready, 1)
            a.activation(Dd[:, :, :], C[:, :, :], ACT.Square).then_inc(csq_ready, 1)
            act.wait_ge(ln_inv, 1)
            a.activation(rs[:, :], rs[:, :], ACT.Sqrt).then_inc(ln_root, 1)
            act.wait_ge(z_ready, 1)
            for ch in range(DC):
                a.activation(Dd[:, ch, :], C[:, ch, :], ACT.Sigmoid, bias=pcol(PAR_A["lnb"] + ch),
                             scale=pcol(PAR_A["lng"] + ch)).then_inc(zs_ready, 1)
            act.wait_ge(act_in, DC)
            out_proj(0, 2)
            norm(1, X, 3)

            def route(l):
                act.wait_ge(ge_in, 2 * l + 1)
                a.activation(r4[:, 1, :, :], r4[:, 0, :, :], ACT.Exp).then_inc(ge_ready, 1)
                act.wait_ge(ge_in, 2 * l + 2)
                a.activation(r1[:, 7, :], r1[:, 5, :], ACT.Exp).then_inc(ge_ready, 1)

            def tokens(l):
                act.wait_ge(ht_mm, 2 * l + 2)
                a.activation(htok[:, 1, :], ps[:, 2:4, :].rearrange("p b n -> p (b n)"), ACT.Copy).then_inc(ht_act, 1)

            def experts(l):
                m = moe[l]
                act.wait_ge(route_ready, l + 1)
                passes = act.value_load(tab[0:1, 0:1], min_val=1, max_val=MAXP)
                act.wait_ge(m.gath, 1)
                a.activation(xg[:, 0:4, :], ps[:, 6, :].rearrange("p (k s) -> p k s", k=4), ACT.Copy).then_inc(m.xga, 1)
                act.wait_ge(m.dnd, 1)
                act.sem_inc(m.dna, 1)
                with act.Fori(0, passes) as i:
                    act.wait_ge(m.used[1], i + 2)
                    act.wait_ge(m.hid, i + 1)
                    a.activation(sigb, ps[:, 4, :], ACT.Sigmoid).then_inc(m.sig, 1)
                    act.wait_ge(m.gath, i + 2)
                    a.activation(xg[:, 0:4, :], ps[:, 6, :].rearrange("p (k s) -> p k s", k=4), ACT.Copy).then_inc(m.xga, 1)
                    act.wait_ge(m.ht_mm, i + 1)
                    a.activation(hidT, ps[:, 4, :].rearrange("p (c s) -> p c s", c=FC), ACT.Copy).then_inc(m.ht, 1)
                    act.wait_ge(m.used[5], i + 2)
                    a.activation(dn[:, 0:512], ps[:, 6, :], ACT.Copy).then_inc(m.dna, 1)

            tokens(0)
            route(0)
            experts(0)

            norm(2, X, 6)
            act.wait_ge(par_ready, 5)
            act.wait_ge(pad_ready, 2)
            for n in range(DC):
                act.wait_ge(ux_mm, n // 2 + 1)
                a.activation(vlru[:, n, LTAPS - 1:], ps[:, n // 2, (n % 2) * T:(n % 2 + 1) * T], ACT.Identity,
                             bias=pcol(PAR_B["bx"] + n)).then_inc(ux_ready, 1)
            for n in range(DC):
                act.wait_ge(q_mm, n // 2 + 1)
                a.activation(B[:, n, :], ps[:, n // 2, (n % 2) * T:(n % 2 + 1) * T], ACT.Identity,
                             bias=pcol(PAR_B["by"] + n)).then_inc(q_ready, 1)
            for q in range(DC // 2):
                act.wait_ge(g_in, q + 1)
                a.activation(sg[:, :, :], sg[:, :, :], ACT.Sigmoid, scale=GELU_B).then_inc(g_sig, 1)
            for h in range(HEADS):
                act.wait_ge(gate_mm, h + 1)
                act.wait_ge(u_ready, DC)
                for j in range(2):
                    n = 2 * h + j
                    a.activation(Dd[:, n, :], ps[:, 2 * (h % 2), j * T:(j + 1) * T], ACT.Sigmoid,
                                 bias=pcol(PAR_B["ba"] + n)).then_inc(rg_ready, 1)
                    a.activation(vflat[:, n, :], ps[:, 2 * (h % 2) + 1, j * T:(j + 1) * T], ACT.Sigmoid,
                                 bias=pcol(PAR_B["bi"] + n)).then_inc(rg_ready, 1)
            act.wait_ge(nk_ready, 1)
            act.wait_ge(rg_ready, 4 * HEADS)
            for n in range(DC):
                a.activation(H[:, n, :], Dd[:, n, :], ACT.Tanh, scale=small[:, 2, n:n + 1]).then_inc(ta_ready, 1)
                act.wait_ge(ta_ready, 2 * n + 1)
                a.activation(Dd[:, n, :], Dd[:, n, :], ACT.Exp, scale=small[:, 2, n:n + 1]).then_inc(ta_ready, 1)
            for h in range(HEADS):
                act.wait_ge(b2_ready, h + 1)
                a.activation(H[:, 2 * h:2 * h + 2, :], H[:, 2 * h:2 * h + 2, :], ACT.Sqrt).then_inc(b_ready, 1)
            for part in range(8, 14):
                ada_rows(part)
            act.wait_ge(hs_ready, DC)
            out_proj(1, 8)
            norm(3, X, 9)
            tokens(1)
            route(1)
            experts(1)
            norm(4, X, 12)
            act.wait_ge(fin_mm, 2)
            a.activation(htok[:, 1, :], ps[:, 2:4, :].rearrange("p b n -> p (b n)"), ACT.Copy).then_inc(ht_act, 1)

        @block.vector
        def _(dve):
            v = nc.vector
            link = Link(dve, dve_link)

            def bc(t):
                return t.rearrange("p (o t) -> p o t", o=1).to_broadcast([P, DC, T])

            dve.wait_ge(consts, 8)
            v.tensor_reduce(sel[:, :], ident[:, 0:P:32], AX.X, ALU.add).then_inc(sel_ready, 1)
            order = (0, 2, 1, 3, 4)
            for n, i in enumerate(order):
                dve.wait_ge(par_mm, n + 1)
                v.tensor_copy(par[:, i * P:i * P + PAR_TILES[i]],
                              ps[:, 4 + n % 4, 0:PAR_TILES[i]]).then_inc(par_ready, 1)
            dve.wait_ge(csig, 1)
            dve.wait_ge(par_ready, 1)
            link(v.tensor_tensor(small[:, 1, :], small[:, 0, :], pcol(PAR_A["c"], DC), ALU.mult))
            v.tensor_copy(cb32[:, :, :], small[:, 1, :].rearrange("p (c o) -> p c o", o=1).to_broadcast([P, DC, 32])).then_inc(cact, 1)
            dve.wait_ge(x_mm, 1)
            link(v.tensor_copy(X[:, 0:4, :].rearrange("p c t -> p (c t)"), ps[:, 0:2, :].rearrange("p b n -> p (b n)")))
            v.tensor_copy(X[:, 4:8, :].rearrange("p c t -> p (c t)"), ps[:, 2:4, :].rearrange("p b n -> p (b n)")).then_inc(x_ready, 1)

            def ada_cols(part):
                dve.wait_ge(cols_mm, part + 1)
                v.tensor_tensor(mod[:, part * DC:(part + 1) * DC], ps[:, 5, 0:DC],
                                pcol(PAR_ADA + part * DC, DC), ALU.add).then_inc(mod_ready, 1)

            def norm(k, gain, sc_part):
                dve.wait_ge(mod_ready, sc_part + 1)
                if k >= 1:
                    dve.wait_ge(h_ready, k * DC)
                v.scalar_tensor_tensor(out=gs[:, :], in0=mod[:, sc_part * DC:(sc_part + 1) * DC], scalar=1.0,
                                       in1=pcol(gain, DC), op0=ALU.add, op1=ALU.mult).then_inc(gs_ready, 1)
                dve.wait_ge(ms_mm, k + 1)
                link(v.tensor_scalar(rs[:, :], ps[:, 4, 0:T], EPS, None, ALU.add))
                v.reciprocal(rs[:, :], rs[:, :]).then_inc(inv_ready, 1)
                dve.wait_ge(root_ready, k + 1)
                v.tensor_tensor(H[:, :, :], X[:, :, :], bc(rs[:, :]), ALU.mult).then_inc(xn_ready, 1)

            def out_proj(k, bias, g1_part):
                dve.wait_ge(mod_ready, g1_part + 1)
                v.tensor_tensor(small[:, 1, :], mod[:, g1_part * DC:(g1_part + 1) * DC], pcol(bias, DC),
                                ALU.mult).then_inc(gb_ready, 1)
                for n in range(DC):
                    dve.wait_ge(o_ready, k * DC + n + 1)
                    ins = v.tensor_tensor(X[:, n, :], X[:, n, :], C[:, n, :], ALU.add)
                    if n < DC - 1:
                        link(ins)
                    else:
                        ins.then_inc(x_ready, 1)
                dve.wait_ge(x_ready, 2 * k + 2)

            for part in range(2):
                ada_cols(part)
            dve.wait_ge(x_ready, 1)
            norm(0, PAR_A["n1"], 1)

            dve.wait_ge(par_ready, 5)
            lam = pcol(PAR_B["lam"], DC)
            link(v.tensor_scalar(small[:, 4, :], lam, -1.0, None, ALU.mult))
            v.tensor_tensor(small[:, 2, :], lam, small[:, 4, :], ALU.max).then_inc(nk_in, 1)
            link(v.tensor_scalar(small[:, 6, :], small[:, 4, :], 0.0, None, ALU.max))
            dve.wait_ge(nk_exp, 1)
            v.tensor_scalar(small[:, 4, :], small[:, 3, :], 1.0, None, ALU.add).then_inc(nk_exp, 1)
            dve.wait_ge(nk_exp, 2)
            link(v.tensor_scalar(small[:, 7, :], small[:, 4, :], 1.0, None, ALU.subtract))
            link(v.tensor_scalar(small[:, 0, :], small[:, 7, :], 0.0, None, ALU.is_equal))
            link(v.tensor_tensor(small[:, 7, :], small[:, 7, :], small[:, 0, :], ALU.add))
            link(v.reciprocal(small[:, 7, :], small[:, 7, :]))
            dve.wait_ge(nk_ln, 1)
            link(v.tensor_tensor(small[:, 5, :], small[:, 5, :], small[:, 0, :], ALU.add))
            link(v.tensor_tensor(small[:, 5, :], small[:, 5, :], small[:, 7, :], ALU.mult))
            link(v.tensor_tensor(small[:, 5, :], small[:, 5, :], small[:, 3, :], ALU.mult))
            link(v.tensor_tensor(small[:, 5, :], small[:, 5, :], small[:, 6, :], ALU.add))
            v.tensor_scalar(small[:, 2, :], small[:, 5, :], -8.0, None, ALU.mult).then_inc(nk_ready, 1)
            dve.wait_ge(pad_ready, 1)
            for m in range(DC):
                dve.wait_ge(sg_ready, m + 1)
                v.scalar_tensor_tensor(out=vconf[:, m, TAPS - 1:], in0=ps[:, m % 4, 0:T], scalar=pcol(PAR_A["b1"] + m),
                                       in1=sg[:, m % 2, :], op0=ALU.add, op1=ALU.mult).then_inc(v_ready, 1)
                dve.wait_ge(v_ready, m + 1)
                conv(v, link, m, conv_dve)
                for part in ADA_AFTER.get(m, ()):
                    ada_cols(part)
            dve.wait_ge(mean_mm, 1)
            v.tensor_tensor(C[:, :, :], B[:, :, :], bc(ps[:, 4, 0:T]), ALU.subtract).then_inc(cen_ready, 1)
            dve.wait_ge(var_mm, 1)
            link(v.tensor_scalar(rs[:, :], ps[:, 4, T:2 * T], EPS, None, ALU.add))
            v.reciprocal(rs[:, :], rs[:, :]).then_inc(ln_inv, 1)
            dve.wait_ge(ln_root, 1)
            v.tensor_tensor(C[:, :, :], C[:, :, :], bc(rs[:, :]), ALU.mult).then_inc(z_ready, 1)
            dve.wait_ge(z_ready, 1)
            for ch in range(DC):
                link(v.tensor_scalar(H[:, ch, :], C[:, ch, :], pcol(PAR_A["lng"] + ch), pcol(PAR_A["lnb"] + ch),
                                     ALU.mult, ALU.add))
                dve.wait_ge(zs_ready, ch + 1)
                v.tensor_tensor(B[:, ch, :], H[:, ch, :], Dd[:, ch, :], ALU.mult).then_inc(act_in, 1)
            out_proj(0, PAR_A["b2"], 2)
            norm(1, PAR_A["n2"], 4)

            def tokens(l):
                dve.wait_ge(ht_mm, 2 * l + 1)
                v.tensor_copy(htok[:, 0, :], ps[:, 0:2, :].rearrange("p b n -> p (b n)")).then_inc(ht_dve, 1)

            def route(l):
                def wide(t, n):
                    return t.rearrange("p (a o) -> p a o", o=1).to_broadcast([P, TT, n])

                dve.wait_ge(lg_mm, l + 1)
                link(v.tensor_copy(lg[:, :, :], ps[:, 5, 0:TT * (NG + NE)].rearrange("p (a g) -> p a g", a=TT)))
                gl, el = lg[:, :, 0:NG], lg[:, :, NG:]
                link(v.tensor_reduce(r1[:, 0, :], gl, AX.X, ALU.max))
                v.tensor_tensor(r4[:, 0, :, :], gl, wide(r1[:, 0, :], NG), ALU.subtract).then_inc(ge_in, 1)
                revg = rev[:, NE - NG:].rearrange("p (o n) -> p o n", o=1).to_broadcast([P, TT, NG])
                reve = rev[:, :].rearrange("p (o n) -> p o n", o=1).to_broadcast([P, TT, NE])
                link(v.tensor_tensor(r4[:, 2, :, :], gl, wide(r1[:, 0, :], NG), ALU.is_equal))
                link(v.tensor_tensor(r4[:, 2, :, :], r4[:, 2, :, :], revg, ALU.mult))
                link(v.tensor_reduce(r1[:, 1, :], r4[:, 2, :, :], AX.X, ALU.max))
                link(v.tensor_tensor(r4[:, 2, :, :], r4[:, 2, :, :], wide(r1[:, 1, :], NG), ALU.is_equal))
                for a in range(TT):
                    gsel = r4[:, 2, a, :].rearrange("p (g o) -> p g o", o=1).to_broadcast([P, NG, EPG])
                    link(v.tensor_tensor(r32[:, 0, a, :].rearrange("p (g e) -> p g e", g=NG),
                                         lg[:, a, NG:].rearrange("p (g e) -> p g e", g=NG), gsel, ALU.mult))
                    link(v.tensor_scalar(r32[:, 1, a, :].rearrange("p (g e) -> p g e", g=NG), gsel, 1.0, BIG,
                                         ALU.subtract, ALU.mult))
                link(v.tensor_tensor(r32[:, 0, :, :], r32[:, 0, :, :], r32[:, 1, :, :], ALU.add))
                for k in range(2):
                    hot = r32[:, 2 + k, :, :]
                    link(v.tensor_reduce(r1[:, 2 + k, :], r32[:, 0, :, :], AX.X, ALU.max))
                    link(v.tensor_tensor(hot, r32[:, 0, :, :], wide(r1[:, 2 + k, :], NE), ALU.is_equal))
                    link(v.tensor_tensor(hot, hot, reve, ALU.mult))
                    link(v.tensor_reduce(r1[:, 4, :], hot, AX.X, ALU.max))
                    link(v.tensor_tensor(hot, hot, wide(r1[:, 4, :], NE), ALU.is_equal))
                    if k == 0:
                        link(v.scalar_tensor_tensor(out=r32[:, 0, :, :], in0=hot, scalar=-3 * BIG, in1=r32[:, 0, :, :],
                                                    op0=ALU.mult, op1=ALU.add))
                v.tensor_tensor(r32[:, 4, :, :], r32[:, 2, :, :], r32[:, 3, :, :], ALU.add).then_inc(mask_ready, 1)
                v.tensor_tensor(r1[:, 5, :], r1[:, 3, :], r1[:, 2, :], ALU.subtract).then_inc(ge_in, 1)
                dve.wait_ge(ge_ready, 2 * l + 1)
                link(v.tensor_reduce(r1[:, 6, :], r4[:, 1, :, :], AX.X, ALU.add))
                dve.wait_ge(ge_ready, 2 * l + 2)
                e2 = r1[:, 7, :]
                link(v.tensor_scalar(r1[:, 8, :], e2, 1.0, None, ALU.add))
                link(v.tensor_tensor(r1[:, 8, :], r1[:, 8, :], r1[:, 6, :], ALU.mult))
                link(v.reciprocal(gw[:, 0, :], r1[:, 8, :]))
                link(v.tensor_tensor(gw[:, 1, :], gw[:, 0, :], e2, ALU.mult))
                dve.wait_ge(rank_mm, l + 1)
                link(v.tensor_copy(cnt[:, 0, :], ps[:, 5, 2 * NE + P:3 * NE + P]))
                cw = cmp3[:, 0:NE, 0:T // SLOTS]
                link(v.tensor_tensor(cw, cnt[:, 0, :].rearrange("p (e o) -> p e o", o=1).to_broadcast([P, NE, T // SLOTS]),
                                     thr[:, :].rearrange("p (o n) -> p o n", o=1).to_broadcast([P, NE, T // SLOTS]), ALU.is_gt))
                link(v.tensor_reduce(cnt[:, 1, :], cw, AX.X, ALU.add))
                link(v.tensor_tensor_scan(cnt[:, 2, :], ones[:, 0:NE], cnt[:, 1, :], 0.0, ALU.mult, ALU.add))
                link(v.tensor_tensor(cnt[:, 3, :], cnt[:, 2, :], cnt[:, 1, :], ALU.subtract))
                link(v.tensor_tensor(cmp3[:, :, :], cnt[:, 2, :].rearrange("p (o e) -> p o e", o=1).to_broadcast([P, 2 * MAXP, NE]),
                                     blk[:, :].rearrange("p (b o) -> p b o", o=1).to_broadcast([P, 2 * MAXP, NE]), ALU.is_le))
                link(v.tensor_reduce(tabf[:, 0:2 * MAXP], cmp3[:, :, :], AX.X, ALU.add))
                link(v.tensor_scalar(tabf[:, 0:2 * MAXP], tabf[:, 0:2 * MAXP], float(NE - 1), None, ALU.min))
                link(v.tensor_copy(tab[0:1, 2:2 + 2 * MAXP], tabf[0:1, 0:2 * MAXP]))
                link(v.tensor_copy(tab[0:1, 1:2], cnt[0:1, 2, NE - 1:NE]))
                link(v.tensor_scalar(tabf[:, 0:MAXP], blk[:, 0:2 * MAXP:2], cnt[:, 2, NE - 1:NE], None, ALU.is_lt))
                link(v.tensor_reduce(tabf[:, MAXP:MAXP + 1], tabf[:, 0:MAXP], AX.X, ALU.add))
                v.tensor_copy(tab[0:1, 0:1], tabf[0:1, MAXP:MAXP + 1]).then_inc(route_ready, 1)
                for a in range(TT):
                    link(v.scalar_tensor_tensor(out=r32[:, 5, a, :], in0=cnt[:, 3, :], scalar=float(SLOTS),
                                                in1=ps[:, 5, P + a * NE:P + (a + 1) * NE], op0=ALU.mult, op1=ALU.add))
                for k in range(2):
                    link(v.tensor_tensor(r32[:, 0, :, :], r32[:, 5, :, :], r32[:, 2 + k, :, :], ALU.mult))
                    link(v.tensor_reduce(gslot[:, k, :], r32[:, 0, :, :], AX.X, ALU.add))

            def experts(l):
                m = moe[l]
                route_ins = Link(dve, m.link)

                def picks(lk, io):
                    for a in range(TT):
                        lk(v.tensor_scalar(pick[:, a, :], io[:], gslot[:, 0, a:a + 1], None, ALU.is_equal))
                        ins = v.scalar_tensor_tensor(out=pick[:, a, :], in0=io[:], scalar=gslot[:, 1, a:a + 1],
                                                     in1=pick[:, a, :], op0=ALU.is_equal, op1=ALU.add)
                        if a < TT - 1:
                            lk(ins)
                        else:
                            ins.then_inc(m.pick, 1)

                picks(route_ins, iota0)
                dve.wait_ge(route_ready, l + 1)
                passes = dve.value_load(tab[0:1, 0:1], min_val=1, max_val=MAXP)
                dve.wait_ge(m.gath, 1)
                v.tensor_copy(xg[:, 4:8, :], ps[:, 7, :].rearrange("p (k s) -> p k s", k=4)).then_inc(m.xgd, 1)
                n0 = route_ins.n
                route_ins(v.memset(scat, 0.0))
                v.memset(dn[:, :], 0.0).then_inc(m.dnd, 1)
                dve.wait_ge(m.dnd, 1)
                dve.sem_inc(m.sc, 1)
                dve.sem_inc(m.hid, 1)
                n0 = route_ins.n
                with dve.Fori(0, passes) as i:
                    lk = Link(dve, m.link, i * EXPERT_LINKS + n0)
                    dve.wait_ge(m.pick, i + 1)
                    dve.wait_ge(m.gath, i + 1)
                    picks(lk, iota1)
                    dve.wait_ge(m.sc, i + 1)
                    for a in range(TT):
                        for k, dst in ((0, gate1), (1, gate2)):
                            lk(v.tensor_scalar(dst[:, a, :], iota0[:], gslot[:, k, a:a + 1], gw[:, k, a:a + 1],
                                               ALU.is_equal, ALU.mult))
                    v.tensor_tensor(gate1[:, :, :], gate1[:, :, :], gate2[:, :, :], ALU.add).then_inc(m.gate, 1)
                    dve.wait_ge(m.pick, i + 2)
                    lk(v.tensor_scalar(gslot[:, :, :], gslot[:, :, :], float(P), None, ALU.subtract))
                    dve.wait_ge(m.sig, i + 1)
                    lk(v.tensor_tensor(hid, ps[:, 4, :], sigb, ALU.mult))
                    dve.wait_ge(m.used[3], i + 2)
                    v.tensor_tensor(hid, hid, ps[:, 5, :], ALU.mult).then_inc(m.hid, 1)
                    dve.wait_ge(m.gath, i + 2)
                    v.tensor_copy(xg[:, 4:8, :], ps[:, 7, :].rearrange("p (k s) -> p k s", k=4)).then_inc(m.xgd, 1)
                    dve.wait_ge(m.sc_mm, i + 1)
                    v.tensor_copy(scat[:, :], ps[:, 5, 0:T]).then_inc(m.sc, 1)
                    dve.wait_ge(m.used[5], i + 2)
                    v.tensor_copy(dn[:, 512:1024], ps[:, 7, :]).then_inc(m.dnd, 1)
                    assert lk.n == EXPERT_LINKS, lk.n
                g2 = 6 * l + 5
                dve.wait_ge(mod_ready, g2 + 1)
                dve.wait_ge(m.y, 1)
                for ch in range(DC):
                    ins = v.scalar_tensor_tensor(out=X[:, ch, :], in0=ps[:, ch // 2, (ch % 2) * T:(ch % 2 + 1) * T],
                                                 scalar=mcol(g2, ch), in1=X[:, ch, :], op0=ALU.mult, op1=ALU.add)
                    if ch < DC - 1:
                        link(ins)
                    else:
                        ins.then_inc(x_ready, 1)
                dve.wait_ge(x_ready, 2 * l + 3)

            tokens(0)
            route(0)
            experts(0)

            dve.memset(vlru[:, :, 0:LTAPS - 1], 0.0).then_inc(pad_ready, 1)
            norm(2, PAR_A["n1"] + DC, 7)
            for n in range(DC):
                dve.wait_ge(ux_ready, n + 1)
                acc = C[:, n, :]
                link(v.tensor_scalar(acc, vlru[:, n, 0:T], pcol(PAR_B["cw"] + n), pcol(PAR_B["cb"] + n),
                                     ALU.mult, ALU.add))
                for k in range(1, LTAPS):
                    ins = v.scalar_tensor_tensor(out=acc, in0=vlru[:, n, k:k + T], scalar=pcol(PAR_B["cw"] + k * DC + n),
                                                 in1=acc, op0=ALU.mult, op1=ALU.add)
                    if k < LTAPS - 1:
                        link(ins)
                    else:
                        ins.then_inc(u_ready, 1)
            dve.wait_ge(y_ready, DC // 2)
            for h in range(HEADS):
                two = slice(2 * h, 2 * h + 2)
                t = H[:, two, :]
                dve.wait_ge(ta_ready, 4 * h + 4)
                link(v.tensor_scalar(sg[:, :, :], t, -1.0, 1.0, ALU.mult, ALU.add))
                link(v.reciprocal(sg[:, :, :], sg[:, :, :]))
                v.scalar_tensor_tensor(out=t, in0=t, scalar=-2.0, in1=sg[:, :, :], op0=ALU.mult,
                                       op1=ALU.mult).then_inc(b2_ready, 1)
                dve.wait_ge(b2_ready, h + 1)
            for h in range(HEADS):
                two = slice(2 * h, 2 * h + 2)
                t = H[:, two, :]
                dve.wait_ge(b_ready, h + 1)
                link(v.tensor_tensor(t, t, vflat[:, two, :], ALU.mult))
                link(v.tensor_tensor(t, t, C[:, two, :], ALU.mult))
                for n in (2 * h, 2 * h + 1):
                    link(v.tensor_tensor_scan(vflat[:, n, :], Dd[:, n, :], H[:, n, :], 0.0, ALU.mult, ALU.add))
                    v.tensor_tensor(B[:, n, :], B[:, n, :], vflat[:, n, :], ALU.mult).then_inc(hs_ready, 1)
            for part in range(8, 14):
                ada_cols(part)
            out_proj(1, PAR_B["bo"], 8)
            norm(3, PAR_A["n2"] + DC, 10)
            tokens(1)
            route(1)
            experts(1)
            norm(4, PAR_A["fin"], 13)
            dve.wait_ge(fin_mm, 1)
            v.tensor_copy(htok[:, 0, :], ps[:, 0:2, :].rearrange("p b n -> p (b n)")).then_inc(ht_dve, 1)

        @block.tensor
        def _(pe):
            mm = nc.tensor.matmul
            kw = dict(skip_group_check=True)
            pe.wait_ge(consts, 8)
            pe.sem_inc(ada_used, 2)
            for q, i in enumerate((0, 2, 1, 3, 4)):
                n = PAR_TILES[i]
                pe.wait_ge(s_par[i], 16 * PAR_DMAS[i])
                if q == 4:
                    pe.wait_ge(par_ready, 1)
                mm(ps[:, 4 + q % 4, 0:n], ptile[i][0:n, :], ident[0:n, 0:n],
                   start=True, stop=True).then_inc(par_mm, 1)
            pe.wait_ge(s_x, 16)
            for ch in range(DC):
                for a in range(TT):
                    last = mm(ps[:, ch // 2, (ch % 2) * T + a * P:(ch % 2) * T + (a + 1) * P],
                              xin[:, a, ch * P:(ch + 1) * P], ident[:], start=True, stop=True)
            last.then_inc(x_mm, 1)

            def ada(part):
                if part == 0:
                    pe.wait_ge(cact, 1)
                    pe.wait_ge(par_ready, 5)
                else:
                    pe.wait_ge(rows_ready, part)
                for h in range(2):
                    pe.wait_ge(ada_landed[h], 16 * (part + 1))
                    for n in range(2):
                        for j in range(4):
                            last = mm(ps[32 * j:32 * j + 32, 6 + n, :], cb32[:, 4 * h + j, :],
                                      adabuf[:, h, j, n * 512:(n + 1) * 512], start=(h == 0), stop=(h == 1), **kw)
                    last.then_inc(ada_used, 1)
                pe.wait_ge(rows_ready, part + 1)
                if part >= 1:
                    pe.wait_ge(mod_ready, part)
                if part == 0:
                    pe.wait_ge(x_ready, 1)
                    pe.wait_ge(sel_ready, 1)
                for ch in range(DC):
                    last = mm(ps[:, 5, ch:ch + 1], rowsum[:, ch * P:(ch + 1) * P], sel[:, :], start=True, stop=True, **kw)
                last.then_inc(cols_mm, 1)

            def norm(k):
                pe.wait_ge(sq_ready, k + 1)
                for ch in range(DC):
                    last = mm(ps[:, 4, 0:T], onesd[:], H[:, ch, :], start=(ch == 0), stop=(ch == DC - 1), **kw)
                last.then_inc(ms_mm, 1)
                pe.wait_ge(h_ready, DC * (k + 1))

            def proj(bank, off, w, col, src):
                for k in range(DC):
                    last = mm(ps[:, bank, off:off + T], w[:, k, col:col + P], src[:, k, :],
                              start=(k == 0), stop=(k == DC - 1), **kw)
                return last

            ada(0)
            ada(1)
            norm(0)

            pe.wait_ge(s_w1, 16)
            pe.wait_ge(par_ready, 5)
            for m in range(DC):
                if m >= 4:
                    pe.wait_ge(v_ready, m - 3)
                proj(m % 4, 0, w1, m * P, H)
                proj(m % 4, T, w1, D + m * P, H).then_inc(glu_mm, 1)
                for part in ADA_AFTER.get(m, ()):
                    ada(part)
            pe.wait_ge(conv_dve, DC)
            for ch in range(DC):
                last = mm(ps[:, 4, 0:T], onesd[:], B[:, ch, :], start=(ch == 0), stop=(ch == DC - 1), **kw)
            last.then_inc(mean_mm, 1)
            pe.wait_ge(csq_ready, 1)
            for ch in range(DC):
                last = mm(ps[:, 4, T:2 * T], onesd[:], Dd[:, ch, :], start=(ch == 0), stop=(ch == DC - 1), **kw)
            last.then_inc(var_mm, 1)
            pe.wait_ge(s_w2, 16)
            pe.wait_ge(act_in, DC)
            for n in range(DC):
                last = proj(n // 2, (n % 2) * T, w2, n * P, B)
                if n % 2:
                    last.then_inc(o_mm, 1)
            norm(1)

            def route(l):
                pe.wait_ge(s_router, 16 * 6)
                pe.wait_ge(o_ready, DC * (l + 1))
                pe.wait_ge(mod_ready, 8 + 6 * l)
                for a in range(TT):
                    for k in range(DC):
                        mm(ps[:, 5, a * (NG + NE):(a + 1) * (NG + NE)], H[:, k, a * P:(a + 1) * P], wgr[:, l, k, :],
                           start=(k == 0), stop=False, **kw)
                    last = mm(ps[:, 5, a * (NG + NE):(a + 1) * (NG + NE)], ones[0:1, :], brow[0:1, l, :],
                              start=False, stop=True, **kw)
                last.then_inc(lg_mm, 1)
                for a in range(TT):
                    for ch in range(DC):
                        last = mm(ps[:, 2 * a + ch // 4, (ch % 4) * P:(ch % 4 + 1) * P], H[:, ch, a * P:(a + 1) * P],
                                  ident[:], start=True, stop=True, **kw)
                    last.then_inc(ht_mm, 1)
                pe.wait_ge(mask_ready, l + 1)
                mask = r32[:, 4, :, :]
                mm(ps[:, 5, P:P + NE], upper[:], mask[:, 0, :], start=True, stop=True, **kw)
                mm(ps[:, 5, P + NE:P + 2 * NE], ones[:], mask[:, 0, :], start=True, stop=False, **kw)
                mm(ps[:, 5, P + NE:P + 2 * NE], upper[:], mask[:, 1, :], start=False, stop=True, **kw)
                mm(ps[:, 5, P + 2 * NE:P + 3 * NE], ones[:], mask[:, 0, :], start=True, stop=False, **kw)
                mm(ps[:, 5, P + 2 * NE:P + 3 * NE], ones[:], mask[:, 1, :], start=False, stop=True, **kw).then_inc(rank_mm, 1)

            def experts(l):
                m = moe[l]
                for ph in range(6):
                    pe.sem_inc(m.used[ph], 1)
                pe.wait_ge(ht_dve, l + 1)
                pe.wait_ge(ht_act, l + 1)

                def gather(n):
                    pe.wait_ge(m.pick, n)
                    for k in range(DC):
                        for a in range(TT):
                            last = mm(ps[:, 6 + k // 4, (k % 4) * P:(k % 4 + 1) * P], htok[:, a, k:D:DC],
                                      pick[:, a, :], start=(a == 0), stop=(a == TT - 1), **kw)
                    last.then_inc(m.gath, 1)

                def scatter():
                    for ch in range(DC):
                        last = mm(ps[:, ch // 2, (ch % 2) * T:(ch % 2 + 1) * T], dn[:, ch * P:(ch + 1) * P],
                                  scat[:, :], start=False, stop=False, **kw)
                    return last

                gather(1)
                pe.wait_ge(m.sc, 1)
                for b in range(4):
                    mm(ps[:, b, :], scat[:, 0:P], htok[:, 0, 0:512], start=True, stop=False, **kw)
                pe.wait_ge(route_ready, l + 1)
                passes = pe.value_load(tab[0:1, 0:1], min_val=1, max_val=MAXP)
                with pe.Fori(0, passes) as i:
                    pe.wait_ge(m.xga, i + 1)
                    pe.wait_ge(m.xgd, i + 1)
                    pe.wait_ge(m.sc, i + 1)
                    for ph in range(4):
                        bank, h = 4 + ph // 2, ph % 2
                        for j in range(NSUB):
                            pe.wait_ge(m.landed[ph * NSUB + j], (i + 1) * 16)
                        for k in range(4):
                            for j in range(NSUB):
                                o = (ph * NSUB + j) * 2048 + k * F
                                last = mm(ps[SLOTS * j:SLOTS * (j + 1), bank, :],
                                          xg[:, 4 * h + k, SLOTS * j:SLOTS * (j + 1)], wbuf[:, o:o + F],
                                          start=(h == 0 and k == 0), stop=(h == 1 and k == 3), **kw)
                        last.then_inc(m.used[ph], 1)
                    pe.wait_ge(m.dna, i + 1)
                    pe.wait_ge(m.dnd, i + 1)
                    gather(i + 2)
                    scatter().then_inc(moe_zero, 1)
                    pe.wait_ge(m.hid, i + 2)
                    for k in range(FC):
                        last = mm(ps[:, 4, k * P:(k + 1) * P], hid[:, k:F:FC], ident[:], start=True, stop=True, **kw)
                    last.then_inc(m.ht_mm, 1)
                    pe.wait_ge(m.gate, i + 1)
                    for a in range(TT):
                        last = mm(ps[:, 5, a * P:(a + 1) * P], gate1[:, a, :], ident[:], start=True, stop=True, **kw)
                    last.then_inc(m.sc_mm, 1)
                    pe.wait_ge(m.ht, i + 1)
                    pe.wait_ge(m.xga, i + 2)
                    pe.wait_ge(m.xgd, i + 2)
                    for h in range(2):
                        for j in range(NSUB):
                            pe.wait_ge(m.landed[(4 + h) * NSUB + j], (i + 1) * 16)
                        for k in range(2):
                            for n in range(2):
                                for j in range(NSUB):
                                    o = ((4 + h) * NSUB + j) * 2048 + k * D + n * 512
                                    last = mm(ps[SLOTS * j:SLOTS * (j + 1), 6 + n, :],
                                              hidT[:, 2 * h + k, SLOTS * j:SLOTS * (j + 1)], wbuf[:, o:o + 512],
                                              start=(h == 0 and k == 0), stop=(h == 1 and k == 1), **kw)
                        last.then_inc(m.used[4 + h], 1)
                pe.wait_ge(m.sc, passes + 1)
                pe.wait_ge(m.dna, passes + 1)
                pe.wait_ge(m.dnd, passes + 1)
                scatter().then_inc(m.y, 1)

            route(0)
            experts(0)

            norm(2)
            pe.wait_ge(s_wx, 16)
            for n in range(DC):
                last = proj(n // 2, (n % 2) * T, rgw[0], n * P, H)
                if n % 2:
                    last.then_inc(ux_mm, 1)
            pe.wait_ge(s_wy, 16)
            for n in range(DC):
                pe.wait_ge(ux_ready, 2 * (n // 2) + 2)
                last = proj(n // 2, (n % 2) * T, rgw[1], n * P, H)
                if n % 2:
                    last.then_inc(q_mm, 1)
            pe.wait_ge(s_wab, 32)
            for h in range(HEADS):
                pe.wait_ge(u_ready, 2 * h + 2)
                if h < 2:
                    pe.wait_ge(q_ready, 4 * h + 4)
                else:
                    pe.wait_ge(rg_ready, 4 * (h - 1))
                for w in range(2):
                    for j in range(2):
                        for k in range(2):
                            last = mm(ps[:, 2 * (h % 2) + w, j * T:(j + 1) * T], wab[:, w, h, k, j * P:(j + 1) * P],
                                      C[:, 2 * h + k, :], start=(k == 0), stop=(k == 1), **kw)
                last.then_inc(gate_mm, 1)
            for part in range(8, 14):
                ada(part)
            pe.wait_ge(s_wo, 16)
            pe.wait_ge(hs_ready, DC)
            pe.wait_ge(rg_ready, 4 * HEADS)
            for n in range(DC):
                last = proj(n // 2, (n % 2) * T, rgw[2], n * P, B)
                if n % 2:
                    last.then_inc(o_mm, 1)
            norm(3)
            route(1)
            experts(1)
            norm(4)
            for a in range(TT):
                for ch in range(DC):
                    last = mm(ps[:, 2 * a + ch // 4, (ch % 4) * P:(ch % 4 + 1) * P], H[:, ch, a * P:(a + 1) * P],
                              ident[:], start=True, stop=True, **kw)
                last.then_inc(fin_mm, 1)


ADA_AFTER = {3: (2,), 5: (3,), 7: (4, 5, 6, 7)}
PAR_DMAS = (9, 8, 2, 1, 1)
EXPERT_LINKS = 9


_INS = ["x", "c", "ada_w", "ada_b", "norm1_g", "norm2_g", "cm_w1", "cm_b1", "cm_dw", "cm_dwb", "cm_ln_g",
        "cm_ln_b", "cm_w2", "cm_b2", "rg_wy", "rg_by", "rg_wx", "rg_bx", "rg_cw", "rg_cb", "rg_wa", "rg_ba",
        "rg_wi", "rg_bi", "rg_lambda", "rg_wo", "rg_bo", "moe_wg", "moe_bg", "moe_wr", "moe_br", "moe_w_gate",
        "moe_w_up", "moe_w_down", "fin_ada_w", "fin_ada_b", "fin_g"]


def kernel(**inputs):
    import numpy as _np
    import concourse.bacc as _bacc
    from concourse import mybir as _mybir
    from concourse.bass_utils import run_bass_kernel_spmd as _run

    nc = _bacc.Bacc("TRN2", target_bir_lowering=False, num_devices=1)
    arrays, args = {}, []
    for name in _INS:
        a = _np.ascontiguousarray(inputs[name])
        arrays[f"in_{name}"] = a
        args.append(nc.dram_tensor(f"in_{name}", a.shape, _mybir.dt.from_np(a.dtype), kind="ExternalInput").ap())
    args.append(nc.dram_tensor("out_0", (1, T, D), F32, kind="ExternalOutput").ap())
    trunk(nc, *args)
    r = _run(nc, [arrays], core_ids=[0])
    return r.results[0]["out_0"]
```

```python
from contextlib import ExitStack

import concourse.bass as bass
from concourse import mybir

F32 = mybir.dt.float32
I32 = mybir.dt.int32
ALU = mybir.AluOpType
ACT = mybir.ActivationFunctionType
AX = mybir.AxisListType

P = 128
T = 256
TT = T // P
D = 1024
DC = D // P
EPS = 1e-6
TAPS = 31
LTAPS = 4
HEADS = 4
NG, NE = 4, 32
EPG = NE // NG
F = 512
FC = F // P
SLOTS = 64
NSUB = P // SLOTS
MAXB = NE + (2 * T - NE) // SLOTS
MAXP = -(-MAXB // NSUB)
BIG = 1e30
GELU_A, GELU_B = 0.044715, 1.5957691216057308

PAR_A = {"n1": 0, "n2": 16, "fin": 32, "b1": 40, "dwb": 56, "lng": 64, "lnb": 72, "b2": 80, "c": 88}
PAR_B = {"by": 128, "bx": 136, "cb": 144, "ba": 152, "bi": 160, "lam": 168, "bo": 176, "cw": 184}
PAR_ADA = 256
PAR_DW = 384
DW_ROWS = TAPS * DC // 2
PAR_TILES = [96, 88, 112, DW_ROWS, DW_ROWS]


def dw_col(k, c):
    r = k * DC + c
    return PAR_DW + (r if r < DW_ROWS else P + r - DW_ROWS)


class Link:

    def __init__(self, eng, sem, base=0):
        self.eng, self.sem, self.base, self.n = eng, sem, base, 0

    def post(self, ins):
        self.n += 1
        ins.then_inc(self.sem, 1)
        return self.base + self.n

    def __call__(self, ins):
        self.eng.wait_ge(self.sem, self.post(ins))


def trunk(nc, x, c, ada_w, ada_b, norm1_g, norm2_g, cm_w1, cm_b1, cm_dw, cm_dwb, cm_ln_g, cm_ln_b,
          cm_w2, cm_b2, rg_wy, rg_by, rg_wx, rg_bx, rg_cw, rg_cb, rg_wa, rg_ba, rg_wi, rg_bi,
          rg_lambda, rg_wo, rg_bo, moe_wg, moe_bg, moe_wr, moe_br, moe_w_gate, moe_w_up,
          moe_w_down, fin_ada_w, fin_ada_b, fin_g, out):
    ctx = ExitStack()
    with ctx:
        def sb(name, shape, dt=F32):
            return ctx.enter_context(nc.sbuf_tensor(name, shape, dt))

        def sem(name):
            return ctx.enter_context(nc.semaphore(name))

        ps = ctx.enter_context(nc.psum_tensor("ps", [P, 8, 512], F32))

        wbuf = sb("wbuf", [P, 24 * 1024])
        adabuf = sb("adabuf", [P, 2, 4, D])
        wab = sb("wab", [P, 2, HEADS, 2, 256])
        X = sb("X", [P, DC, T])
        H = sb("H", [P, DC, T])
        B = sb("B", [P, DC, T])
        C = sb("C", [P, DC, T])
        Dd = sb("Dd", [P, DC, T])
        V = sb("V", [P, DC * (T + TAPS - 1)])
        sg = sb("sg", [P, 2, T])
        rowsum = sb("rowsum", [P, D])
        modraw = sb("modraw", [P, 14 * DC])
        par = sb("par", [P, 5 * P])
        mod = sb("mod", [P, 14 * DC])
        wgr = sb("wgr", [P, 2, DC, NG + NE])
        brow = sb("brow", [1, 2, NG + NE])
        cb32 = sb("cb32", [P, DC, 32])
        rs = sb("rs", [P, T])
        gs = sb("gs", [P, DC])
        gb = sb("gb", [P, DC])
        small = sb("small", [P, 8, DC])
        ident = sb("ident", [P, P])
        onesd = sb("onesd", [P, P])
        ones = sb("ones", [P, P])
        eps = sb("eps", [P, 1])
        upper = sb("upper", [P, P])
        sel = sb("sel", [P, 1])
        iota0 = sb("iota0", [P, P])
        iota1 = sb("iota1", [P, P])
        rev = sb("rev", [P, NE])
        blk = sb("blk", [P, 2 * MAXP])
        thr = sb("thr", [P, T // SLOTS])
        lg = sb("lg", [P, TT, NG + NE])
        r4 = sb("r4", [P, 3, TT, NG])
        r1 = sb("r1", [P, 16, TT])
        cnt = sb("cnt", [P, 4, NE])
        cmp3 = H[:, 0:5, :].rearrange("p c t -> p (c t)").rearrange("p (b e) -> p b e", e=NE)
        dflat = Dd[:, :, :].rearrange("p c t -> p (c t)")
        r32 = dflat[:, 0:6 * TT * NE].rearrange("p (i a e) -> p i a e", i=6, a=TT)
        dfree = 6 * TT * NE
        tabf = sb("tabf", [P, 4 * MAXP])
        tab = sb("tab", [1, 4 * MAXP + 2], I32)
        gslot = sb("gslot", [P, 2, TT])
        gw = sb("gw", [P, 2, TT])
        pick, gate1, gate2 = (dflat[:, dfree + i * TT * P:dfree + (i + 1) * TT * P].rearrange("p (a s) -> p a s", a=TT)
                              for i in range(3))
        scat = sg[:, 0, :]

        w1 = wbuf[:, 0:16384].rearrange("p (k n) -> p k n", k=DC)
        w2 = wbuf[:, 16384:24576].rearrange("p (k n) -> p k n", k=DC)
        rgw = [wbuf[:, i * 8192:(i + 1) * 8192].rearrange("p (k n) -> p k n", k=DC) for i in range(3)]
        vconf = V[:, :].rearrange("p (c t) -> p c t", c=DC)
        vlru = V[:, 0:DC * (T + LTAPS - 1)].rearrange("p (c t) -> p c t", c=DC)
        vflat = V[:, 0:DC * T].rearrange("p (c t) -> p c t", c=DC)
        htok = B[:, :, :].rearrange("p (a c) t -> p a (c t)", a=TT)
        xg = C[:, 0:4, :].rearrange("p c t -> p (c t)").rearrange("p (k s) -> p k s", k=DC)
        hid = V[:, 0:F]
        hidT = V[:, F:2 * F].rearrange("p (c s) -> p c s", c=FC)
        dn = V[:, 2 * F:2 * F + D]
        sigb = C[:, 4:6, :].rearrange("p c t -> p (c t)")
        xin = B[:, :, :].rearrange("p (a c) t -> p a (c t)", a=TT)
        ada_alt = {part: wbuf[:, o:o + DC * D].rearrange("p (k n) -> p k n", k=DC)
                   for part, o in ((1, 16384), (6, 0), (10, 0))}
        ptile = [wab[:, 0, 0, 0, 0:P] if i == 1 else C[:, i, 0:P] for i in range(5)]

        diag = [t[:, i // 2, (i % 2) * P:(i % 2 + 1) * P] for t in (C, Dd) for i in range(NDIAG // 2)]

        s_x = sem("s_x")
        s_par = [sem(f"s_par{i}") for i in range(5)]
        s_router = sem("s_router")
        s_w1 = [sem(f"s_w1_{q}") for q in range(DC // 2)]
        s_w2 = sem("s_w2")
        s_wx, s_wy, s_wo, s_wab = sem("s_wx"), sem("s_wy"), sem("s_wo"), sem("s_wab")
        ada_landed = [sem("ada_landed0"), sem("ada_landed1")]
        ada_alt_landed = sem("ada_alt_landed")
        ada_used = sem("ada_used")
        consts = sem("consts")
        pool_link = sem("pool_link")
        act_link = sem("act_link")
        dve_link = sem("dve_link")
        sel_ready = sem("sel_ready")
        par_mm, par_ready = sem("par_mm"), sem("par_ready")
        x_mm, x_ready = sem("x_mm"), sem("x_ready")
        csig, cact = sem("csig"), sem("cact")
        rows_ready, cols_mm, cols_ready, mod_ready = sem("rows_ready"), sem("cols_mm"), sem("cols_ready"), sem("mod_ready")
        sq_ready, ms_mm, xn_ready, h_ready = sem("sq_ready"), sem("ms_mm"), sem("xn_ready"), sem("h_ready")
        gs_ready = sem("gs_ready")
        root_ready, ln_root = sem("root_ready"), sem("ln_root")
        b2_ready, b_ready = sem("b2_ready"), sem("b_ready")
        glu_mm, sg_ready, v_ready = sem("glu_mm"), sem("sg_ready"), sem("v_ready")
        pad_ready = sem("pad_ready")
        conv_dve, conv_mm, conv_pe = sem("conv_dve"), sem("conv_mm"), sem("conv_pe")
        diag_ready, diag_used = sem("diag_ready"), sem("diag_used")
        mean_mm, cen_ready, csq_ready, var_mm, z_ready = sem("mean_mm"), sem("cen_ready"), sem("csq_ready"), sem("var_mm"), sem("z_ready")
        zs_ready, act_in = sem("zs_ready"), sem("act_in")
        o_mm = sem("o_mm")
        pool_mod, xb_ready = sem("pool_mod"), sem("xb_ready")
        ux_mm, ux_ready, u_ready = sem("ux_mm"), sem("ux_ready"), sem("u_ready")
        q_mm, q_ready, g_in, g_sig, y_ready = sem("q_mm"), sem("q_ready"), sem("g_in"), sem("g_sig"), sem("y_ready")
        gate_mm, rg_ready, ta_ready, nk_in, nk_exp, nk_ln, nk_ready = (sem(n) for n in (
            "gate_mm", "rg_ready", "ta_ready", "nk_in", "nk_exp", "nk_ln", "nk_ready"))
        iu_ready, hs_ready = sem("iu_ready"), sem("hs_ready")
        lg_mm, ge_in, ge_ready, mask_ready, rank_mm, route_ready = (sem(n) for n in (
            "lg_mm", "ge_in", "ge_ready", "mask_ready", "rank_mm", "route_ready"))
        ht_mm, ht_dve, ht_act = sem("ht_mm"), sem("ht_dve"), sem("ht_act")
        fin_mm, s_out = sem("fin_mm"), sem("s_out")

        class Moe:
            def __init__(self, l):
                def s(n):
                    return sem(f"moe{l}_{n}")
                self.landed = [s(f"landed{i}") for i in range(6 * NSUB)]
                self.used = [s(f"used{i}") for i in range(6)]
                self.pick, self.gate, self.link = s("pick"), s("gate"), s("link")
                self.gath, self.xga, self.xgd = s("gather"), s("xg_act"), s("xg_dve")
                self.sig, self.hid = s("sig"), s("hid")
                self.ht_mm, self.ht = s("hidT_mm"), s("hidT")
                self.sc_mm, self.sc = s("scat_mm"), s("scat")
                self.dna, self.dnd = s("dn_act"), s("dn_dve")
                self.y = s("y")

        moe = [Moe(0), Moe(1)]

        def pcol(off, n=1):
            return par[:, off:off + n]

        def v8(t):
            return t.rearrange("l (c p) -> (l c) p", p=P)

        def mcol(part, ch):
            return mod[:, part * DC + ch:part * DC + ch + 1]

        def ada_src(part):
            if part < 12:
                return ada_w[part // 6, :, (part % 6) * D:(part % 6 + 1) * D]
            return fin_ada_w[:, (part - 12) * D:(part - 11) * D]

        block = ctx.enter_context(nc.Block())

        @block.sync
        def _(sp):
            def ada_load(part):
                src = ada_src(part).rearrange("(k p) n -> p k n", p=P)
                if part in ADA_ALT:
                    sp.dma_start(ada_alt[part], src).then_inc(ada_alt_landed, 16)
                    return
                n = ADA_BUF.index(part)
                for h in range(2):
                    if (part, h) == (0, 1):
                        sp.wait_ge(s_par[0], 16 * PAR_DMAS[0])
                    if part:
                        sp.wait_ge(ada_used, 2 * ADA_BUF[n - 1] + h + 1)
                    sp.dma_start(adabuf[:, h, :, :], src[:, 4 * h:4 * h + 4, :]).then_inc(ada_landed[h], 16)

            def rows(w):
                return w.rearrange("(k p) n -> p k n", p=P)

            def experts_src(l):
                return [w[l].rearrange("e (p k) f -> (e p) (k f)", p=P) for w in (moe_w_gate, moe_w_up, moe_w_down)]

            def guess(l, matrix):
                for h in range(2):
                    for j in range(NSUB):
                        slot = (2 * matrix + h) * NSUB + j
                        sp.dma_start(wbuf[:, slot * 2048:(slot + 1) * 2048],
                                     experts_src(l)[matrix][j * P:(j + 1) * P, h * 2048:(h + 1) * 2048]
                                     ).then_inc(moe[l].landed[slot], 16)

            def vec(tile, row, src, n):
                sp.dma_start(ptile[tile][row:row + n, :], src).then_inc(s_par[tile], 16)

            sp.dma_start(xin, x[0].rearrange("(a p) d -> p a d", p=P)).then_inc(s_x, 16)
            ada_load(0)
            ada_load(1)
            for q in range(DC // 2):
                for half in range(2):
                    cols = slice(half * D + 2 * q * P, half * D + 2 * (q + 1) * P)
                    sp.dma_start(w1[:, :, cols], rows(cm_w1[0])[:, :, cols]).then_inc(s_w1[q], 16)
            for n, t in (("by", rg_by), ("bx", rg_bx), ("cb", rg_cb), ("lam", rg_lambda), ("bo", rg_bo)):
                vec(1, PAR_B[n] - P, v8(t), 8)
            vec(1, PAR_B["ba"] - P, rg_ba[0].rearrange("h (c p) -> (h c) p", p=P), 8)
            vec(1, PAR_B["bi"] - P, rg_bi[0].rearrange("h (c p) -> (h c) p", p=P), 8)
            vec(1, PAR_B["cw"] - P, rg_cw[0].rearrange("k (c p) -> (k c) p", p=P), 32)
            for l in range(2):
                sp.dma_start(wgr[:, l, :, 0:NG], moe_wg[l].rearrange("(k p) g -> p k g", p=P)).then_inc(s_router, 16)
                sp.dma_start(wgr[:, l, :, NG:], moe_wr[l].rearrange("(k p) g -> p k g", p=P)).then_inc(s_router, 16)
            sp.dma_start(brow[0:1, :, 0:NG], moe_bg.rearrange("(a l) g -> a l g", a=1)).then_inc(s_router, 16)
            sp.dma_start(brow[0:1, :, NG:], moe_br.rearrange("(a l) g -> a l g", a=1)).then_inc(s_router, 16)
            ada_load(2)
            sp.wait_ge(ada_used, 4)
            sp.dma_start(w2, rows(cm_w2[0])).then_inc(s_w2, 16)
            ada_load(3)
            sp.wait_ge(glu_mm, DC)
            ada_load(6)
            guess(0, 1)
            ada_load(4)
            ada_load(5)
            sp.wait_ge(o_mm, DC // 2)
            guess(0, 2)
            sp.wait_ge(ada_used, 2 * 6 + 2)
            guess(0, 0)
            ada_load(7)

            def experts(l):
                m = moe[l]
                sp.wait_ge(route_ready, l + 1)
                passes = sp.value_load(tab[0:1, 0:1], min_val=1, max_val=MAXP)
                with sp.Fori(1, passes + 1) as turn:
                    ids = [sp.value_load(tab[0:1, bass.ds(turn * NSUB + j, 1)], min_val=0, max_val=NE - 1)
                           for j in range(NSUB)]
                    load = [sp.value_load(tab[0:1, bass.ds(turn * NSUB + j + 2 * MAXP, 1)], min_val=0, max_val=1)
                            for j in range(NSUB)]
                    for ph in range(6):
                        src, h = experts_src(l)[ph // 2], ph % 2
                        for j in range(NSUB):
                            slot = ph * NSUB + j
                            dst = wbuf[:, slot * 2048:(slot + 1) * 2048]
                            sp.wait_ge(m.landed[slot], turn * 16)
                            sp.wait_ge(m.used[ph], turn)
                            sp.dma_start(dst, src[bass.ds(ids[j] * P, P), h * 2048:(h + 1) * 2048],
                                         cond=(load[j] > 0)).then_inc(m.landed[slot], 16)
                return sp.snap(passes + 1)

            all_used = experts(0)
            ada_load(8)
            for i, (w, s) in enumerate(((rg_wy, s_wy), (rg_wx, s_wx), (rg_wo, s_wo))):
                sp.wait_ge(moe[0].used[2 * i], all_used)
                sp.wait_ge(moe[0].used[2 * i + 1], all_used)
                sp.dma_start(rgw[i], rows(w[0])).then_inc(s, 16)
                if i == 1:
                    for n, g in enumerate((rg_wa, rg_wi)):
                        sp.dma_start(wab[:, n, :, :, :], g[0].rearrange("h (i p) j -> p h i j", p=P)).then_inc(s_wab, 16)
            ada_load(9)
            sp.wait_ge(q_mm, DC // 2)
            ada_load(10)
            sp.wait_ge(ux_mm, DC // 2)
            guess(1, 1)
            ada_load(11)
            sp.wait_ge(ada_used, 2 * 10 + 2)
            guess(1, 0)
            ada_load(12)
            sp.wait_ge(o_mm, DC)
            guess(1, 2)
            ada_load(13)
            experts(1)
            for a in range(TT):
                sp.wait_ge((ht_dve, ht_act)[a], (1, 2 * TT + 1)[a])
                sp.dma_start(out[0, a * P:(a + 1) * P, :], htok[:, a, :]).then_inc(s_out, 16)
            sp.wait_ge(s_out, 16 * TT)

        @block.gpsimd
        def _(pool):
            link = Link(pool, pool_link)
            g = nc.gpsimd
            link(g.memset(ident[:], 0.0))
            link(g.memset(ones[:], 1.0))
            g.affine_select(out=ident[:], in_=ident[:], compare_op=ALU.not_equal, fill=1.0, base=0,
                            pattern=[[-1, P]], channel_multiplier=1).then_inc(consts, 1)
            g.affine_select(out=upper[:], in_=ones[:], compare_op=ALU.is_gt, fill=0.0, base=0,
                            pattern=[[1, P]], channel_multiplier=-1).then_inc(consts, 1)
            g.memset(onesd[:], 1.0 / D).then_inc(consts, 1)
            kw = dict(allow_small_or_imprecise_dtypes=True)
            g.iota(iota0[:], [[1, P]], base=0, channel_multiplier=0, **kw).then_inc(consts, 1)
            g.iota(iota1[:], [[1, P]], base=P, channel_multiplier=0, **kw).then_inc(consts, 1)
            g.iota(rev[:], [[-1, NE]], base=NE, channel_multiplier=0, **kw).then_inc(consts, 1)
            g.iota(blk[:], [[1, 2 * MAXP]], base=0, channel_multiplier=0, **kw).then_inc(consts, 1)
            g.iota(thr[:], [[SLOTS, T // SLOTS]], base=0, channel_multiplier=0, **kw).then_inc(consts, 1)
            g.memset(eps[:], EPS).then_inc(consts, 1)
            g.memset(vconf[:, :, 0:TAPS - 1], 0.0).then_inc(pad_ready, 1)

            pool.wait_ge(par_ready, 4)
            for n, (ch, k) in enumerate((ch, k) for ch in PE_CHUNKS for k in range(TAPS)):
                if n >= NDIAG:
                    pool.wait_ge(diag_used, n - NDIAG + 1)
                g.tensor_scalar(diag[n % NDIAG], ident[:], pcol(dw_col(k, ch)), None, ALU.mult).then_inc(diag_ready, 1)

            def x_bias(l, part, bias):
                gate = mod[:, part * DC:(part + 1) * DC]
                pool.wait_ge(cols_ready, part + 1)
                link(g.tensor_tensor(gate, modraw[:, part * DC:(part + 1) * DC],
                                     par[:, PAR_ADA + part * DC:PAR_ADA + (part + 1) * DC], ALU.add))
                link(g.tensor_tensor(gb[:, :], gate, pcol(bias, DC), ALU.mult))
                pool.wait_ge(xn_ready, (2 * l + 1) * DC // 2)
                for n in range(DC):
                    g.tensor_scalar(X[:, n, :], X[:, n, :], gb[:, n:n + 1], None, ALU.add).then_inc(xb_ready, 1)

            x_bias(0, 2, PAR_A["b2"])

            for q in range(DC // 2):
                y = B[:, 2 * q:2 * q + 2, :]
                pool.wait_ge(q_ready, 2 * q + 2)
                link(g.tensor_tensor(sg[:, :, :], y, y, ALU.mult))
                link(g.tensor_scalar(sg[:, :, :], sg[:, :, :], GELU_A, 1.0, ALU.mult, ALU.add))
                g.tensor_tensor(sg[:, :, :], sg[:, :, :], y, ALU.mult).then_inc(g_in, 1)
                pool.wait_ge(g_sig, q + 1)
                g.tensor_tensor(y, y, sg[:, :, :], ALU.mult).then_inc(y_ready, 1)
                pool.wait_ge(y_ready, q + 1)
            pool.wait_ge(par_ready, 5)
            x_bias(1, 8, PAR_B["bo"])
            for h in range(HEADS):
                two = slice(2 * h, 2 * h + 2)
                pool.wait_ge(rg_ready, 4 * (h + 1))
                g.tensor_tensor(vflat[:, two, :], vflat[:, two, :], C[:, two, :], ALU.mult).then_inc(iu_ready, 1)

        @block.scalar
        def _(act):
            a = nc.scalar
            link = Link(act, act_link)

            def vec(tile, row, src, n):
                act.dma_start(ptile[tile][row:row + n, :], src).then_inc(s_par[tile], 16)

            vec(0, PAR_A["c"], v8(c), 8)
            vec(0, PAR_A["n1"], v8(norm1_g), 16)
            vec(0, PAR_A["n2"], v8(norm2_g), 16)
            vec(0, PAR_A["fin"], fin_g.rearrange("(c p) -> c p", p=P), 8)
            vec(0, PAR_A["b1"], v8(cm_b1), 16)
            for n, t in (("dwb", cm_dwb), ("lng", cm_ln_g), ("lnb", cm_ln_b), ("b2", cm_b2)):
                vec(0, PAR_A[n], v8(t), 8)
            vec(2, 0, ada_b.rearrange("l (c p) -> (l c) p", p=P), 96)
            vec(2, 96, fin_ada_b.rearrange("(c p) -> c p", p=P), 16)
            dwr = cm_dw[0].rearrange("k (c p) -> (k c) p", p=P)
            vec(3, 0, dwr[0:DW_ROWS, :], DW_ROWS)
            vec(4, 0, dwr[DW_ROWS:2 * DW_ROWS, :], DW_ROWS)

            def ada_rows(part):
                act.wait_ge(ada_used, 2 * part + 2)
                a.activation(rowsum[:, :], ps[:, 6:8, :].rearrange("p b n -> p (b n)"), ACT.Copy).then_inc(rows_ready, 1)

            def ada_back(part):
                act.wait_ge(cols_mm, part + 1)
                a.activation(modraw[:, part * DC:(part + 1) * DC], ps[:, 6, 0:DC], ACT.Copy).then_inc(cols_ready, 1)

            def ada(part):
                ada_rows(part)
                ada_back(part)

            def norm_squares(k):
                for ch in range(DC):
                    act.wait_ge(x_ready, k * DC + ch + 1)
                    a.activation(H[:, ch, :], X[:, ch, :], ACT.Square).then_inc(sq_ready, 1)

            def norm_root(k):
                act.wait_ge(ms_mm, k + 1)
                a.activation(rs[:, :], ps[:, 4, 0:T], ACT.Sqrt, bias=eps[:, 0:1]).then_inc(root_ready, 1)

            def norm_stats(k):
                norm_squares(k)
                norm_root(k)

            def norm_out(k, sh_part):
                act.wait_ge(gs_ready, k + 1)
                for ch in range(DC):
                    act.wait_ge(xn_ready, (k * DC + ch) // 2 + 1)
                    a.activation(H[:, ch, :], H[:, ch, :], ACT.Identity, bias=mcol(sh_part, ch),
                                 scale=gs[:, ch:ch + 1]).then_inc(h_ready, 1)

            norm_squares(0)
            act.wait_ge(par_ready, 1)
            a.activation(small[:, 0, :], pcol(PAR_A["c"], DC), ACT.Sigmoid).then_inc(csig, 1)
            act.wait_ge(consts, 9)
            norm_root(0)
            ada(0)
            ada(1)
            norm_out(0, 0)

            for m in range(DC):
                act.wait_ge(glu_mm, m + 1)
                if m >= 2:
                    act.wait_ge(v_ready, m - 1)
                a.activation(sg[:, m % 2, :], ps[:, m % 4, T:2 * T], ACT.Sigmoid,
                             bias=pcol(PAR_A["b1"] + DC + m)).then_inc(sg_ready, 1)
                if m in ADA_IN_W1:
                    ada(ADA_IN_W1[m])
            for n, ch in enumerate(PE_CHUNKS):
                act.wait_ge(conv_mm, n + 1)
                a.activation(B[:, ch, :], ps[:, 5, 0:T], ACT.Identity, bias=pcol(PAR_A["dwb"] + ch)).then_inc(conv_pe, 1)
            for q in range(DC // 2):
                act.wait_ge(cen_ready, q + 1)
                a.activation(Dd[:, 2 * q:2 * q + 2, :], C[:, 2 * q:2 * q + 2, :], ACT.Square).then_inc(csq_ready, 1)
            act.wait_ge(var_mm, 1)
            a.activation(rs[:, :], ps[:, 5, T:2 * T], ACT.Sqrt, bias=eps[:, 0:1]).then_inc(ln_root, 1)
            for ch in range(DC):
                act.wait_ge(z_ready, ch // 2 + 1)
                a.activation(Dd[:, ch, :], C[:, ch, :], ACT.Sigmoid, bias=pcol(PAR_A["lnb"] + ch),
                             scale=pcol(PAR_A["lng"] + ch)).then_inc(zs_ready, 1)
            ada(3)
            ada(4)
            act.wait_ge(nk_in, 1)
            a.activation(small[:, 3, :], small[:, 2, :], ACT.Exp, scale=-1.0).then_inc(nk_exp, 1)
            act.wait_ge(nk_exp, 2)
            a.activation(small[:, 5, :], small[:, 4, :], ACT.Ln).then_inc(nk_ln, 1)
            norm_stats(1)
            norm_out(1, 3)

            def route(l):
                act.wait_ge(ge_in, 2 * l + 1)
                a.activation(r4[:, 1, :, :], r4[:, 0, :, :], ACT.Exp).then_inc(ge_ready, 1)
                act.wait_ge(ge_in, 2 * l + 2)
                a.activation(r1[:, 7, :], r1[:, 5, :], ACT.Exp).then_inc(ge_ready, 1)

            def tokens(l):
                for t in range(TT):
                    act.wait_ge(ht_mm, l + 1)
                    a.activation(htok[:, t, :], ps[:, 2 * t:2 * t + 2, :].rearrange("p b n -> p (b n)"),
                                 ACT.Copy).then_inc(ht_act, 1)

            def experts(l, part):
                m = moe[l]
                act.wait_ge(m.gath, 1)
                a.activation(xg[:, 0:4, :], ps[:, 6, :].rearrange("p (k s) -> p k s", k=4), ACT.Copy).then_inc(m.xga, 1)
                act.sem_inc(m.dna, 1)
                act.wait_ge(route_ready, l + 1)
                passes = act.value_load(tab[0:1, 0:1], min_val=1, max_val=MAXP)

                def turn(i):
                    act.wait_ge(m.used[1], i + 2)
                    act.wait_ge(m.hid, i + 1)
                    a.activation(sigb, ps[:, 4, :], ACT.Sigmoid).then_inc(m.sig, 1)
                    if isinstance(i, int):
                        ada(part)
                    act.wait_ge(m.gath, i + 2)
                    a.activation(xg[:, 0:4, :], ps[:, 6, :].rearrange("p (k s) -> p k s", k=4), ACT.Copy).then_inc(m.xga, 1)
                    act.wait_ge(m.ht_mm, i + 1)
                    a.activation(hidT, ps[:, 4, :].rearrange("p (c s) -> p c s", c=FC), ACT.Copy).then_inc(m.ht, 1)
                    act.wait_ge(m.used[5], i + 2)
                    a.activation(dn[:, 0:512], ps[:, 6, :], ACT.Copy).then_inc(m.dna, 1)

                turn(0)
                with act.Fori(1, passes) as i:
                    turn(i)

            ada_rows(5)
            tokens(0)
            ada_back(5)
            ada(6)
            route(0)
            experts(0, 7)

            norm_stats(2)
            norm_out(2, 6)
            ada(8)
            for n in range(DC):
                act.wait_ge(q_mm, n // 2 + 1)
                a.activation(B[:, n, :], ps[:, n // 2, (n % 2) * T:(n % 2 + 1) * T], ACT.Identity,
                             bias=pcol(PAR_B["by"] + n)).then_inc(q_ready, 1)
            for q in range(DC // 2):
                act.wait_ge(g_in, q + 1)
                a.activation(sg[:, :, :], sg[:, :, :], ACT.Sigmoid, scale=GELU_B).then_inc(g_sig, 1)
            act.wait_ge(pad_ready, 2)
            for n in range(DC):
                act.wait_ge(ux_mm, n // 2 + 1)
                a.activation(vlru[:, n, LTAPS - 1:], ps[:, n // 2, (n % 2) * T:(n % 2 + 1) * T], ACT.Identity,
                             bias=pcol(PAR_B["bx"] + n)).then_inc(ux_ready, 1)
            for h in range(HEADS):
                act.wait_ge(gate_mm, h + 1)
                act.wait_ge(u_ready, DC)
                for j in range(2):
                    n = 2 * h + j
                    a.activation(Dd[:, n, :], ps[:, 2 * (h % 2), j * T:(j + 1) * T], ACT.Sigmoid,
                                 bias=pcol(PAR_B["ba"] + n)).then_inc(rg_ready, 1)
                    a.activation(vflat[:, n, :], ps[:, 2 * (h % 2) + 1, j * T:(j + 1) * T], ACT.Sigmoid,
                                 bias=pcol(PAR_B["bi"] + n)).then_inc(rg_ready, 1)
            act.wait_ge(nk_ready, 1)
            act.wait_ge(rg_ready, 4 * HEADS)
            for n in range(DC):
                a.activation(H[:, n, :], Dd[:, n, :], ACT.Tanh, scale=small[:, 2, n:n + 1]).then_inc(ta_ready, 1)
                act.wait_ge(ta_ready, 2 * n + 1)
                a.activation(Dd[:, n, :], Dd[:, n, :], ACT.Exp, scale=small[:, 2, n:n + 1]).then_inc(ta_ready, 1)
            for h in range(HEADS):
                act.wait_ge(b2_ready, h + 1)
                a.activation(H[:, 2 * h:2 * h + 2, :], H[:, 2 * h:2 * h + 2, :], ACT.Sqrt, scale=-1.0).then_inc(b_ready, 1)
            ada(9)
            ada(10)
            norm_stats(3)
            norm_out(3, 9)
            ada_rows(11)
            tokens(1)
            ada_back(11)
            ada(12)
            route(1)
            experts(1, 13)
            norm_stats(4)
            norm_out(4, 12)
            act.wait_ge(fin_mm, 2)
            a.activation(htok[:, 1, :], ps[:, 2:4, :].rearrange("p b n -> p (b n)"), ACT.Copy).then_inc(ht_act, 1)

        @block.vector
        def _(dve):
            v = nc.vector
            link = Link(dve, dve_link)

            dve.wait_ge(consts, 9)
            v.tensor_reduce(sel[:, :], ident[:, 0:P:32], AX.X, ALU.add).then_inc(sel_ready, 1)
            for ch in range(DC):
                dve.wait_ge(x_mm, ch // 2 + 1)
                v.tensor_copy(X[:, ch, :], ps[:, ch // 2, (ch % 2) * T:(ch % 2 + 1) * T]).then_inc(x_ready, 1)

            def params(n, i):
                dve.wait_ge(par_mm, n + 1)
                v.tensor_copy(par[:, i * P:i * P + PAR_TILES[i]],
                              ps[:, 4 + n % 4, 0:PAR_TILES[i]]).then_inc(par_ready, 1)

            params(0, 0)
            dve.wait_ge(csig, 1)
            dve.wait_ge(par_ready, 1)
            link(v.tensor_tensor(small[:, 1, :], small[:, 0, :], pcol(PAR_A["c"], DC), ALU.mult))
            v.tensor_copy(cb32[:, :, :], small[:, 1, :].rearrange("p (c o) -> p c o", o=1).to_broadcast([P, DC, 32])).then_inc(cact, 1)
            for n, i in enumerate((2, 3, 4)):
                params(n + 1, i)

            mods = [0]

            def ada_bias(first, last):
                dve.wait_ge(cols_ready, last + 1)
                both = slice(first * DC, (last + 1) * DC)
                v.tensor_tensor(mod[:, both], modraw[:, both], par[:, PAR_ADA + first * DC:PAR_ADA + (last + 1) * DC],
                                ALU.add).then_inc(mod_ready, 1)
                mods[0] += 1
                dve.wait_ge(mod_ready, mods[0])

            def norm_gain(k, gain, sc_part):
                if k >= 1:
                    dve.wait_ge(h_ready, k * DC)
                v.scalar_tensor_tensor(out=gs[:, :], in0=mod[:, sc_part * DC:(sc_part + 1) * DC], scalar=1.0,
                                       in1=pcol(gain, DC), op0=ALU.add, op1=ALU.mult).then_inc(gs_ready, 1)

            def pairs(t):
                return t.rearrange("p (o t) -> p o t", o=1).to_broadcast([P, 2, T])

            def norm_out(k):
                dve.wait_ge(root_ready, k + 1)
                link(v.reciprocal(rs[:, :], rs[:, :]))
                dve.wait_ge(x_ready, (k + 1) * DC)
                for q in range(DC // 2):
                    two = slice(2 * q, 2 * q + 2)
                    v.tensor_tensor(H[:, two, :], X[:, two, :], pairs(rs[:, :]), ALU.mult).then_inc(xn_ready, 1)

            def out_proj(k, g1_part):
                for n in range(DC):
                    dve.wait_ge(o_mm, (k * DC + n) // 2 + 1)
                    dve.wait_ge(xb_ready, k * DC + n + 1)
                    v.scalar_tensor_tensor(out=X[:, n, :], in0=ps[:, n // 2, (n % 2) * T:(n % 2 + 1) * T],
                                           scalar=mcol(g1_part, n), in1=X[:, n, :], op0=ALU.mult,
                                           op1=ALU.add).then_inc(x_ready, 1)

            norm_out(0)

            ada_bias(0, 1)
            norm_gain(0, PAR_A["n1"], 1)

            dve.wait_ge(pad_ready, 1)

            def glu(m):
                dve.wait_ge(sg_ready, m + 1)
                v.scalar_tensor_tensor(out=vconf[:, m, TAPS - 1:], in0=ps[:, m % 4, 0:T], scalar=pcol(PAR_A["b1"] + m),
                                       in1=sg[:, m % 2, :], op0=ALU.add, op1=ALU.mult).then_inc(v_ready, 1)

            glu(0)
            glu(1)
            for g in range(0, DVE_CHUNKS, 2):
                dve.wait_ge(v_ready, g + 2)
                before = {}
                for k in range(TAPS):
                    for ch in (g, g + 1):
                        acc = B[:, ch, :]
                        if k == 0:
                            ins = v.tensor_scalar(acc, vconf[:, ch, 0:T], pcol(dw_col(0, ch)), pcol(PAR_A["dwb"] + ch),
                                                  ALU.mult, ALU.add)
                        else:
                            dve.wait_ge(dve_link, before[ch])
                            ins = v.scalar_tensor_tensor(out=acc, in0=vconf[:, ch, k:k + T], scalar=pcol(dw_col(k, ch)),
                                                         in1=acc, op0=ALU.mult, op1=ALU.add)
                        if k < TAPS - 1:
                            before[ch] = link.post(ins)
                        else:
                            ins.then_inc(conv_dve, 1)
                    if (g, k) in GLU_AT:
                        glu(GLU_AT[g, k])
            params(4, 1)
            dve.wait_ge(mean_mm, 1)
            for q in range(DC // 2):
                two = slice(2 * q, 2 * q + 2)
                v.tensor_tensor(C[:, two, :], B[:, two, :], pairs(ps[:, 4, 0:T]), ALU.subtract).then_inc(cen_ready, 1)
            dve.wait_ge(ln_root, 1)
            link(v.reciprocal(rs[:, :], rs[:, :]))

            def silu(ch):
                dve.wait_ge(dve_link, affine[ch])
                dve.wait_ge(zs_ready, ch + 1)
                v.tensor_tensor(B[:, ch, :], H[:, ch, :], Dd[:, ch, :], ALU.mult).then_inc(act_in, 1)

            affine = {}
            for q in range(DC // 2):
                two = slice(2 * q, 2 * q + 2)
                v.tensor_tensor(C[:, two, :], C[:, two, :], pairs(rs[:, :]), ALU.mult).then_inc(z_ready, 1)
                dve.wait_ge(z_ready, q + 1)
                for ch in (2 * q, 2 * q + 1):
                    affine[ch] = link.post(v.tensor_scalar(H[:, ch, :], C[:, ch, :], pcol(PAR_A["lng"] + ch),
                                                           pcol(PAR_A["lnb"] + ch), ALU.mult, ALU.add))
                    if q:
                        silu(ch - 2)
            silu(DC - 2)
            silu(DC - 1)
            ada_bias(3, 4)
            norm_gain(1, PAR_A["n2"], 4)
            dve.wait_ge(par_ready, 5)
            lam = pcol(PAR_B["lam"], DC)
            link(v.tensor_scalar(small[:, 4, :], lam, -1.0, None, ALU.mult))
            v.tensor_tensor(small[:, 2, :], lam, small[:, 4, :], ALU.max).then_inc(nk_in, 1)
            link(v.tensor_scalar(small[:, 6, :], small[:, 4, :], 0.0, None, ALU.max))
            dve.wait_ge(nk_exp, 1)
            v.tensor_scalar(small[:, 4, :], small[:, 3, :], 1.0, None, ALU.add).then_inc(nk_exp, 1)
            dve.wait_ge(nk_exp, 2)
            link(v.tensor_scalar(small[:, 7, :], small[:, 4, :], 1.0, None, ALU.subtract))
            link(v.tensor_scalar(small[:, 0, :], small[:, 7, :], 0.0, None, ALU.is_equal))
            link(v.tensor_tensor(small[:, 7, :], small[:, 7, :], small[:, 0, :], ALU.add))
            link(v.reciprocal(small[:, 7, :], small[:, 7, :]))
            dve.wait_ge(nk_ln, 1)
            link(v.tensor_tensor(small[:, 5, :], small[:, 5, :], small[:, 0, :], ALU.add))
            link(v.tensor_tensor(small[:, 5, :], small[:, 5, :], small[:, 7, :], ALU.mult))
            link(v.tensor_tensor(small[:, 5, :], small[:, 5, :], small[:, 3, :], ALU.mult))
            link(v.tensor_tensor(small[:, 5, :], small[:, 5, :], small[:, 6, :], ALU.add))
            v.tensor_scalar(small[:, 2, :], small[:, 5, :], -8.0, None, ALU.mult).then_inc(nk_ready, 1)
            out_proj(0, 2)
            norm_out(1)

            def picks(lk, io, done):
                first = [lk.post(v.tensor_scalar(pick[:, a, :], io[:], gslot[:, 0, a:a + 1], None, ALU.is_equal))
                         for a in range(TT)]
                for a in range(TT):
                    lk.eng.wait_ge(lk.sem, first[a])
                    ins = v.scalar_tensor_tensor(out=pick[:, a, :], in0=io[:], scalar=gslot[:, 1, a:a + 1],
                                                 in1=pick[:, a, :], op0=ALU.is_equal, op1=ALU.add)
                    if a < TT - 1:
                        last = lk.post(ins)
                        lk.eng.wait_ge(lk.sem, last)
                    else:
                        ins.then_inc(done, 1)

            def route(l, route_ins):
                v.memset(scat, 0.0).then_inc(moe[l].sc, 1)
                dve.sem_inc(moe[l].hid, 1)
                dve.sem_inc(moe[l].dnd, 1)

                def wide(t, n):
                    return t.rearrange("p (a o) -> p a o", o=1).to_broadcast([P, TT, n])

                dve.wait_ge(lg_mm, l + 1)
                link(v.tensor_copy(lg[:, :, :], ps[:, 5, 0:TT * (NG + NE)].rearrange("p (a g) -> p a g", a=TT)))
                gl, el = lg[:, :, 0:NG], lg[:, :, NG:]
                link(v.tensor_reduce(r1[:, 0, :], gl, AX.X, ALU.max))
                v.tensor_tensor(r4[:, 0, :, :], gl, wide(r1[:, 0, :], NG), ALU.subtract).then_inc(ge_in, 1)
                revg = rev[:, NE - NG:].rearrange("p (o n) -> p o n", o=1).to_broadcast([P, TT, NG])
                reve = rev[:, :].rearrange("p (o n) -> p o n", o=1).to_broadcast([P, TT, NE])
                link(v.tensor_tensor(r4[:, 2, :, :], gl, wide(r1[:, 0, :], NG), ALU.is_equal))
                link(v.tensor_tensor(r4[:, 2, :, :], r4[:, 2, :, :], revg, ALU.mult))
                link(v.tensor_reduce(r1[:, 1, :], r4[:, 2, :, :], AX.X, ALU.max))
                link(v.tensor_tensor(r4[:, 2, :, :], r4[:, 2, :, :], wide(r1[:, 1, :], NG), ALU.is_equal))
                for a in range(TT):
                    gsel = r4[:, 2, a, :].rearrange("p (g o) -> p g o", o=1).to_broadcast([P, NG, EPG])
                    link(v.tensor_tensor(r32[:, 0, a, :].rearrange("p (g e) -> p g e", g=NG),
                                         lg[:, a, NG:].rearrange("p (g e) -> p g e", g=NG), gsel, ALU.mult))
                    link(v.tensor_scalar(r32[:, 1, a, :].rearrange("p (g e) -> p g e", g=NG), gsel, 1.0, BIG,
                                         ALU.subtract, ALU.mult))
                link(v.tensor_tensor(r32[:, 0, :, :], r32[:, 0, :, :], r32[:, 1, :, :], ALU.add))
                for k in range(2):
                    hot = r32[:, 2 + k, :, :]
                    link(v.tensor_reduce(r1[:, 2 + k, :], r32[:, 0, :, :], AX.X, ALU.max))
                    link(v.tensor_tensor(hot, r32[:, 0, :, :], wide(r1[:, 2 + k, :], NE), ALU.is_equal))
                    link(v.tensor_tensor(hot, hot, reve, ALU.mult))
                    link(v.tensor_reduce(r1[:, 4, :], hot, AX.X, ALU.max))
                    link(v.tensor_tensor(hot, hot, wide(r1[:, 4, :], NE), ALU.is_equal))
                    if k == 0:
                        link(v.scalar_tensor_tensor(out=r32[:, 0, :, :], in0=hot, scalar=-3 * BIG, in1=r32[:, 0, :, :],
                                                    op0=ALU.mult, op1=ALU.add))
                v.tensor_tensor(r32[:, 4, :, :], r32[:, 2, :, :], r32[:, 3, :, :], ALU.add).then_inc(mask_ready, 1)
                v.tensor_tensor(r1[:, 5, :], r1[:, 3, :], r1[:, 2, :], ALU.subtract).then_inc(ge_in, 1)
                dve.wait_ge(rank_mm, l + 1)
                link(v.tensor_copy(cnt[:, 0, :], ps[:, 5, 2 * NE + P:3 * NE + P]))
                cw = cmp3[:, 0:NE, 0:T // SLOTS]
                link(v.tensor_tensor(cw, cnt[:, 0, :].rearrange("p (e o) -> p e o", o=1).to_broadcast([P, NE, T // SLOTS]),
                                     thr[:, :].rearrange("p (o n) -> p o n", o=1).to_broadcast([P, NE, T // SLOTS]), ALU.is_gt))
                link(v.tensor_reduce(cnt[:, 1, :], cw, AX.X, ALU.add))
                link(v.tensor_tensor_scan(cnt[:, 2, :], ones[:, 0:NE], cnt[:, 1, :], 0.0, ALU.mult, ALU.add))
                link(v.tensor_tensor(cnt[:, 3, :], cnt[:, 2, :], cnt[:, 1, :], ALU.subtract))
                for a in range(TT):
                    link(v.scalar_tensor_tensor(out=r32[:, 5, a, :], in0=cnt[:, 3, :], scalar=float(SLOTS),
                                                in1=ps[:, 5, P + a * NE:P + (a + 1) * NE], op0=ALU.mult, op1=ALU.add))
                hits = [link.post(v.tensor_tensor(r32[:, k, :, :], r32[:, 5, :, :], r32[:, 2 + k, :, :], ALU.mult))
                        for k in range(2)]
                for k in range(2):
                    dve.wait_ge(dve_link, hits[k])
                    slots = link.post(v.tensor_reduce(gslot[:, k, :], r32[:, k, :, :], AX.X, ALU.add))
                dve.wait_ge(dve_link, slots)
                picks(route_ins, iota0, moe[l].pick)
                link(v.tensor_tensor(cmp3[:, :, :], cnt[:, 2, :].rearrange("p (o e) -> p o e", o=1).to_broadcast([P, 2 * MAXP, NE]),
                                     blk[:, :].rearrange("p (b o) -> p b o", o=1).to_broadcast([P, 2 * MAXP, NE]), ALU.is_le))
                link(v.tensor_reduce(tabf[:, 0:2 * MAXP], cmp3[:, :, :], AX.X, ALU.add))
                link(v.tensor_scalar(tabf[:, 0:2 * MAXP], tabf[:, 0:2 * MAXP], float(NE - 1), None, ALU.min))
                load = tabf[:, 2 * MAXP:4 * MAXP]
                link(v.tensor_scalar(load, blk[:, :], cnt[:, 2, NE - 1:NE], None, ALU.is_lt))
                link(v.tensor_tensor(cnt[:, 0, 0:NSUB], tabf[:, 0:NSUB], blk[:, 0:NSUB], ALU.not_equal))
                link(v.tensor_tensor(load[:, 0:NSUB], load[:, 0:NSUB], cnt[:, 0, 0:NSUB], ALU.mult))
                link(v.tensor_copy(tab[0:1, 2:2 + 4 * MAXP], tabf[0:1, 0:4 * MAXP]))
                link(v.tensor_scalar(tabf[:, 0:MAXP], blk[:, 0:2 * MAXP:2], cnt[:, 2, NE - 1:NE], None, ALU.is_lt))
                link(v.tensor_reduce(tabf[:, MAXP:MAXP + 1], tabf[:, 0:MAXP], AX.X, ALU.add))
                v.tensor_copy(tab[0:1, 0:1], tabf[0:1, MAXP:MAXP + 1]).then_inc(route_ready, 1)

            def experts(l, route_ins):
                m = moe[l]
                dve.wait_ge(m.gath, 1)
                v.tensor_copy(xg[:, 4:8, :], ps[:, 7, :].rearrange("p (k s) -> p k s", k=4)).then_inc(m.xgd, 1)
                dve.wait_ge(ge_ready, 2 * l + 1)
                link(v.tensor_reduce(r1[:, 6, :], r4[:, 1, :, :], AX.X, ALU.add))
                dve.wait_ge(ge_ready, 2 * l + 2)
                e2 = r1[:, 7, :]
                link(v.tensor_scalar(r1[:, 8, :], e2, 1.0, None, ALU.add))
                link(v.tensor_tensor(r1[:, 8, :], r1[:, 8, :], r1[:, 6, :], ALU.mult))
                link(v.reciprocal(gw[:, 0, :], r1[:, 8, :]))
                link(v.tensor_tensor(gw[:, 1, :], gw[:, 0, :], e2, ALU.mult))
                dve.wait_ge(route_ready, l + 1)
                passes = dve.value_load(tab[0:1, 0:1], min_val=1, max_val=MAXP)
                n0 = route_ins.n
                with dve.Fori(0, passes) as i:
                    lk = Link(dve, m.link, i * EXPERT_LINKS + n0)
                    dve.wait_ge(m.pick, i + 1)
                    dve.wait_ge(m.gath, i + 1)
                    picks(lk, iota1, m.pick)
                    dve.wait_ge(m.sc, i + 1)
                    for a in range(TT):
                        for k, dst in ((0, gate1), (1, gate2)):
                            lk(v.tensor_scalar(dst[:, a, :], iota0[:], gslot[:, k, a:a + 1], gw[:, k, a:a + 1],
                                               ALU.is_equal, ALU.mult))
                    v.tensor_tensor(gate1[:, :, :], gate1[:, :, :], gate2[:, :, :], ALU.add).then_inc(m.gate, 1)
                    dve.wait_ge(m.pick, i + 2)
                    lk(v.tensor_scalar(gslot[:, :, :], gslot[:, :, :], float(P), None, ALU.subtract))
                    dve.wait_ge(m.sig, i + 1)
                    lk(v.tensor_tensor(hid, ps[:, 4, :], sigb, ALU.mult))
                    dve.wait_ge(m.used[3], i + 2)
                    v.tensor_tensor(hid, hid, ps[:, 5, :], ALU.mult).then_inc(m.hid, 1)
                    dve.wait_ge(m.gath, i + 2)
                    v.tensor_copy(xg[:, 4:8, :], ps[:, 7, :].rearrange("p (k s) -> p k s", k=4)).then_inc(m.xgd, 1)
                    dve.wait_ge(m.sc_mm, i + 1)
                    v.tensor_copy(scat[:, :], ps[:, 5, 0:T]).then_inc(m.sc, 1)
                    dve.wait_ge(m.used[5], i + 2)
                    v.tensor_copy(dn[:, 512:1024], ps[:, 7, :]).then_inc(m.dnd, 1)
                    assert lk.n == EXPERT_LINKS, lk.n
                ada_bias(*((5, 7), (11, 13))[l])
                g2 = 6 * l + 5
                dve.wait_ge(m.y, 1)
                for ch in range(DC):
                    v.scalar_tensor_tensor(out=X[:, ch, :], in0=ps[:, ch // 2, (ch % 2) * T:(ch % 2 + 1) * T],
                                           scalar=mcol(g2, ch), in1=X[:, ch, :], op0=ALU.mult,
                                           op1=ALU.add).then_inc(x_ready, 1)

            route_link = Link(dve, moe[0].link)
            route(0, route_link)
            experts(0, route_link)

            dve.memset(vlru[:, :, 0:LTAPS - 1], 0.0).then_inc(pad_ready, 1)
            norm_gain(2, PAR_A["n1"] + DC, 7)
            norm_out(2)
            for q in range(DC // 2):
                before = {}
                for k in range(LTAPS):
                    for n in (2 * q, 2 * q + 1):
                        acc = C[:, n, :]
                        if k == 0:
                            dve.wait_ge(ux_ready, n + 1)
                            ins = v.tensor_scalar(acc, vlru[:, n, 0:T], pcol(PAR_B["cw"] + n), pcol(PAR_B["cb"] + n),
                                                  ALU.mult, ALU.add)
                        else:
                            dve.wait_ge(dve_link, before[n])
                            ins = v.scalar_tensor_tensor(out=acc, in0=vlru[:, n, k:k + T], scalar=pcol(PAR_B["cw"] + k * DC + n),
                                                         in1=acc, op0=ALU.mult, op1=ALU.add)
                        if k < LTAPS - 1:
                            before[n] = link.post(ins)
                        else:
                            ins.then_inc(u_ready, 1)
            dve.wait_ge(y_ready, DC // 2)
            for h in range(HEADS):
                two = slice(2 * h, 2 * h + 2)
                t = H[:, two, :]
                dve.wait_ge(ta_ready, 4 * h + 4)
                link(v.tensor_tensor(sg[:, :, :], Dd[:, two, :], Dd[:, two, :], ALU.mult))
                v.scalar_tensor_tensor(out=t, in0=sg[:, :, :], scalar=1.0, in1=t, op0=ALU.add,
                                       op1=ALU.mult).then_inc(b2_ready, 1)
                dve.wait_ge(b2_ready, h + 1)
            for h in range(HEADS):
                two = slice(2 * h, 2 * h + 2)
                t = H[:, two, :]
                dve.wait_ge(b_ready, h + 1)
                dve.wait_ge(iu_ready, h + 1)
                link(v.tensor_tensor(t, t, vflat[:, two, :], ALU.mult))
                states = [link.post(v.tensor_tensor_scan(vflat[:, n, :], Dd[:, n, :], H[:, n, :], 0.0, ALU.mult, ALU.add))
                          for n in (2 * h, 2 * h + 1)]
                for n in (2 * h, 2 * h + 1):
                    dve.wait_ge(dve_link, states[n % 2])
                    v.tensor_tensor(B[:, n, :], B[:, n, :], vflat[:, n, :], ALU.mult).then_inc(hs_ready, 1)
            ada_bias(9, 10)
            norm_gain(3, PAR_A["n2"] + DC, 10)
            out_proj(1, 8)
            norm_out(3)
            route_link = Link(dve, moe[1].link)
            route(1, route_link)
            experts(1, route_link)
            norm_gain(4, PAR_A["fin"], 13)
            norm_out(4)
            dve.wait_ge(fin_mm, 1)
            v.tensor_copy(htok[:, 0, :], ps[:, 0:2, :].rearrange("p b n -> p (b n)")).then_inc(ht_dve, 1)

        @block.tensor
        def _(pe):
            mm = nc.tensor.matmul
            kw = dict(skip_group_check=True)
            pe.wait_ge(consts, 9)
            pe.wait_ge(s_x, 16)
            for ch in range(DC):
                for a in range(TT):
                    last = mm(ps[:, ch // 2, (ch % 2) * T + a * P:(ch % 2) * T + (a + 1) * P],
                              xin[:, a, ch * P:(ch + 1) * P], ident[:], start=True, stop=True, **kw)
                if ch % 2:
                    last.then_inc(x_mm, 1)

            def params(q, i):
                n = PAR_TILES[i]
                pe.wait_ge(s_par[i], 16 * PAR_DMAS[i])
                mm(ps[:, 4 + q % 4, 0:n], ptile[i][0:n, :], ident[0:n, 0:n],
                   start=True, stop=True).then_inc(par_mm, 1)

            params(0, 0)
            def ada_sum(part):
                if part == 0:
                    pe.wait_ge(cact, 1)
                else:
                    pe.wait_ge(cols_ready, part)
                for h in range(2):
                    if part in ADA_ALT:
                        pe.wait_ge(ada_alt_landed, 16 * (ADA_ALT.index(part) + 1))
                    else:
                        pe.wait_ge(ada_landed[h], 16 * (ADA_BUF.index(part) + 1))
                    for n in range(2):
                        for j in range(4):
                            w = ada_alt[part][:, 4 * h + j, :] if part in ADA_ALT else adabuf[:, h, j, :]
                            last = mm(ps[32 * j:32 * j + 32, 6 + n, :], cb32[:, 4 * h + j, :],
                                      w[:, n * 512:(n + 1) * 512], start=(h == 0), stop=(h == 1), **kw)
                    last.then_inc(ada_used, 1)

            def ada_cols(part):
                pe.wait_ge(rows_ready, part + 1)
                if part == 0:
                    pe.wait_ge(sel_ready, 1)
                for ch in range(DC):
                    last = mm(ps[:, 6, ch:ch + 1], rowsum[:, ch * P:(ch + 1) * P], sel[:, :], start=True, stop=True, **kw)
                last.then_inc(cols_mm, 1)

            def ada(part):
                ada_sum(part)
                ada_cols(part)

            def mean_square(k, ch):
                pe.wait_ge(sq_ready, k * DC + ch + 1)
                last = mm(ps[:, 4, 0:T], onesd[:], H[:, ch, :], start=(ch == 0), stop=(ch == DC - 1), **kw)
                if ch == DC - 1:
                    last.then_inc(ms_mm, 1)

            def norm(k):
                for ch in range(DC):
                    mean_square(k, ch)

            def proj(bank, off, w, col, src, ready=None, base=0):
                for k in range(DC):
                    if ready is not None:
                        pe.wait_ge(ready, base + k + 1)
                    last = mm(ps[:, bank, off:off + T], w[:, k, col:col + P], src[:, k, :],
                              start=(k == 0), stop=(k == DC - 1), **kw)
                return last

            def proj_all(w, src, ready, base, done, free=None, between=None, after=None):
                for k in range(DC // 2):
                    pe.wait_ge(ready, base + k + 1)
                    for n in range(DC):
                        if k == 0 and n % 2 == 0 and free is not None:
                            pe.wait_ge(free, n + 2)
                        mm(ps[:, n // 2, (n % 2) * T:(n % 2 + 1) * T], w[:, k, n * P:(n + 1) * P], src[:, k, :],
                           start=(k == 0 and n % 2 == 0), stop=False, **kw)
                if between is not None:
                    between()
                pe.wait_ge(ready, base + DC)
                for n in range(DC):
                    for k in range(DC // 2, DC):
                        last = mm(ps[:, n // 2, (n % 2) * T:(n % 2 + 1) * T], w[:, k, n * P:(n + 1) * P], src[:, k, :],
                                  start=False, stop=(k == DC - 1), **kw)
                    if n % 2:
                        last.then_inc(done, 1)
                        if after is not None and n > 1:
                            after(n - 3)
                            after(n - 2)
                if after is not None:
                    after(DC - 2)
                    after(DC - 1)

            pe.wait_ge(par_ready, 1)
            norm(0)
            for q, i in enumerate((2, 3, 4)):
                params(q + 1, i)
            pe.wait_ge(par_ready, 4)
            ada(0)
            ada(1)

            for m in range(DC):
                pe.wait_ge(s_w1[m // 2], 32)
                if m >= 4:
                    pe.wait_ge(v_ready, m - 3)
                proj(m % 4, 0, w1, m * P, H, h_ready if m == 0 else None)
                proj(m % 4, T, w1, D + m * P, H).then_inc(glu_mm, 1)
                if m in ADA_IN_W1:
                    ada(ADA_IN_W1[m])
            pe.wait_ge(root_ready, 1)
            params(4, 1)
            for n, ch in enumerate(PE_CHUNKS):
                pe.wait_ge(v_ready, ch + 1)
                if n:
                    pe.wait_ge(conv_pe, n)
                for k in range(TAPS):
                    pe.wait_ge(diag_ready, n * TAPS + k + 1)
                    last = mm(ps[:, 5, 0:T], diag[(n * TAPS + k) % NDIAG], vconf[:, ch, k:k + T],
                              start=(k == 0), stop=(k == TAPS - 1), **kw)
                    if k < TAPS - 1:
                        last.then_inc(diag_used, 1)
                last.then_inc(conv_mm, 1)
            pe.wait_ge(par_ready, 5)
            order = [*range(DVE_CHUNKS - 2), *PE_CHUNKS, DVE_CHUNKS - 2, DVE_CHUNKS - 1]
            for n, ch in enumerate(order):
                if ch < DVE_CHUNKS:
                    pe.wait_ge(conv_dve, ch + 1)
                else:
                    pe.wait_ge(conv_pe, ch + 1 - DVE_CHUNKS)
                last = mm(ps[:, 4, 0:T], onesd[:], B[:, ch, :], start=(n == 0), stop=(n == DC - 1), **kw)
            last.then_inc(mean_mm, 1)
            for ch in range(DC):
                pe.wait_ge(csq_ready, ch // 2 + 1)
                last = mm(ps[:, 5, T:2 * T], onesd[:], Dd[:, ch, :], start=(ch == 0), stop=(ch == DC - 1), **kw)
            last.then_inc(var_mm, 1)
            ada_sum(3)

            def parts_3_4():
                ada_cols(3)
                ada(4)

            pe.wait_ge(s_w2, 16)
            proj_all(w2, B, act_in, 0, o_mm, between=parts_3_4, after=lambda ch: mean_square(1, ch))

            def route(l):
                ada_sum((5, 11)[l])
                pe.wait_ge(s_router, 16 * 6)
                pe.wait_ge(x_ready, DC * (2 * l + 2))
                logits = [ps[:, 5, a * (NG + NE):(a + 1) * (NG + NE)] for a in range(TT)]
                for k in range(DC):
                    pe.wait_ge(h_ready, DC * (2 * l + 1) + k + 1)
                    for a in range(TT):
                        mm(logits[a], H[:, k, a * P:(a + 1) * P], wgr[:, l, k, :], start=(k == 0 and a == 0), stop=False, **kw)
                for a in range(TT):
                    last = mm(logits[a], ones[0:1, :], brow[0:1, l, :], start=False, stop=True, **kw)
                last.then_inc(lg_mm, 1)
                for a in range(TT):
                    for ch in range(DC):
                        last = mm(ps[:, 2 * a + ch // 4, (ch % 4) * P:(ch % 4 + 1) * P], H[:, ch, a * P:(a + 1) * P],
                                  ident[:], start=True, stop=True, **kw)
                last.then_inc(ht_mm, 1)
                ada_cols((5, 11)[l])
                ada_sum((6, 12)[l])
                pe.wait_ge(mask_ready, l + 1)
                mask = r32[:, 4, :, :]
                mm(ps[:, 5, P:P + NE], upper[:], mask[:, 0, :], start=True, stop=True, **kw)
                mm(ps[:, 5, P + NE:P + 2 * NE], ones[:], mask[:, 0, :], start=True, stop=False, **kw)
                mm(ps[:, 5, P + NE:P + 2 * NE], upper[:], mask[:, 1, :], start=False, stop=True, **kw)
                mm(ps[:, 5, P + 2 * NE:P + 3 * NE], ones[:], mask[:, 0, :], start=True, stop=False, **kw)
                mm(ps[:, 5, P + 2 * NE:P + 3 * NE], ones[:], mask[:, 1, :], start=False, stop=True, **kw).then_inc(rank_mm, 1)
                ada_cols((6, 12)[l])

            def experts(l, part):
                m = moe[l]
                for ph in range(6):
                    pe.sem_inc(m.used[ph], 1)
                pe.wait_ge(ht_act, TT * (l + 1))

                def gather(n):
                    pe.wait_ge(m.pick, n)
                    for k in range(DC):
                        for a in range(TT):
                            last = mm(ps[:, 6 + k // 4, (k % 4) * P:(k % 4 + 1) * P], htok[:, a, k:D:DC],
                                      pick[:, a, :], start=(a == 0), stop=(a == TT - 1), **kw)
                    last.then_inc(m.gath, 1)

                def scatter():
                    for ch in range(DC):
                        last = mm(ps[:, ch // 2, (ch % 2) * T:(ch % 2 + 1) * T], dn[:, ch * P:(ch + 1) * P],
                                  scat[:, :], start=False, stop=False, **kw)
                    return last

                pe.wait_ge(cols_ready, (7, 13)[l])
                gather(1)
                pe.wait_ge(m.sc, 1)
                for b in range(4):
                    mm(ps[:, b, :], scat[:, 0:P], htok[:, 0, 0:512], start=True, stop=False, **kw)
                pe.wait_ge(route_ready, l + 1)
                passes = pe.value_load(tab[0:1, 0:1], min_val=1, max_val=MAXP)

                def turn(i):
                    pe.wait_ge(m.xga, i + 1)
                    pe.wait_ge(m.xgd, i + 1)
                    pe.wait_ge(m.sc, i + 1)
                    for ph in range(4):
                        bank, h = 4 + ph // 2, ph % 2
                        for j in range(NSUB):
                            pe.wait_ge(m.landed[ph * NSUB + j], (i + 2) * 16)
                        for k in range(4):
                            for j in range(NSUB):
                                o = (ph * NSUB + j) * 2048 + k * F
                                last = mm(ps[SLOTS * j:SLOTS * (j + 1), bank, :],
                                          xg[:, 4 * h + k, SLOTS * j:SLOTS * (j + 1)], wbuf[:, o:o + F],
                                          start=(h == 0 and k == 0), stop=(h == 1 and k == 3), **kw)
                        last.then_inc(m.used[ph], 1)
                    if isinstance(i, int):
                        ada(part)
                        pe.wait_ge(cols_ready, part + 1)
                    pe.wait_ge(m.dna, i + 1)
                    pe.wait_ge(m.dnd, i + 1)
                    gather(i + 2)
                    if not isinstance(i, int):
                        scatter()
                    pe.wait_ge(m.hid, i + 2)
                    for k in range(FC):
                        last = mm(ps[:, 4, k * P:(k + 1) * P], hid[:, k:F:FC], ident[:], start=True, stop=True, **kw)
                    last.then_inc(m.ht_mm, 1)
                    pe.wait_ge(m.gate, i + 1)
                    for a in range(TT):
                        last = mm(ps[:, 5, a * P:(a + 1) * P], gate1[:, a, :], ident[:], start=True, stop=True, **kw)
                    last.then_inc(m.sc_mm, 1)
                    pe.wait_ge(m.ht, i + 1)
                    pe.wait_ge(m.xga, i + 2)
                    pe.wait_ge(m.xgd, i + 2)
                    for h in range(2):
                        for j in range(NSUB):
                            pe.wait_ge(m.landed[(4 + h) * NSUB + j], (i + 2) * 16)
                        for k in range(2):
                            for n in range(2):
                                for j in range(NSUB):
                                    o = ((4 + h) * NSUB + j) * 2048 + k * D + n * 512
                                    last = mm(ps[SLOTS * j:SLOTS * (j + 1), 6 + n, :],
                                              hidT[:, 2 * h + k, SLOTS * j:SLOTS * (j + 1)], wbuf[:, o:o + 512],
                                              start=(h == 0 and k == 0), stop=(h == 1 and k == 1), **kw)
                        last.then_inc(m.used[4 + h], 1)

                turn(0)
                with pe.Fori(1, passes) as i:
                    turn(i)
                pe.wait_ge(m.sc, passes + 1)
                pe.wait_ge(m.dna, passes + 1)
                pe.wait_ge(m.dnd, passes + 1)
                scatter().then_inc(m.y, 1)

            route(0)
            experts(0, 7)

            norm(2)
            ada_sum(8)
            pe.wait_ge(s_wy, 16)
            proj_all(rgw[0], H, h_ready, 2 * DC, q_mm, between=lambda: ada_cols(8))
            pe.wait_ge(s_wx, 16)
            proj_all(rgw[1], H, h_ready, 2 * DC, ux_mm, free=q_ready)
            pe.wait_ge(s_wab, 32)
            for h in range(HEADS):
                pe.wait_ge(u_ready, 2 * h + 2)
                if h < 2:
                    pe.wait_ge(ux_ready, 4 * h + 4)
                else:
                    pe.wait_ge(rg_ready, 4 * (h - 1))
                for w in range(2):
                    for j in range(2):
                        for k in range(2):
                            last = mm(ps[:, 2 * (h % 2) + w, j * T:(j + 1) * T], wab[:, w, h, k, j * P:(j + 1) * P],
                                      C[:, 2 * h + k, :], start=(k == 0), stop=(k == 1), **kw)
                last.then_inc(gate_mm, 1)
            ada(9)
            ada_sum(10)
            pe.wait_ge(s_wo, 16)
            pe.wait_ge(rg_ready, 4 * HEADS)
            proj_all(rgw[2], B, hs_ready, 0, o_mm, between=lambda: ada_cols(10), after=lambda ch: mean_square(3, ch))
            route(1)
            experts(1, 13)
            norm(4)
            pe.wait_ge(h_ready, 5 * DC)
            for a in range(TT):
                for ch in range(DC):
                    last = mm(ps[:, 2 * a + ch // 4, (ch % 4) * P:(ch % 4 + 1) * P], H[:, ch, a * P:(a + 1) * P],
                              ident[:], start=True, stop=True, **kw)
                last.then_inc(fin_mm, 1)


PAR_DMAS = (9, 8, 2, 1, 1)
EXPERT_LINKS = 9
DVE_CHUNKS = 6
PE_CHUNKS = (6, 7)
NDIAG = 32
GLU_AT = {(0, 8): 2, (0, 17): 3, (2, 5): 4, (2, 14): 5, (2, 23): 6, (4, 0): 7}
ADA_ALT = (1, 6, 10)
ADA_BUF = tuple(part for part in range(14) if part not in ADA_ALT)
ADA_IN_W1 = {3: 2}
DMA_SCRATCH = 1024


_INS = ["x", "c", "ada_w", "ada_b", "norm1_g", "norm2_g", "cm_w1", "cm_b1", "cm_dw", "cm_dwb", "cm_ln_g",
        "cm_ln_b", "cm_w2", "cm_b2", "rg_wy", "rg_by", "rg_wx", "rg_bx", "rg_cw", "rg_cb", "rg_wa", "rg_ba",
        "rg_wi", "rg_bi", "rg_lambda", "rg_wo", "rg_bo", "moe_wg", "moe_bg", "moe_wr", "moe_br", "moe_w_gate",
        "moe_w_up", "moe_w_down", "fin_ada_w", "fin_ada_b", "fin_g"]


def kernel(**inputs):
    import numpy as _np
    import concourse.bacc as _bacc
    from concourse import mybir as _mybir
    from concourse.bass_utils import run_bass_kernel_spmd as _run

    nc = _bacc.Bacc("TRN2", target_bir_lowering=False, num_devices=1, dynamic_dma_scratch_size=DMA_SCRATCH)
    arrays, args = {}, []
    for name in _INS:
        a = _np.ascontiguousarray(inputs[name])
        arrays[f"in_{name}"] = a
        args.append(nc.dram_tensor(f"in_{name}", a.shape, _mybir.dt.from_np(a.dtype), kind="ExternalInput").ap())
    args.append(nc.dram_tensor("out_0", (1, T, D), F32, kind="ExternalOutput").ap())
    trunk(nc, *args)
    r = _run(nc, [arrays], core_ids=[0])
    return r.results[0]["out_0"]
```

```python
from contextlib import ExitStack

import concourse.bass as bass
from concourse import mybir

F32 = mybir.dt.float32
I32 = mybir.dt.int32
ALU = mybir.AluOpType
ACT = mybir.ActivationFunctionType
AX = mybir.AxisListType

P = 128
T = 256
TT = T // P
D = 1024
DC = D // P
EPS = 1e-6
TAPS = 31
LTAPS = 4
HEADS = 4
NG, NE = 4, 32
EPG = NE // NG
F = 512
FC = F // P
SLOTS = 64
NSUB = P // SLOTS
MAXB = NE + (2 * T - NE) // SLOTS
MAXP = -(-MAXB // NSUB)
MINP = 2 * T // SLOTS // NSUB
TAB = 2
BIG = 1e30
GELU_A, GELU_B = 0.044715, 1.5957691216057308

PAR_A = {"n1": 0, "n2": 16, "fin": 32, "b1": 40, "dwb": 56, "lng": 64, "lnb": 72, "b2": 80, "c": 88}
PAR_B = {"by": 128, "bx": 136, "cb": 144, "ba": 152, "bi": 160, "lam": 168, "bo": 176, "cw": 184}
PAR_ADA = 256
PAR_DW = 384
DW_ROWS = TAPS * DC // 2
PAR_TILES = [96, 88, 112, DW_ROWS, DW_ROWS]


def dw_col(k, c):
    r = k * DC + c
    return PAR_DW + (r if r < DW_ROWS else P + r - DW_ROWS)


def conv_order():
    order, at, glus = [], {ch: 0 for ch in DVE_CHUNKS}, 0
    while glus < DC or any(k < TAPS for k in at.values()):
        left = [ch for ch in DVE_CHUNKS if ch < glus and at[ch] < TAPS][:2]
        if glus < DC and (not left or len(order) >= GLU_EVERY * glus - GLU_AHEAD):
            order.append(("GLU", glus))
            glus += 1
            continue
        for ch in left:
            order.append((ch, at[ch]))
            at[ch] += 1
    return order


class Link:

    def __init__(self, eng, sem, base=0):
        self.eng, self.sem, self.base, self.n = eng, sem, base, 0

    def post(self, ins):
        self.n += 1
        ins.then_inc(self.sem, 1)
        return self.base + self.n

    def __call__(self, ins):
        self.eng.wait_ge(self.sem, self.post(ins))


def trunk(nc, x, c, ada_w, ada_b, norm1_g, norm2_g, cm_w1, cm_b1, cm_dw, cm_dwb, cm_ln_g, cm_ln_b,
          cm_w2, cm_b2, rg_wy, rg_by, rg_wx, rg_bx, rg_cw, rg_cb, rg_wa, rg_ba, rg_wi, rg_bi,
          rg_lambda, rg_wo, rg_bo, moe_wg, moe_bg, moe_wr, moe_br, moe_w_gate, moe_w_up,
          moe_w_down, fin_ada_w, fin_ada_b, fin_g, out):
    ctx = ExitStack()
    with ctx:
        def sb(name, shape, dt=F32):
            return ctx.enter_context(nc.sbuf_tensor(name, shape, dt))

        def sem(name):
            return ctx.enter_context(nc.semaphore(name))

        ps = ctx.enter_context(nc.psum_tensor("ps", [P, 8, 512], F32))

        wbuf = sb("wbuf", [P, 24 * 1024])
        adabuf = sb("adabuf", [P, 2, 4, D])
        wab = sb("wab", [P, 2, HEADS, 2, 256])
        spare = sb("spare", [P, 2048])
        X = sb("X", [P, DC, T])
        H = sb("H", [P, DC, T])
        B = sb("B", [P, DC, T])
        C = sb("C", [P, DC, T])
        Dd = sb("Dd", [P, DC, T])
        V = sb("V", [P, DC * (T + TAPS - 1)])
        sg = sb("sg", [P, 2, T])
        rowsum = sb("rowsum", [P, D])
        modraw = sb("modraw", [P, 14 * DC])
        par = sb("par", [P, 5 * P])
        mod = sb("mod", [P, 14 * DC])
        wgr = sb("wgr", [P, 2, DC, NG + NE])
        brow = sb("brow", [1, 2, NG + NE])
        cb32 = sb("cb32", [P, DC, 32])
        rs = sb("rs", [P, T])
        gs = sb("gs", [P, DC])
        gb = sb("gb", [P, DC])
        small = sb("small", [P, 8, DC])
        ident = sb("ident", [P, P])
        onesd = sb("onesd", [P, P])
        ones = sb("ones", [P, P])
        eps = sb("eps", [P, 1])
        upper = sb("upper", [P, P])
        sel = sb("sel", [P, 1])
        iota0 = sb("iota0", [P, P])
        iota1 = sb("iota1", [P, P])
        rev = sb("rev", [P, NE])
        blk = sb("blk", [P, 2 * MAXP])
        thr = sb("thr", [P, T // SLOTS])
        lg = sb("lg", [P, TT, NG + NE])
        r4 = sb("r4", [P, 3, TT, NG])
        r1 = sb("r1", [P, 16, TT])
        cnt = sb("cnt", [P, 4, NE])
        cmp3 = V[:, 0:2 * MAXP * NE].rearrange("p (b e) -> p b e", e=NE)
        dflat = Dd[:, :, :].rearrange("p c t -> p (c t)")
        r32 = dflat[:, 0:6 * TT * NE].rearrange("p (i a e) -> p i a e", i=6, a=TT)
        dfree = 6 * TT * NE
        tabf = sb("tabf", [P, 4 * MAXP + 2 * NSUB])
        tab = sb("tab", [1, TAB + 4 * MAXP + 2 * NSUB], I32)
        gslot = sb("gslot", [P, 2, TT])
        gw = sb("gw", [P, 2, TT])
        pick, gate1, gate2 = (dflat[:, dfree + i * TT * P:dfree + (i + 1) * TT * P].rearrange("p (a s) -> p a s", a=TT)
                              for i in range(3))
        scat = sg[:, 0, :]

        w1 = wbuf[:, 0:16384].rearrange("p (k n) -> p k n", k=DC)
        w2 = wbuf[:, 16384:24576].rearrange("p (k n) -> p k n", k=DC)
        rgw = [wbuf[:, i * 8192:(i + 1) * 8192].rearrange("p (k n) -> p k n", k=DC) for i in range(3)]
        vconf = V[:, :].rearrange("p (c t) -> p c t", c=DC)
        vlru = V[:, 0:DC * (T + LTAPS - 1)].rearrange("p (c t) -> p c t", c=DC)
        vflat = V[:, 0:DC * T].rearrange("p (c t) -> p c t", c=DC)
        htok = B[:, :, :].rearrange("p (a c) t -> p a (c t)", a=TT)
        xg = C[:, 0:4, :].rearrange("p c t -> p (c t)").rearrange("p (k s) -> p k s", k=DC)
        hid = V[:, 0:F]
        hidT = V[:, F:2 * F].rearrange("p (c s) -> p c s", c=FC)
        dn = V[:, 2 * F:2 * F + D]
        sigb = C[:, 4:6, :].rearrange("p c t -> p (c t)")
        xin = B[:, :, :].rearrange("p (a c) t -> p a (c t)", a=TT)
        ada_alt = {part: wbuf[:, o:o + DC * D].rearrange("p (k n) -> p k n", k=DC)
                   for part, o in ((1, 16384), (3, 0), (11, 0))}
        ptile = [wab[:, 0, 0, 0, 0:P] if i == 1 else C[:, i, 0:P] for i in range(5)]

        diag = [t[:, i // 2, (i % 2) * P:(i % 2 + 1) * P] for t in (C, Dd) for i in range(2 * DC)]
        prod = [spare[:, i * T:(i + 1) * T] for i in range(DC)]

        wflat = wab[:, :, :, :, :].rearrange("p a h i j -> p (a h i j)")
        second = [wflat[:, 0:2048], wflat[:, 2048:4096], spare[:, :], H[:, :, :].rearrange("p c t -> p (c t)")]
        second += [adabuf[:, h, 2 * j:2 * j + 2, :].rearrange("p k n -> p (k n)") for h in range(2) for j in range(NSUB)]
        up_aside = [16 * len(ADA_BUF) + 32 * i for i in range(1, 3)]

        gain_diag, shift_diag = (spare[:, i * D:(i + 1) * D].rearrange("p (c n) -> p c n", c=DC) for i in range(2))
        shift_rows = rowsum

        s_x = sem("s_x")
        s_par = [sem(f"s_par{i}") for i in range(5)]
        s_router = sem("s_router")
        side_landed = [sem(f"side_landed{q}") for q in range(DC // 2)]
        s_w2 = sem("s_w2")
        s_wx, s_wy, s_wo, s_wab = sem("s_wx"), sem("s_wy"), sem("s_wo"), sem("s_wab")
        ada_landed = [sem("ada_landed0"), sem("ada_landed1")]
        ada_alt_landed = sem("ada_alt_landed")
        ada_used = sem("ada_used")
        consts = sem("consts")
        pool_link = sem("pool_link")
        dve_link = sem("dve_link")
        sel_ready = sem("sel_ready")
        par_mm, par_ready = sem("par_mm"), sem("par_ready")
        x_mm, x_ready = sem("x_mm"), sem("x_ready")
        csig, cact = sem("csig"), sem("cact")
        rows_ready, cols_mm, cols_ready, mod_ready = sem("rows_ready"), sem("cols_mm"), sem("cols_ready"), sem("mod_ready")
        sq_ready, ms_mm, xn_ready, h_ready = sem("sq_ready"), sem("ms_mm"), sem("xn_ready"), sem("h_ready")
        gs_ready = sem("gs_ready")
        root_ready, ln_root = sem("root_ready"), sem("ln_root")
        b2_ready, b_ready = sem("b2_ready"), sem("b_ready")
        glu_mm, sg_ready, v_ready = sem("glu_mm"), sem("sg_ready"), sem("v_ready")
        pad_ready = sem("pad_ready")
        conv_dve, conv_mm, conv_pe = sem("conv_dve"), sem("conv_mm"), sem("conv_pe")
        diag_ready, prod_ready, conv_pool = sem("diag_ready"), sem("prod_ready"), sem("conv_pool")
        mean_mm, cen_ready, csq_ready, var_mm, z_ready = sem("mean_mm"), sem("cen_ready"), sem("csq_ready"), sem("var_mm"), sem("z_ready")
        zs_ready, act_in = sem("zs_ready"), sem("act_in")
        o_mm = sem("o_mm")
        xb_ready = sem("xb_ready")
        ux_mm, ux_ready, u_ready = sem("ux_mm"), sem("ux_ready"), sem("u_ready")
        q_mm, q_ready, g_in, g_sig, y_ready = sem("q_mm"), sem("q_ready"), sem("g_in"), sem("g_sig"), sem("y_ready")
        gate_mm, rg_ready, ta_ready, nk_in, nk_exp, nk_ln, nk_ready = (sem(n) for n in (
            "gate_mm", "rg_ready", "ta_ready", "nk_in", "nk_exp", "nk_ln", "nk_ready"))
        iu_ready, hs_ready = sem("iu_ready"), sem("hs_ready")
        lg_mm, ge_in, ge_ready, mask_ready, rank_mm, route_ready = (sem(n) for n in (
            "lg_mm", "ge_in", "ge_ready", "mask_ready", "rank_mm", "route_ready"))
        ht_mm, ht_act, out_ready = sem("ht_mm"), sem("ht_act"), sem("out_ready")
        fin_mm, s_out = sem("fin_mm"), sem("s_out")

        class Moe:
            def __init__(self, l):
                def s(n):
                    return sem(f"moe{l}_{n}")
                self.landed = [s(f"landed{i}") for i in range(6 * NSUB)]
                self.used = [s(f"used{i}") for i in range(6)]
                self.pick, self.gate, self.link = s("pick"), s("gate"), s("link")
                self.gath, self.xga, self.xgd = s("gather"), s("xg_act"), s("xg_dve")
                self.sig, self.hid = s("sig"), s("hid")
                self.ht_mm, self.ht = s("hidT_mm"), s("hidT")
                self.sc_mm, self.sc = s("scat_mm"), s("scat")
                self.dna, self.dnd = s("dn_act"), s("dn_dve")
                self.y = s("y")

        moe = [Moe(0), Moe(1)]

        def pcol(off, n=1):
            return par[:, off:off + n]

        def v8(t):
            return t.rearrange("l (c p) -> (l c) p", p=P)

        def ada_acc(part):
            if part == 7:
                return rowsum[:, :]
            if part in (9, 10, 11):
                return spare[:, (part % 2) * D:(part % 2 + 1) * D]
            return V[:, (part % 2) * D:(part % 2 + 1) * D]

        def mcol(part, ch):
            return mod[:, part * DC + ch:part * DC + ch + 1]

        def ada_src(part):
            if part < 12:
                return ada_w[part // 6, :, (part % 6) * D:(part % 6 + 1) * D]
            return fin_ada_w[:, (part - 12) * D:(part - 11) * D]

        block = ctx.enter_context(nc.Block())

        @block.sync
        def _(sp):
            def ada_load(part):
                src = ada_src(part).rearrange("(k p) n -> p k n", p=P)
                if part in ADA_ALT:
                    sp.dma_start(ada_alt[part], src).then_inc(ada_alt_landed, 16)
                    return
                n = ADA_BUF.index(part)
                for h in range(2):
                    if (part, h) == (0, 1):
                        sp.wait_ge(s_par[0], 16 * PAR_DMAS[0])
                    if part:
                        sp.wait_ge(ada_used, 2 * ADA_BUF[n - 1] + h + 1)
                    sp.dma_start(adabuf[:, h, :, :], src[:, 4 * h:4 * h + 4, :]).then_inc(ada_landed[h], 16)

            def rows(w):
                return w.rearrange("(k p) n -> p k n", p=P)

            def experts_src(l):
                return [w[l].rearrange("e (p k) f -> (e p) (k f)", p=P) for w in (moe_w_gate, moe_w_up, moe_w_down)]

            def guess(l, matrix):
                for h in range(2):
                    for j in range(NSUB):
                        slot = (2 * matrix + h) * NSUB + j
                        sp.dma_start(wbuf[:, slot * 2048:(slot + 1) * 2048],
                                     experts_src(l)[matrix][j * P:(j + 1) * P, h * 2048:(h + 1) * 2048]
                                     ).then_inc(moe[l].landed[slot], 16)

            def vec(tile, row, src, n):
                sp.dma_start(ptile[tile][row:row + n, :], src).then_inc(s_par[tile], 16)

            def guess_second(l, slots):
                for slot in slots:
                    ph, j = slot // NSUB, slot % NSUB
                    sp.dma_start(second[slot], experts_src(l)[ph // 2][(NSUB + j) * P:(NSUB + j + 1) * P,
                                                                      (ph % 2) * 2048:(ph % 2 + 1) * 2048]
                                 ).then_inc(side_landed[slot] if ph < 2 else ada_landed[ph - 2], 16)

            sp.dma_start(xin, x[0].rearrange("(a p) d -> p a d", p=P)).then_inc(s_x, 16)
            ada_load(0)
            ada_load(1)
            for q in range(DC // 2):
                for half in range(2):
                    cols = slice(half * D + 2 * q * P, half * D + 2 * (q + 1) * P)
                    sp.dma_start(w1[:, :, cols], rows(cm_w1[0])[:, :, cols]).then_inc(side_landed[q], 16)
            for n, t in (("by", rg_by), ("bx", rg_bx), ("cb", rg_cb), ("lam", rg_lambda), ("bo", rg_bo)):
                vec(1, PAR_B[n] - P, v8(t), 8)
            vec(1, PAR_B["ba"] - P, rg_ba[0].rearrange("h (c p) -> (h c) p", p=P), 8)
            vec(1, PAR_B["bi"] - P, rg_bi[0].rearrange("h (c p) -> (h c) p", p=P), 8)
            vec(1, PAR_B["cw"] - P, rg_cw[0].rearrange("k (c p) -> (k c) p", p=P), 32)
            for l in range(2):
                sp.dma_start(wgr[:, l, :, 0:NG], moe_wg[l].rearrange("(k p) g -> p k g", p=P)).then_inc(s_router, 16)
                sp.dma_start(wgr[:, l, :, NG:], moe_wr[l].rearrange("(k p) g -> p k g", p=P)).then_inc(s_router, 16)
            sp.dma_start(brow[0:1, :, 0:NG], moe_bg.rearrange("(a l) g -> a l g", a=1)).then_inc(s_router, 16)
            sp.dma_start(brow[0:1, :, NG:], moe_br.rearrange("(a l) g -> a l g", a=1)).then_inc(s_router, 16)
            ada_load(2)
            sp.wait_ge(ada_used, 4)
            sp.dma_start(w2, rows(cm_w2[0])).then_inc(s_w2, 16)
            sp.wait_ge(glu_mm, DC)
            ada_load(3)
            ada_load(4)
            guess(0, 1)
            sp.wait_ge(par_mm, 5)
            guess_second(0, (0, 1))
            sp.wait_ge(conv_pool, (TAPS - 1) * len(POOL_CHUNKS))
            guess_second(0, (2,))
            sp.wait_ge(ada_used, 2 * 3 + 2)
            guess(0, 0)
            ada_load(5)
            sp.wait_ge(o_mm, DC // 2)
            ada_load(6)
            guess(0, 2)
            sp.wait_ge(ht_mm, 1)
            guess_second(0, (3,))
            ada_load(7)

            def experts(l):
                m = moe[l]
                sp.wait_ge(route_ready, l + 1)
                passes = sp.value_load(tab[0:1, 0:1], min_val=MINP, max_val=MAXP)

                def entries(start, most):
                    return [sp.value_load(tab[0:1, bass.ds(start + j + TAB, 1)], min_val=0, max_val=most)
                            for j in range(NSUB)]

                def load(ph, j, dst, ids, flags, landed):
                    src = experts_src(l)[ph // 2]
                    sp.dma_start(dst, src[bass.ds(ids[j] * P, P), (ph % 2) * 2048:(ph % 2 + 1) * 2048],
                                 cond=(flags[j] > 0)).then_inc(landed, 16)

                def half(ph, ids, flags, landed, used):
                    for j in range(NSUB):
                        slot = ph * NSUB + j
                        sp.wait_ge(m.landed[slot], landed)
                        sp.wait_ge(m.used[ph], used)
                        load(ph, j, wbuf[:, slot * 2048:(slot + 1) * 2048], ids, flags, m.landed[slot])

                ids, flags = entries(0, NE - 1), entries(4 * MAXP, 1)
                for ph in range(6):
                    half(ph, ids, flags, 16, 1)
                ids, flags = entries(NSUB, NE - 1), entries(4 * MAXP + NSUB, 1)
                for slot in range(2 * NSUB):
                    sp.wait_ge(side_landed[slot], 16 * (2 * l + 3))
                    load(slot // NSUB, slot % NSUB, second[slot], ids, flags, side_landed[slot])
                for ph in range(2, ASIDE[l]):
                    sp.wait_ge(ada_landed[ph - 2], up_aside[0])
                    for j in range(NSUB):
                        load(ph, j, second[ph * NSUB + j], ids, flags, ada_landed[ph - 2])
                ids3, there3 = entries(2 * NSUB, NE - 1), entries(2 * MAXP + 2 * NSUB, 1)
                for ph in range(ASIDE[l]):
                    half(ph, ids3, there3, 2 * 16, 2)
                there = entries(2 * MAXP + NSUB, 1)
                for ph in range(ASIDE[l], 6):
                    half(ph, ids, there, 2 * 16, 2)
                for ph in range(ASIDE[l], 6):
                    half(ph, ids3, there3, 3 * 16, 3)
                with sp.Fori(4, passes + 1) as turn:
                    ids = entries((turn - 1) * NSUB, NE - 1)
                    there = entries((turn - 1) * NSUB + 2 * MAXP, 1)
                    for ph in range(6):
                        half(ph, ids, there, (turn - 1) * 16 if ph < ASIDE[l] else turn * 16, turn)
                return sp.snap(passes + 1)

            all_used = experts(0)
            ada_load(8)
            for i, (w, s) in enumerate(((rg_wy, s_wy), (rg_wx, s_wx), (rg_wo, s_wo))):
                if i == 2:
                    ada_load(9)
                sp.wait_ge(moe[0].used[2 * i], all_used)
                sp.wait_ge(moe[0].used[2 * i + 1], all_used)
                sp.dma_start(rgw[i], rows(w[0])).then_inc(s, 16)
                if i == 1:
                    for n, g in enumerate((rg_wa, rg_wi)):
                        sp.dma_start(wab[:, n, :, :, :], g[0].rearrange("h (i p) j -> p h i j", p=P)).then_inc(s_wab, 16)
            ada_load(10)
            sp.wait_ge(q_mm, DC // 2)
            ada_load(11)
            ada_load(12)
            sp.wait_ge(ux_mm, DC // 2)
            guess(1, 1)
            sp.wait_ge(ada_used, 2 * 11 + 2)
            guess(1, 0)
            sp.wait_ge(gate_mm, HEADS)
            guess_second(1, (0, 1))
            sp.wait_ge(cols_mm, 12)
            guess_second(1, (2,))
            ada_load(13)
            sp.wait_ge(o_mm, DC)
            guess(1, 2)
            sp.wait_ge(ht_mm, 2)
            guess_second(1, (3,))
            sp.wait_ge(ada_used, 2 * 13 + 2)
            guess_second(1, (4, 5, 6, 7))
            experts(1)
            for a in range(TT):
                for n in range(2):
                    sp.wait_ge(out_ready, 2 * a + n + 1)
                    sp.dma_start(out[0, a * P:(a + 1) * P, n * 512:(n + 1) * 512],
                                 htok[:, a, n * 512:(n + 1) * 512]).then_inc(s_out, 16)
            sp.wait_ge(s_out, 16 * TT * 2)

        @block.gpsimd
        def _(pool):
            link = Link(pool, pool_link)
            g = nc.gpsimd
            link(g.memset(ident[:], 0.0))
            link(g.memset(ones[:], 1.0))
            g.affine_select(out=ident[:], in_=ident[:], compare_op=ALU.not_equal, fill=1.0, base=0,
                            pattern=[[-1, P]], channel_multiplier=1).then_inc(consts, 1)
            g.affine_select(out=upper[:], in_=ones[:], compare_op=ALU.is_gt, fill=0.0, base=0,
                            pattern=[[1, P]], channel_multiplier=-1).then_inc(consts, 1)
            g.memset(onesd[:], 1.0 / D).then_inc(consts, 1)
            kw = dict(allow_small_or_imprecise_dtypes=True)
            g.iota(iota0[:], [[1, P]], base=0, channel_multiplier=0, **kw).then_inc(consts, 1)
            g.iota(iota1[:], [[1, P]], base=P, channel_multiplier=0, **kw).then_inc(consts, 1)
            g.iota(rev[:], [[-1, NE]], base=NE, channel_multiplier=0, **kw).then_inc(consts, 1)
            g.iota(blk[:], [[1, 2 * MAXP]], base=0, channel_multiplier=0, **kw).then_inc(consts, 1)
            g.iota(thr[:], [[SLOTS, T // SLOTS]], base=0, channel_multiplier=0, **kw).then_inc(consts, 1)
            g.memset(eps[:], EPS).then_inc(consts, 1)
            g.memset(vconf[:, :, 0:TAPS - 1], 0.0).then_inc(pad_ready, 1)

            pool.wait_ge(par_ready, 4)
            for k in range(TAPS):
                g.tensor_scalar(diag[k], ident[:], pcol(dw_col(k, PE_CHUNK)), None, ALU.mult).then_inc(diag_ready, 1)
            for n, ch in enumerate(POOL_CHUNKS):
                for k in range(1, TAPS):
                    add = n * (TAPS - 1) + k - 1
                    pool.wait_ge(prod_ready, add + n + 2)
                    pool.wait_ge(conv_pool, add)
                    g.tensor_tensor(B[:, ch, :], B[:, ch, :], prod[add % DC], ALU.add).then_inc(conv_pool, 1)

            def x_bias(l, part, bias):
                gate = mod[:, part * DC:(part + 1) * DC]
                pool.wait_ge(cols_ready, part + 1)
                link(g.tensor_tensor(gate, modraw[:, part * DC:(part + 1) * DC],
                                     par[:, PAR_ADA + part * DC:PAR_ADA + (part + 1) * DC], ALU.add))
                link(g.tensor_tensor(gb[:, :], gate, pcol(bias, DC), ALU.mult))
                pool.wait_ge(xn_ready, (2 * l + 1) * DC // 2)
                for n in range(DC):
                    g.tensor_scalar(X[:, n, :], X[:, n, :], gb[:, n:n + 1], None, ALU.add).then_inc(xb_ready, 1)

            x_bias(0, 2, PAR_A["b2"])

            for q in range(DC // 2):
                y = B[:, 2 * q:2 * q + 2, :]
                pool.wait_ge(q_ready, 2 * q + 2)
                link(g.tensor_tensor(sg[:, :, :], y, y, ALU.mult))
                link(g.tensor_scalar(sg[:, :, :], sg[:, :, :], GELU_A, 1.0, ALU.mult, ALU.add))
                g.tensor_tensor(sg[:, :, :], sg[:, :, :], y, ALU.mult).then_inc(g_in, 1)
                pool.wait_ge(g_sig, q + 1)
                g.tensor_tensor(y, y, sg[:, :, :], ALU.mult).then_inc(y_ready, 1)
                pool.wait_ge(y_ready, q + 1)
            pool.wait_ge(par_ready, 5)
            x_bias(1, 8, PAR_B["bo"])
            for h in range(HEADS):
                two = slice(2 * h, 2 * h + 2)
                pool.wait_ge(rg_ready, 4 * (h + 1))
                g.tensor_tensor(vflat[:, two, :], vflat[:, two, :], C[:, two, :], ALU.mult).then_inc(iu_ready, 1)

            pool.wait_ge(gs_ready, 5)
            pool.wait_ge(moe[1].used[1], 3)
            for ch in range(DC):
                g.tensor_scalar(gain_diag[:, ch, :], ident[:], gs[:, ch:ch + 1], None, ALU.mult).then_inc(diag_ready, 1)
                g.tensor_scalar(shift_diag[:, ch, :], ident[:], mcol(12, ch), None, ALU.mult).then_inc(diag_ready, 1)

        @block.scalar
        def _(act):
            a = nc.scalar

            def vec(tile, row, src, n):
                act.dma_start(ptile[tile][row:row + n, :], src).then_inc(s_par[tile], 16)

            vec(0, PAR_A["c"], v8(c), 8)
            vec(0, PAR_A["n1"], v8(norm1_g), 16)
            vec(0, PAR_A["n2"], v8(norm2_g), 16)
            vec(0, PAR_A["fin"], fin_g.rearrange("(c p) -> c p", p=P), 8)
            vec(0, PAR_A["b1"], v8(cm_b1), 16)
            for n, t in (("dwb", cm_dwb), ("lng", cm_ln_g), ("lnb", cm_ln_b), ("b2", cm_b2)):
                vec(0, PAR_A[n], v8(t), 8)
            vec(2, 0, ada_b.rearrange("l (c p) -> (l c) p", p=P), 96)
            vec(2, 96, fin_ada_b.rearrange("(c p) -> c p", p=P), 16)
            dwr = cm_dw[0].rearrange("k (c p) -> (k c) p", p=P)
            vec(3, 0, dwr[0:DW_ROWS, :], DW_ROWS)
            vec(4, 0, dwr[DW_ROWS:2 * DW_ROWS, :], DW_ROWS)

            def ada_rows(part):
                act.wait_ge(ada_used, 2 * part + 2)
                a.activation(rowsum[:, :], ps[:, 6:8, :].rearrange("p b n -> p (b n)"), ACT.Copy).then_inc(rows_ready, 1)

            def ada_back(part):
                act.wait_ge(cols_mm, part + 1)
                a.activation(modraw[:, part * DC:(part + 1) * DC], ps[:, 6, 0:DC], ACT.Copy).then_inc(cols_ready, 1)

            def ada(part):
                ada_rows(part)
                ada_back(part)

            def norm_squares(k):
                for ch in range(DC):
                    act.wait_ge(x_ready, k * DC + ch + 1)
                    a.activation(H[:, ch, :], X[:, ch, :], ACT.Square).then_inc(sq_ready, 1)

            def norm_root(k):
                act.wait_ge(ms_mm, k + 1)
                a.activation(rs[:, :], ps[:, 4, 0:T], ACT.Sqrt, bias=eps[:, 0:1]).then_inc(root_ready, 1)

            def norm_stats(k):
                norm_squares(k)
                norm_root(k)

            def norm_out(k, sh_part):
                act.wait_ge(gs_ready, k + 1)
                for ch in range(DC):
                    act.wait_ge(xn_ready, (k * DC + ch) // 2 + 1)
                    a.activation(H[:, ch, :], H[:, ch, :], ACT.Identity, bias=mcol(sh_part, ch),
                                 scale=gs[:, ch:ch + 1]).then_inc(h_ready, 1)

            norm_squares(0)
            act.wait_ge(par_ready, 1)
            a.activation(small[:, 0, :], pcol(PAR_A["c"], DC), ACT.Sigmoid).then_inc(csig, 1)
            act.wait_ge(consts, 9)
            norm_root(0)
            ada(0)
            ada(1)
            norm_out(0, 0)

            todo = [(n, k) for n in range(len(POOL_CHUNKS)) for k in range(TAPS)]
            for m in range(DC):
                act.wait_ge(glu_mm, m + 1)
                if m >= 2:
                    act.wait_ge(v_ready, m - 1)
                a.activation(sg[:, m % 2, :], ps[:, m % 4, T:2 * T], ACT.Sigmoid,
                             bias=pcol(PAR_A["b1"] + DC + m)).then_inc(sg_ready, 1)
                if m == DC - 1:
                    ada_rows(2)
                for n, k in todo[PRODUCTS * (m - 2):PRODUCTS * (m - 1) if m < DC - 1 else None] if m >= 2 else ():
                    ch = POOL_CHUNKS[n]
                    act.wait_ge(v_ready, ch + 1)
                    w = pcol(dw_col(k, ch))
                    if k == 0:
                        a.activation(B[:, ch, :], vconf[:, ch, 0:T], ACT.Identity, bias=pcol(PAR_A["dwb"] + ch),
                                     scale=w).then_inc(prod_ready, 1)
                    else:
                        add = n * (TAPS - 1) + k - 1
                        if add >= DC:
                            act.wait_ge(conv_pool, add - DC + 1)
                        a.activation(prod[add % DC], vconf[:, ch, k:k + T], ACT.Copy, scale=w).then_inc(prod_ready, 1)
            ada_back(2)
            act.wait_ge(conv_mm, 1)
            a.activation(B[:, PE_CHUNK, :], ps[:, 5, 0:T], ACT.Identity, bias=pcol(PAR_A["dwb"] + PE_CHUNK)).then_inc(conv_pe, 1)
            for q in range(DC // 2):
                act.wait_ge(cen_ready, q + 1)
                a.activation(Dd[:, 2 * q:2 * q + 2, :], C[:, 2 * q:2 * q + 2, :], ACT.Square).then_inc(csq_ready, 1)
            act.wait_ge(var_mm, 1)
            a.activation(rs[:, :], ps[:, 5, T:2 * T], ACT.Sqrt, bias=eps[:, 0:1]).then_inc(ln_root, 1)
            for ch in range(DC):
                act.wait_ge(z_ready, ch // 2 + 1)
                a.activation(Dd[:, ch, :], C[:, ch, :], ACT.Sigmoid, bias=pcol(PAR_A["lnb"] + ch),
                             scale=pcol(PAR_A["lng"] + ch)).then_inc(zs_ready, 1)
            ada(3)
            act.wait_ge(nk_in, 1)
            a.activation(small[:, 3, :], small[:, 2, :], ACT.Exp, scale=-1.0).then_inc(nk_exp, 1)
            act.wait_ge(nk_exp, 2)
            a.activation(small[:, 5, :], small[:, 4, :], ACT.Ln).then_inc(nk_ln, 1)
            norm_squares(1)
            ada_back(4)
            norm_root(1)
            norm_out(1, 3)

            def route(l):
                act.wait_ge(ge_in, 2 * l + 1)
                a.activation(r4[:, 1, :, :], r4[:, 0, :, :], ACT.Exp).then_inc(ge_ready, 1)
                act.wait_ge(ge_in, 2 * l + 2)
                a.activation(r1[:, 7, :], r1[:, 5, :], ACT.Exp).then_inc(ge_ready, 1)

            def tokens(l):
                for t in range(TT):
                    act.wait_ge(ht_mm, l + 1)
                    a.activation(htok[:, t, :], ps[:, 2 * t:2 * t + 2, :].rearrange("p b n -> p (b n)"),
                                 ACT.Copy).then_inc(ht_act, 1)

            def experts(l, part):
                m = moe[l]
                act.wait_ge(m.gath, 1)
                a.activation(xg[:, 0:4, :], ps[:, 6, :].rearrange("p (k s) -> p k s", k=4), ACT.Copy).then_inc(m.xga, 1)
                act.sem_inc(m.dna, 1)
                act.wait_ge(route_ready, l + 1)
                passes = act.value_load(tab[0:1, 0:1], min_val=MINP, max_val=MAXP)

                def turn(i):
                    act.wait_ge(m.used[1], i + 2)
                    act.wait_ge(m.hid, i + 1)
                    a.activation(sigb, ps[:, 4, :], ACT.Sigmoid).then_inc(m.sig, 1)
                    if isinstance(i, int) and part is not None:
                        ada_back(part)
                    act.wait_ge(m.gath, i + 2)
                    a.activation(xg[:, 0:4, :], ps[:, 6, :].rearrange("p (k s) -> p k s", k=4), ACT.Copy).then_inc(m.xga, 1)
                    act.wait_ge(m.ht_mm, i + 1)
                    a.activation(hidT, ps[:, 4, :].rearrange("p (c s) -> p c s", c=FC), ACT.Copy).then_inc(m.ht, 1)
                    act.wait_ge(m.used[5], i + 2)
                    a.activation(dn[:, 0:512], ps[:, 6, :], ACT.Copy).then_inc(m.dna, 1)

                turn(0)
                with act.Fori(1, passes) as i:
                    turn(i)

            ada_rows(5)
            tokens(0)
            ada_back(5)
            ada(6)
            route(0)
            experts(0, 7)

            norm_stats(2)
            norm_out(2, 6)
            ada(8)
            for n in range(DC):
                act.wait_ge(q_mm, n // 2 + 1)
                a.activation(B[:, n, :], ps[:, n // 2, (n % 2) * T:(n % 2 + 1) * T], ACT.Identity,
                             bias=pcol(PAR_B["by"] + n)).then_inc(q_ready, 1)
            for q in range(DC // 2):
                act.wait_ge(g_in, q + 1)
                a.activation(sg[:, :, :], sg[:, :, :], ACT.Sigmoid, scale=GELU_B).then_inc(g_sig, 1)
                if q == 2:
                    ada_back(9)
            act.wait_ge(pad_ready, 2)
            for n in range(DC):
                act.wait_ge(ux_mm, n // 2 + 1)
                a.activation(vlru[:, n, LTAPS - 1:], ps[:, n // 2, (n % 2) * T:(n % 2 + 1) * T], ACT.Identity,
                             bias=pcol(PAR_B["bx"] + n)).then_inc(ux_ready, 1)
            ada_back(10)

            def decay(h):
                act.wait_ge(nk_ready, 1)
                act.wait_ge(rg_ready, 4 * h + 4)
                for n in (2 * h, 2 * h + 1):
                    a.activation(H[:, n, :], Dd[:, n, :], ACT.Tanh, scale=small[:, 2, n:n + 1]).then_inc(ta_ready, 1)
                    act.wait_ge(ta_ready, 2 * n + 1)
                    a.activation(Dd[:, n, :], Dd[:, n, :], ACT.Exp, scale=small[:, 2, n:n + 1]).then_inc(ta_ready, 1)

            for h in range(HEADS):
                act.wait_ge(gate_mm, h + 1)
                act.wait_ge(u_ready, DC)
                for j in range(2):
                    n = 2 * h + j
                    a.activation(Dd[:, n, :], ps[:, 2 * (h % 2), j * T:(j + 1) * T], ACT.Sigmoid,
                                 bias=pcol(PAR_B["ba"] + n)).then_inc(rg_ready, 1)
                    a.activation(vflat[:, n, :], ps[:, 2 * (h % 2) + 1, j * T:(j + 1) * T], ACT.Sigmoid,
                                 bias=pcol(PAR_B["bi"] + n)).then_inc(rg_ready, 1)
                if h == 1:
                    decay(0)
                    decay(1)
            decay(2)
            decay(3)
            ada_back(11)
            for h in range(HEADS):
                act.wait_ge(b2_ready, h + 1)
                a.activation(H[:, 2 * h:2 * h + 2, :], H[:, 2 * h:2 * h + 2, :], ACT.Sqrt, scale=-1.0).then_inc(b_ready, 1)
            norm_squares(3)
            ada_back(12)
            norm_root(3)
            norm_out(3, 9)
            ada_rows(13)
            tokens(1)
            ada_back(13)
            route(1)
            experts(1, None)
            act.wait_ge(fin_mm, 1)
            a.activation(shift_rows[:, :], ps[:, 6:8, :].rearrange("p b n -> p (b n)"), ACT.Copy).then_inc(rows_ready, 1)
            norm_squares(4)
            act.wait_ge(ms_mm, 5)
            a.activation(rs[:, 0:TT], ps[:, 0, 0:TT], ACT.Sqrt, bias=eps[:, 0:1]).then_inc(root_ready, 1)

        @block.vector
        def _(dve):
            v = nc.vector
            link = Link(dve, dve_link)

            dve.wait_ge(consts, 9)
            v.tensor_reduce(sel[:, :], ident[:, 0:P:32], AX.X, ALU.add).then_inc(sel_ready, 1)
            for ch in range(DC):
                dve.wait_ge(x_mm, ch // 2 + 1)
                v.tensor_copy(X[:, ch, :], ps[:, ch // 2, (ch % 2) * T:(ch % 2 + 1) * T]).then_inc(x_ready, 1)

            def params(n, i):
                dve.wait_ge(par_mm, n + 1)
                v.tensor_copy(par[:, i * P:i * P + PAR_TILES[i]],
                              ps[:, 4 + n % 4, 0:PAR_TILES[i]]).then_inc(par_ready, 1)

            params(0, 0)
            dve.wait_ge(csig, 1)
            dve.wait_ge(par_ready, 1)
            link(v.tensor_tensor(small[:, 1, :], small[:, 0, :], pcol(PAR_A["c"], DC), ALU.mult))
            v.tensor_copy(cb32[:, :, :], small[:, 1, :].rearrange("p (c o) -> p c o", o=1).to_broadcast([P, DC, 32])).then_inc(cact, 1)
            for n, i in enumerate((2, 3, 4)):
                params(n + 1, i)

            def ada_rows(part):
                dve.wait_ge(ada_used, 2 * part)
                if part in (7, 11):
                    dve.wait_ge(cols_mm, part - 1 if part == 11 else part)
                for h in range(2):
                    if part in ADA_ALT:
                        dve.wait_ge(ada_alt_landed, 16 * (ADA_ALT.index(part) + 1))
                    else:
                        dve.wait_ge(ada_landed[h], 16 * (ADA_BUF.index(part) + 1))
                    for j in range(4):
                        w = ada_alt[part][:, 4 * h + j, :] if part in ADA_ALT else adabuf[:, h, j, :]
                        ck, acc = small[:, 1, 4 * h + j:4 * h + j + 1], ada_acc(part)
                        if h == j == 0:
                            ins = v.tensor_scalar(acc, w, ck, None, ALU.mult)
                        else:
                            ins = v.scalar_tensor_tensor(out=acc, in0=w, scalar=ck, in1=acc,
                                                         op0=ALU.mult, op1=ALU.add)
                        if j < 3:
                            link(ins)
                        else:
                            ins.then_inc(ada_used, 1)
                            dve.wait_ge(ada_used, 2 * part + h + 1)

            mods = [0]

            def ada_bias(first, last):
                dve.wait_ge(cols_ready, last + 1)
                both = slice(first * DC, (last + 1) * DC)
                v.tensor_tensor(mod[:, both], modraw[:, both], par[:, PAR_ADA + first * DC:PAR_ADA + (last + 1) * DC],
                                ALU.add).then_inc(mod_ready, 1)
                mods[0] += 1
                dve.wait_ge(mod_ready, mods[0])

            def norm_gain(k, gain, sc_part):
                if k >= 1:
                    dve.wait_ge(h_ready, k * DC)
                v.scalar_tensor_tensor(out=gs[:, :], in0=mod[:, sc_part * DC:(sc_part + 1) * DC], scalar=1.0,
                                       in1=pcol(gain, DC), op0=ALU.add, op1=ALU.mult).then_inc(gs_ready, 1)

            def pairs(t):
                return t.rearrange("p (o t) -> p o t", o=1).to_broadcast([P, 2, T])

            def norm_out(k):
                dve.wait_ge(root_ready, k + 1)
                link(v.reciprocal(rs[:, :], rs[:, :]))
                dve.wait_ge(x_ready, (k + 1) * DC)
                for q in range(DC // 2):
                    two = slice(2 * q, 2 * q + 2)
                    v.tensor_tensor(H[:, two, :], X[:, two, :], pairs(rs[:, :]), ALU.mult).then_inc(xn_ready, 1)

            def out_proj(k, g1_part):
                for n in range(DC):
                    dve.wait_ge(o_mm, (k * DC + n) // 2 + 1)
                    dve.wait_ge(xb_ready, k * DC + n + 1)
                    v.scalar_tensor_tensor(out=X[:, n, :], in0=ps[:, n // 2, (n % 2) * T:(n % 2 + 1) * T],
                                           scalar=mcol(g1_part, n), in1=X[:, n, :], op0=ALU.mult,
                                           op1=ALU.add).then_inc(x_ready, 1)

            norm_out(0)

            ada_bias(0, 1)
            norm_gain(0, PAR_A["n1"], 1)

            dve.wait_ge(pad_ready, 1)

            def glu(m):
                dve.wait_ge(sg_ready, m + 1)
                v.scalar_tensor_tensor(out=vconf[:, m, TAPS - 1:], in0=ps[:, m % 4, 0:T], scalar=pcol(PAR_A["b1"] + m),
                                       in1=sg[:, m % 2, :], op0=ALU.add, op1=ALU.mult).then_inc(v_ready, 1)

            before = {}
            for ch, k in conv_order():
                if ch == "GLU":
                    glu(k)
                    continue
                acc = B[:, ch, :]
                if k == 0:
                    dve.wait_ge(v_ready, ch + 1)
                    ins = v.tensor_scalar(acc, vconf[:, ch, 0:T], pcol(dw_col(0, ch)), pcol(PAR_A["dwb"] + ch),
                                          ALU.mult, ALU.add)
                else:
                    dve.wait_ge(dve_link, before[ch])
                    ins = v.scalar_tensor_tensor(out=acc, in0=vconf[:, ch, k:k + T], scalar=pcol(dw_col(k, ch)),
                                                 in1=acc, op0=ALU.mult, op1=ALU.add)
                if k < TAPS - 1:
                    before[ch] = link.post(ins)
                else:
                    ins.then_inc(conv_dve, 1)
            params(4, 1)
            dve.wait_ge(mean_mm, 1)
            for q in range(DC // 2):
                two = slice(2 * q, 2 * q + 2)
                v.tensor_tensor(C[:, two, :], B[:, two, :], pairs(ps[:, 4, 0:T]), ALU.subtract).then_inc(cen_ready, 1)
            dve.wait_ge(ln_root, 1)
            link(v.reciprocal(rs[:, :], rs[:, :]))

            def silu(ch):
                dve.wait_ge(dve_link, affine[ch])
                dve.wait_ge(zs_ready, ch + 1)
                v.tensor_tensor(B[:, ch, :], H[:, ch, :], Dd[:, ch, :], ALU.mult).then_inc(act_in, 1)

            affine = {}
            for q in range(DC // 2):
                two = slice(2 * q, 2 * q + 2)
                v.tensor_tensor(C[:, two, :], C[:, two, :], pairs(rs[:, :]), ALU.mult).then_inc(z_ready, 1)
                dve.wait_ge(z_ready, q + 1)
                for ch in (2 * q, 2 * q + 1):
                    affine[ch] = link.post(v.tensor_scalar(H[:, ch, :], C[:, ch, :], pcol(PAR_A["lng"] + ch),
                                                           pcol(PAR_A["lnb"] + ch), ALU.mult, ALU.add))
                    if q:
                        silu(ch - 2)
            silu(DC - 2)
            silu(DC - 1)
            ada_rows(4)
            dve.wait_ge(par_ready, 5)
            lam = pcol(PAR_B["lam"], DC)
            link(v.tensor_scalar(small[:, 4, :], lam, -1.0, None, ALU.mult))
            v.tensor_tensor(small[:, 2, :], lam, small[:, 4, :], ALU.max).then_inc(nk_in, 1)
            link(v.tensor_scalar(small[:, 6, :], small[:, 4, :], 0.0, None, ALU.max))
            dve.wait_ge(nk_exp, 1)
            v.tensor_scalar(small[:, 4, :], small[:, 3, :], 1.0, None, ALU.add).then_inc(nk_exp, 1)
            dve.wait_ge(nk_exp, 2)
            link(v.tensor_scalar(small[:, 7, :], small[:, 4, :], 1.0, None, ALU.subtract))
            link(v.tensor_scalar(small[:, 0, :], small[:, 7, :], 0.0, None, ALU.is_equal))
            link(v.tensor_tensor(small[:, 7, :], small[:, 7, :], small[:, 0, :], ALU.add))
            link(v.reciprocal(small[:, 7, :], small[:, 7, :]))
            dve.wait_ge(nk_ln, 1)
            link(v.tensor_tensor(small[:, 5, :], small[:, 5, :], small[:, 0, :], ALU.add))
            link(v.tensor_tensor(small[:, 5, :], small[:, 5, :], small[:, 7, :], ALU.mult))
            link(v.tensor_tensor(small[:, 5, :], small[:, 5, :], small[:, 3, :], ALU.mult))
            link(v.tensor_tensor(small[:, 5, :], small[:, 5, :], small[:, 6, :], ALU.add))
            v.tensor_scalar(small[:, 2, :], small[:, 5, :], -8.0, None, ALU.mult).then_inc(nk_ready, 1)
            out_proj(0, 2)
            ada_bias(3, 4)
            norm_gain(1, PAR_A["n2"], 4)
            norm_out(1)

            def picks(lk, io, done):
                first = [lk.post(v.tensor_scalar(pick[:, a, :], io[:], gslot[:, 0, a:a + 1], None, ALU.is_equal))
                         for a in range(TT)]
                for a in range(TT):
                    lk.eng.wait_ge(lk.sem, first[a])
                    ins = v.scalar_tensor_tensor(out=pick[:, a, :], in0=io[:], scalar=gslot[:, 1, a:a + 1],
                                                 in1=pick[:, a, :], op0=ALU.is_equal, op1=ALU.add)
                    if a < TT - 1:
                        last = lk.post(ins)
                        lk.eng.wait_ge(lk.sem, last)
                    else:
                        ins.then_inc(done, 1)

            def route(l, route_ins):
                v.memset(scat, 0.0).then_inc(moe[l].sc, 1)
                dve.sem_inc(moe[l].hid, 1)
                dve.sem_inc(moe[l].dnd, 1)

                def wide(t, n):
                    return t.rearrange("p (a o) -> p a o", o=1).to_broadcast([P, TT, n])

                dve.wait_ge(lg_mm, l + 1)
                link(v.tensor_copy(lg[:, :, :], ps[:, 5, 0:TT * (NG + NE)].rearrange("p (a g) -> p a g", a=TT)))
                gl, el = lg[:, :, 0:NG], lg[:, :, NG:]
                link(v.tensor_reduce(r1[:, 0, :], gl, AX.X, ALU.max))
                v.tensor_tensor(r4[:, 0, :, :], gl, wide(r1[:, 0, :], NG), ALU.subtract).then_inc(ge_in, 1)
                revg = rev[:, NE - NG:].rearrange("p (o n) -> p o n", o=1).to_broadcast([P, TT, NG])
                reve = rev[:, :].rearrange("p (o n) -> p o n", o=1).to_broadcast([P, TT, NE])
                link(v.tensor_tensor(r4[:, 2, :, :], gl, wide(r1[:, 0, :], NG), ALU.is_equal))
                link(v.tensor_tensor(r4[:, 2, :, :], r4[:, 2, :, :], revg, ALU.mult))
                link(v.tensor_reduce(r1[:, 1, :], r4[:, 2, :, :], AX.X, ALU.max))
                link(v.tensor_tensor(r4[:, 2, :, :], r4[:, 2, :, :], wide(r1[:, 1, :], NG), ALU.is_equal))
                for a in range(TT):
                    gsel = r4[:, 2, a, :].rearrange("p (g o) -> p g o", o=1).to_broadcast([P, NG, EPG])
                    link(v.tensor_tensor(r32[:, 0, a, :].rearrange("p (g e) -> p g e", g=NG),
                                         lg[:, a, NG:].rearrange("p (g e) -> p g e", g=NG), gsel, ALU.mult))
                    link(v.tensor_scalar(r32[:, 1, a, :].rearrange("p (g e) -> p g e", g=NG), gsel, 1.0, BIG,
                                         ALU.subtract, ALU.mult))
                link(v.tensor_tensor(r32[:, 0, :, :], r32[:, 0, :, :], r32[:, 1, :, :], ALU.add))
                for k in range(2):
                    hot = r32[:, 2 + k, :, :]
                    link(v.tensor_reduce(r1[:, 2 + k, :], r32[:, 0, :, :], AX.X, ALU.max))
                    link(v.tensor_tensor(hot, r32[:, 0, :, :], wide(r1[:, 2 + k, :], NE), ALU.is_equal))
                    link(v.tensor_tensor(hot, hot, reve, ALU.mult))
                    link(v.tensor_reduce(r1[:, 4, :], hot, AX.X, ALU.max))
                    link(v.tensor_tensor(hot, hot, wide(r1[:, 4, :], NE), ALU.is_equal))
                    if k == 0:
                        link(v.scalar_tensor_tensor(out=r32[:, 0, :, :], in0=hot, scalar=-3 * BIG, in1=r32[:, 0, :, :],
                                                    op0=ALU.mult, op1=ALU.add))
                v.tensor_tensor(r32[:, 4, :, :], r32[:, 2, :, :], r32[:, 3, :, :], ALU.add).then_inc(mask_ready, 1)
                v.tensor_tensor(r1[:, 5, :], r1[:, 3, :], r1[:, 2, :], ALU.subtract).then_inc(ge_in, 1)
                dve.wait_ge(rank_mm, l + 1)
                link(v.tensor_copy(cnt[:, 0, :], ps[:, 5, 2 * NE + P:3 * NE + P]))
                cw = cmp3[:, 0:NE, 0:T // SLOTS]
                link(v.tensor_tensor(cw, cnt[:, 0, :].rearrange("p (e o) -> p e o", o=1).to_broadcast([P, NE, T // SLOTS]),
                                     thr[:, :].rearrange("p (o n) -> p o n", o=1).to_broadcast([P, NE, T // SLOTS]), ALU.is_gt))
                link(v.tensor_reduce(cnt[:, 1, :], cw, AX.X, ALU.add))
                link(v.tensor_tensor_scan(cnt[:, 2, :], ones[:, 0:NE], cnt[:, 1, :], 0.0, ALU.mult, ALU.add))
                link(v.tensor_tensor(cnt[:, 3, :], cnt[:, 2, :], cnt[:, 1, :], ALU.subtract))
                for a in range(TT):
                    link(v.scalar_tensor_tensor(out=r32[:, 5, a, :], in0=cnt[:, 3, :], scalar=float(SLOTS),
                                                in1=ps[:, 5, P + a * NE:P + (a + 1) * NE], op0=ALU.mult, op1=ALU.add))
                hits = [link.post(v.tensor_tensor(r32[:, k, :, :], r32[:, 5, :, :], r32[:, 2 + k, :, :], ALU.mult))
                        for k in range(2)]
                for k in range(2):
                    dve.wait_ge(dve_link, hits[k])
                    slots = link.post(v.tensor_reduce(gslot[:, k, :], r32[:, k, :, :], AX.X, ALU.add))
                dve.wait_ge(dve_link, slots)
                picks(route_ins, iota0, moe[l].pick)
                link(v.tensor_tensor(cmp3[:, :, :], cnt[:, 2, :].rearrange("p (o e) -> p o e", o=1).to_broadcast([P, 2 * MAXP, NE]),
                                     blk[:, :].rearrange("p (b o) -> p b o", o=1).to_broadcast([P, 2 * MAXP, NE]), ALU.is_le))
                link(v.tensor_reduce(tabf[:, 0:2 * MAXP], cmp3[:, :, :], AX.X, ALU.add))
                link(v.tensor_scalar(tabf[:, 0:2 * MAXP], tabf[:, 0:2 * MAXP], float(NE - 1), None, ALU.min))
                there, other = tabf[:, 2 * MAXP:4 * MAXP], tabf[:, 4 * MAXP:]
                link(v.tensor_scalar(there, blk[:, :], cnt[:, 2, NE - 1:NE], None, ALU.is_lt))
                link(v.tensor_tensor(other, tabf[:, 0:2 * NSUB], blk[:, 0:2 * NSUB], ALU.not_equal))
                link(v.tensor_tensor(other, there[:, 0:2 * NSUB], other, ALU.mult))
                link(v.tensor_copy(tab[0:1, TAB:], tabf[0:1, :]))
                link(v.tensor_scalar(tabf[:, 0:MAXP], blk[:, 0:2 * MAXP:2], cnt[:, 2, NE - 1:NE], None, ALU.is_lt))
                link(v.tensor_reduce(tabf[:, MAXP:MAXP + 1], tabf[:, 0:MAXP], AX.X, ALU.add))
                v.tensor_copy(tab[0:1, 0:1], tabf[0:1, MAXP:MAXP + 1]).then_inc(route_ready, 1)

            def experts(l, route_ins, part):
                m = moe[l]
                dve.wait_ge(m.gath, 1)
                v.tensor_copy(xg[:, 4:8, :], ps[:, 7, :].rearrange("p (k s) -> p k s", k=4)).then_inc(m.xgd, 1)
                dve.wait_ge(ge_ready, 2 * l + 1)
                link(v.tensor_reduce(r1[:, 6, :], r4[:, 1, :, :], AX.X, ALU.add))
                dve.wait_ge(ge_ready, 2 * l + 2)
                e2 = r1[:, 7, :]
                link(v.tensor_scalar(r1[:, 8, :], e2, 1.0, None, ALU.add))
                link(v.tensor_tensor(r1[:, 8, :], r1[:, 8, :], r1[:, 6, :], ALU.mult))
                link(v.reciprocal(gw[:, 0, :], r1[:, 8, :]))
                link(v.tensor_tensor(gw[:, 1, :], gw[:, 0, :], e2, ALU.mult))
                ada_bias(*((5, 6), (11, 13))[l])
                if l == 1:
                    norm_gain(4, PAR_A["fin"], 13)
                dve.wait_ge(route_ready, l + 1)
                passes = dve.value_load(tab[0:1, 0:1], min_val=MINP, max_val=MAXP)
                n0 = route_ins.n

                def turn(i):
                    lk = Link(dve, m.link, i * EXPERT_LINKS + n0)
                    dve.wait_ge(m.pick, i + 1)
                    dve.wait_ge(m.gath, i + 1)
                    picks(lk, iota1, m.pick)
                    dve.wait_ge(m.sc, i + 1)
                    for a in range(TT):
                        for k, dst in ((0, gate1), (1, gate2)):
                            lk(v.tensor_scalar(dst[:, a, :], iota0[:], gslot[:, k, a:a + 1], gw[:, k, a:a + 1],
                                               ALU.is_equal, ALU.mult))
                    v.tensor_tensor(gate1[:, :, :], gate1[:, :, :], gate2[:, :, :], ALU.add).then_inc(m.gate, 1)
                    dve.wait_ge(m.pick, i + 2)
                    lk(v.tensor_scalar(gslot[:, :, :], gslot[:, :, :], float(P), None, ALU.subtract))
                    if isinstance(i, int) and part is not None:
                        ada_rows(part)
                    dve.wait_ge(m.sig, i + 1)
                    lk(v.tensor_tensor(hid, ps[:, 4, :], sigb, ALU.mult))
                    dve.wait_ge(m.used[3], i + 2)
                    v.tensor_tensor(hid, hid, ps[:, 5, :], ALU.mult).then_inc(m.hid, 1)
                    dve.wait_ge(m.gath, i + 2)
                    v.tensor_copy(xg[:, 4:8, :], ps[:, 7, :].rearrange("p (k s) -> p k s", k=4)).then_inc(m.xgd, 1)
                    dve.wait_ge(m.sc_mm, i + 1)
                    v.tensor_copy(scat[:, :], ps[:, 5, 0:T]).then_inc(m.sc, 1)
                    dve.wait_ge(m.used[5], i + 2)
                    v.tensor_copy(dn[:, 512:1024], ps[:, 7, :]).then_inc(m.dnd, 1)
                    assert lk.n == EXPERT_LINKS, lk.n

                turn(0)
                with dve.Fori(1, passes) as i:
                    turn(i)
                g2 = 6 * l + 5
                for ch in range(DC):
                    dve.wait_ge(m.y, ch // 2 + 1)
                    v.scalar_tensor_tensor(out=X[:, ch, :], in0=ps[:, ch // 2, (ch % 2) * T:(ch % 2 + 1) * T],
                                           scalar=mcol(g2, ch), in1=X[:, ch, :], op0=ALU.mult,
                                           op1=ALU.add).then_inc(x_ready, 1)

            route_link = Link(dve, moe[0].link)
            route(0, route_link)
            experts(0, route_link, 7)

            dve.memset(vlru[:, :, 0:LTAPS - 1], 0.0).then_inc(pad_ready, 1)
            ada_bias(7, 7)
            norm_gain(2, PAR_A["n1"] + DC, 7)
            norm_out(2)
            ada_rows(9)
            ada_rows(10)
            for q in range(DC // 2):
                before = {}
                for k in range(LTAPS):
                    for n in (2 * q, 2 * q + 1):
                        acc = C[:, n, :]
                        if k == 0:
                            dve.wait_ge(ux_ready, n + 1)
                            ins = v.tensor_scalar(acc, vlru[:, n, 0:T], pcol(PAR_B["cw"] + n), pcol(PAR_B["cb"] + n),
                                                  ALU.mult, ALU.add)
                        else:
                            dve.wait_ge(dve_link, before[n])
                            ins = v.scalar_tensor_tensor(out=acc, in0=vlru[:, n, k:k + T], scalar=pcol(PAR_B["cw"] + k * DC + n),
                                                         in1=acc, op0=ALU.mult, op1=ALU.add)
                        if k < LTAPS - 1:
                            before[n] = link.post(ins)
                        else:
                            ins.then_inc(u_ready, 1)
            ada_rows(11)
            dve.wait_ge(y_ready, DC // 2)
            for h in range(HEADS):
                two = slice(2 * h, 2 * h + 2)
                t = H[:, two, :]
                dve.wait_ge(ta_ready, 4 * h + 4)
                link(v.tensor_tensor(sg[:, :, :], Dd[:, two, :], Dd[:, two, :], ALU.mult))
                v.scalar_tensor_tensor(out=t, in0=sg[:, :, :], scalar=1.0, in1=t, op0=ALU.add,
                                       op1=ALU.mult).then_inc(b2_ready, 1)
                dve.wait_ge(b2_ready, h + 1)
            for h in range(HEADS):
                two = slice(2 * h, 2 * h + 2)
                t = H[:, two, :]
                dve.wait_ge(b_ready, h + 1)
                dve.wait_ge(iu_ready, h + 1)
                link(v.tensor_tensor(t, t, vflat[:, two, :], ALU.mult))
                states = [link.post(v.tensor_tensor_scan(vflat[:, n, :], Dd[:, n, :], H[:, n, :], 0.0, ALU.mult, ALU.add))
                          for n in (2 * h, 2 * h + 1)]
                for n in (2 * h, 2 * h + 1):
                    dve.wait_ge(dve_link, states[n % 2])
                    v.tensor_tensor(B[:, n, :], B[:, n, :], vflat[:, n, :], ALU.mult).then_inc(hs_ready, 1)
            dve.wait_ge(hs_ready, DC)
            ada_rows(12)
            ada_bias(9, 10)
            norm_gain(3, PAR_A["n2"] + DC, 10)
            out_proj(1, 8)
            norm_out(3)
            route_link = Link(dve, moe[1].link)
            route(1, route_link)
            experts(1, route_link, None)
            dve.wait_ge(root_ready, 5)
            link(v.reciprocal(rs[:, 0:TT], rs[:, 0:TT]))
            dve.wait_ge(rows_ready, 15 - len(ADA_DVE))
            for a in range(TT):
                for n in range(2):
                    if n == 0:
                        dve.wait_ge(fin_mm, a + 2)
                    v.scalar_tensor_tensor(out=htok[:, a, n * 512:(n + 1) * 512], in0=ps[:, 4 + 2 * a + n, :],
                                           scalar=rs[:, a:a + 1], in1=shift_rows[:, n * 512:(n + 1) * 512],
                                           op0=ALU.mult, op1=ALU.add).then_inc(out_ready, 1)

        @block.tensor
        def _(pe):
            mm = nc.tensor.matmul
            kw = dict(skip_group_check=True)
            pe.wait_ge(consts, 9)
            pe.wait_ge(s_x, 16)
            for ch in range(DC):
                for a in range(TT):
                    last = mm(ps[:, ch // 2, (ch % 2) * T + a * P:(ch % 2) * T + (a + 1) * P],
                              xin[:, a, ch * P:(ch + 1) * P], ident[:], start=True, stop=True, **kw)
                if ch % 2:
                    last.then_inc(x_mm, 1)

            def params(q, i):
                n = PAR_TILES[i]
                pe.wait_ge(s_par[i], 16 * PAR_DMAS[i])
                mm(ps[:, 4 + q % 4, 0:n], ptile[i][0:n, :], ident[0:n, 0:n],
                   start=True, stop=True).then_inc(par_mm, 1)

            params(0, 0)
            def ada_sum(part):
                if part == 0:
                    pe.wait_ge(cact, 1)
                else:
                    pe.wait_ge(cols_ready, part)
                for h in range(2):
                    if part in ADA_ALT:
                        pe.wait_ge(ada_alt_landed, 16 * (ADA_ALT.index(part) + 1))
                    else:
                        pe.wait_ge(ada_landed[h], 16 * (ADA_BUF.index(part) + 1))
                    for n in range(2):
                        for j in range(4):
                            w = ada_alt[part][:, 4 * h + j, :] if part in ADA_ALT else adabuf[:, h, j, :]
                            last = mm(ps[32 * j:32 * j + 32, 6 + n, :], cb32[:, 4 * h + j, :],
                                      w[:, n * 512:(n + 1) * 512], start=(h == 0), stop=(h == 1), **kw)
                    last.then_inc(ada_used, 1)

            def ada_cols(part):
                if part in ADA_DVE:
                    pe.wait_ge(ada_used, 2 * part + 2)
                    pe.wait_ge(cols_ready, part)
                else:
                    pe.wait_ge(rows_ready, part + 1 - sum(p < part for p in ADA_DVE))
                rows, by = (ada_acc(part), ones[:, 0:1]) if part in ADA_DVE else (rowsum, sel[:, :])
                if part == 0:
                    pe.wait_ge(sel_ready, 1)
                for ch in range(DC):
                    last = mm(ps[:, 6, ch:ch + 1], rows[:, ch * P:(ch + 1) * P], by, start=True, stop=True, **kw)
                last.then_inc(cols_mm, 1)

            def ada(part):
                ada_sum(part)
                ada_cols(part)

            def mean_square(k, ch):
                pe.wait_ge(sq_ready, k * DC + ch + 1)
                last = mm(ps[:, 4, 0:T], onesd[:], H[:, ch, :], start=(ch == 0), stop=(ch == DC - 1), **kw)
                if ch == DC - 1:
                    last.then_inc(ms_mm, 1)

            def norm(k):
                for ch in range(DC):
                    mean_square(k, ch)

            def proj(bank, off, w, col, src, ready=None, base=0):
                for k in range(DC):
                    if ready is not None:
                        pe.wait_ge(ready, base + k + 1)
                    last = mm(ps[:, bank, off:off + T], w[:, k, col:col + P], src[:, k, :],
                              start=(k == 0), stop=(k == DC - 1), **kw)
                return last

            def proj_all(w, src, ready, base, done, free=None, between=None, after=None):
                for k in range(DC // 2):
                    pe.wait_ge(ready, base + k + 1)
                    for n in range(DC):
                        if k == 0 and n % 2 == 0 and free is not None:
                            pe.wait_ge(free, n + 2)
                        mm(ps[:, n // 2, (n % 2) * T:(n % 2 + 1) * T], w[:, k, n * P:(n + 1) * P], src[:, k, :],
                           start=(k == 0 and n % 2 == 0), stop=False, **kw)
                if between is not None:
                    between()
                pe.wait_ge(ready, base + DC)
                for n in range(DC):
                    for k in range(DC // 2, DC):
                        last = mm(ps[:, n // 2, (n % 2) * T:(n % 2 + 1) * T], w[:, k, n * P:(n + 1) * P], src[:, k, :],
                                  start=False, stop=(k == DC - 1), **kw)
                    if n % 2:
                        last.then_inc(done, 1)
                        if after is not None and n > 1:
                            after(n - 3)
                            after(n - 2)
                if after is not None:
                    after(DC - 2)
                    after(DC - 1)

            pe.wait_ge(par_ready, 1)
            norm(0)
            for q, i in enumerate((2, 3, 4)):
                params(q + 1, i)
            pe.wait_ge(par_ready, 4)
            ada(0)
            ada(1)

            for m in range(DC):
                pe.wait_ge(side_landed[m // 2], 32)
                if m >= 4:
                    pe.wait_ge(v_ready, m - 3)
                proj(m % 4, 0, w1, m * P, H, h_ready if m == 0 else None)
                proj(m % 4, T, w1, D + m * P, H).then_inc(glu_mm, 1)
            pe.wait_ge(root_ready, 1)
            params(4, 1)
            ada_sum(2)
            pe.wait_ge(v_ready, PE_CHUNK + 1)
            for k in range(TAPS):
                pe.wait_ge(diag_ready, k + 1)
                last = mm(ps[:, 5, 0:T], diag[k], vconf[:, PE_CHUNK, k:k + T], start=(k == 0), stop=(k == TAPS - 1), **kw)
            last.then_inc(conv_mm, 1)
            ada_cols(2)
            pe.wait_ge(par_ready, 5)
            for n, ch in enumerate((*DVE_CHUNKS[:-2], *POOL_CHUNKS, PE_CHUNK, *DVE_CHUNKS[-2:])):
                if ch in DVE_CHUNKS:
                    pe.wait_ge(conv_dve, DVE_CHUNKS.index(ch) + 1)
                elif ch in POOL_CHUNKS:
                    pe.wait_ge(conv_pool, (TAPS - 1) * (POOL_CHUNKS.index(ch) + 1))
                else:
                    pe.wait_ge(conv_pe, 1)
                last = mm(ps[:, 4, 0:T], onesd[:], B[:, ch, :], start=(n == 0), stop=(n == DC - 1), **kw)
            last.then_inc(mean_mm, 1)
            for ch in range(DC):
                pe.wait_ge(csq_ready, ch // 2 + 1)
                last = mm(ps[:, 5, T:2 * T], onesd[:], Dd[:, ch, :], start=(ch == 0), stop=(ch == DC - 1), **kw)
            last.then_inc(var_mm, 1)
            ada_sum(3)
            pe.wait_ge(s_w2, 16)
            proj_all(w2, B, act_in, 0, o_mm, between=lambda: ada_cols(3), after=lambda ch: mean_square(1, ch))
            ada_cols(4)

            def route(l):
                ada_sum((5, 13)[l])
                pe.wait_ge(s_router, 16 * 6)
                pe.wait_ge(x_ready, DC * (2 * l + 2))
                logits = [ps[:, 5, a * (NG + NE):(a + 1) * (NG + NE)] for a in range(TT)]
                for k in range(DC):
                    pe.wait_ge(h_ready, DC * (2 * l + 1) + k + 1)
                    for a in range(TT):
                        mm(logits[a], H[:, k, a * P:(a + 1) * P], wgr[:, l, k, :], start=(k == 0 and a == 0), stop=False, **kw)
                for a in range(TT):
                    last = mm(logits[a], ones[0:1, :], brow[0:1, l, :], start=False, stop=True, **kw)
                last.then_inc(lg_mm, 1)
                for a in range(TT):
                    for ch in range(DC):
                        last = mm(ps[:, 2 * a + ch // 4, (ch % 4) * P:(ch % 4 + 1) * P], H[:, ch, a * P:(a + 1) * P],
                                  ident[:], start=True, stop=True, **kw)
                last.then_inc(ht_mm, 1)
                ada_cols((5, 13)[l])
                if l == 0:
                    ada_sum(6)
                pe.wait_ge(mask_ready, l + 1)
                mask = r32[:, 4, :, :]
                mm(ps[:, 5, P:P + NE], upper[:], mask[:, 0, :], start=True, stop=True, **kw)
                mm(ps[:, 5, P + NE:P + 2 * NE], ones[:], mask[:, 0, :], start=True, stop=False, **kw)
                mm(ps[:, 5, P + NE:P + 2 * NE], upper[:], mask[:, 1, :], start=False, stop=True, **kw)
                mm(ps[:, 5, P + 2 * NE:P + 3 * NE], ones[:], mask[:, 0, :], start=True, stop=False, **kw)
                mm(ps[:, 5, P + 2 * NE:P + 3 * NE], ones[:], mask[:, 1, :], start=False, stop=True, **kw).then_inc(rank_mm, 1)
                if l == 0:
                    ada_cols(6)

            def experts(l, part):
                m = moe[l]
                for ph in range(6):
                    pe.sem_inc(m.used[ph], 1)
                pe.wait_ge(ht_act, TT * (l + 1))

                def gather(n):
                    pe.wait_ge(m.pick, n)
                    for k in range(DC):
                        for a in range(TT):
                            last = mm(ps[:, 6 + k // 4, (k % 4) * P:(k % 4 + 1) * P], htok[:, a, k:D:DC],
                                      pick[:, a, :], start=(a == 0), stop=(a == TT - 1), **kw)
                    last.then_inc(m.gath, 1)

                def scatter(done=None):
                    for ch in range(DC):
                        last = mm(ps[:, ch // 2, (ch % 2) * T:(ch % 2 + 1) * T], dn[:, ch * P:(ch + 1) * P],
                                  scat[:, :], start=False, stop=False, **kw)
                        if done is not None and ch % 2:
                            last.then_inc(done, 1)

                pe.wait_ge(cols_ready, (7, 14)[l])
                gather(1)
                pe.wait_ge(m.sc, 1)
                for b in range(4):
                    mm(ps[:, b, :], scat[:, 0:P], htok[:, 0, 0:512], start=True, stop=False, **kw)
                pe.wait_ge(route_ready, l + 1)
                passes = pe.value_load(tab[0:1, 0:1], min_val=MINP, max_val=MAXP)

                def turn(i):
                    pe.wait_ge(m.xga, i + 1)
                    pe.wait_ge(m.xgd, i + 1)
                    pe.wait_ge(m.sc, i + 1)
                    for ph in range(4):
                        bank, h = 4 + ph // 2, ph % 2
                        aside = isinstance(i, int) and i == 1 and ph < ASIDE[l]
                        w = []
                        for j in range(NSUB):
                            slot = ph * NSUB + j
                            if aside:
                                if ph < 2:
                                    pe.wait_ge(side_landed[slot], 16 * (2 * l + 4))
                                elif j == 0:
                                    pe.wait_ge(ada_landed[ph - 2], up_aside[1])
                                w.append(second[slot])
                            else:
                                pe.wait_ge(m.landed[slot], (i + 1 if not isinstance(i, int) and ph < ASIDE[l] else i + 2) * 16)
                                w.append(wbuf[:, slot * 2048:(slot + 1) * 2048])
                        for k in range(4):
                            for j in range(NSUB):
                                last = mm(ps[SLOTS * j:SLOTS * (j + 1), bank, :],
                                          xg[:, 4 * h + k, SLOTS * j:SLOTS * (j + 1)], w[j][:, k * F:(k + 1) * F],
                                          start=(h == 0 and k == 0), stop=(h == 1 and k == 3), **kw)
                        last.then_inc(m.used[ph], 1)
                    if isinstance(i, int) and i == 0 and part is not None:
                        ada_cols(part)
                        pe.wait_ge(cols_ready, part + 1)
                    pe.wait_ge(m.dna, i + 1)
                    pe.wait_ge(m.dnd, i + 1)
                    gather(i + 2)
                    if not (isinstance(i, int) and i == 0):
                        scatter()
                    pe.wait_ge(m.hid, i + 2)
                    for k in range(FC):
                        last = mm(ps[:, 4, k * P:(k + 1) * P], hid[:, k:F:FC], ident[:], start=True, stop=True, **kw)
                    last.then_inc(m.ht_mm, 1)
                    pe.wait_ge(m.gate, i + 1)
                    for a in range(TT):
                        last = mm(ps[:, 5, a * P:(a + 1) * P], gate1[:, a, :], ident[:], start=True, stop=True, **kw)
                    last.then_inc(m.sc_mm, 1)
                    pe.wait_ge(m.ht, i + 1)
                    pe.wait_ge(m.xga, i + 2)
                    pe.wait_ge(m.xgd, i + 2)
                    for h in range(2):
                        for j in range(NSUB):
                            pe.wait_ge(m.landed[(4 + h) * NSUB + j], (i + 2) * 16)
                        for k in range(2):
                            for n in range(2):
                                for j in range(NSUB):
                                    o = ((4 + h) * NSUB + j) * 2048 + k * D + n * 512
                                    last = mm(ps[SLOTS * j:SLOTS * (j + 1), 6 + n, :],
                                              hidT[:, 2 * h + k, SLOTS * j:SLOTS * (j + 1)], wbuf[:, o:o + 512],
                                              start=(h == 0 and k == 0), stop=(h == 1 and k == 1), **kw)
                        last.then_inc(m.used[4 + h], 1)

                turn(0)
                turn(1)
                with pe.Fori(2, passes) as i:
                    turn(i)
                pe.wait_ge(m.sc, passes + 1)
                pe.wait_ge(m.dna, passes + 1)
                pe.wait_ge(m.dnd, passes + 1)
                scatter(m.y)

            route(0)
            experts(0, 7)

            norm(2)
            ada_sum(8)
            pe.wait_ge(s_wy, 16)
            proj_all(rgw[0], H, h_ready, 2 * DC, q_mm, between=lambda: ada_cols(8))
            pe.wait_ge(s_wx, 16)
            proj_all(rgw[1], H, h_ready, 2 * DC, ux_mm, free=q_ready, between=lambda: ada_cols(9))
            ada_cols(10)
            pe.wait_ge(s_wab, 32)
            for h in range(HEADS):
                pe.wait_ge(u_ready, 2 * h + 2)
                if h < 2:
                    pe.wait_ge(ux_ready, 4 * h + 4)
                else:
                    pe.wait_ge(rg_ready, 4 * (h - 1))
                for w in range(2):
                    for j in range(2):
                        for k in range(2):
                            last = mm(ps[:, 2 * (h % 2) + w, j * T:(j + 1) * T], wab[:, w, h, k, j * P:(j + 1) * P],
                                      C[:, 2 * h + k, :], start=(k == 0), stop=(k == 1), **kw)
                last.then_inc(gate_mm, 1)
            ada_cols(11)
            pe.wait_ge(s_wo, 16)
            pe.wait_ge(rg_ready, 4 * HEADS)
            proj_all(rgw[2], B, hs_ready, 0, o_mm, after=lambda ch: mean_square(3, ch))
            ada_cols(12)
            route(1)
            experts(1, None)
            pe.wait_ge(diag_ready, TAPS + 2 * DC)
            for ch in range(DC):
                last = mm(ps[:, 6 + ch // 4, (ch % 4) * P:(ch % 4 + 1) * P], ones[:], shift_diag[:, ch, :],
                          start=True, stop=True, **kw)
            last.then_inc(fin_mm, 1)
            for ch in range(DC):
                pe.wait_ge(x_ready, 4 * DC + ch + 1)
                if ch == 0:
                    pe.wait_ge(rows_ready, 15 - len(ADA_DVE))
                for a in range(TT):
                    last = mm(ps[:, 4 + 2 * a + ch // 4, (ch % 4) * P:(ch % 4 + 1) * P], X[:, ch, a * P:(a + 1) * P],
                              gain_diag[:, ch, :], start=True, stop=True, **kw)
                    if ch == DC - 1:
                        last.then_inc(fin_mm, 1)
            pe.wait_ge(x_ready, 5 * DC)
            for ch in range(DC):
                pe.wait_ge(sq_ready, 4 * DC + ch + 1)
                for a in range(TT):
                    last = mm(ps[:, 0, a:a + 1], H[:, ch, a * P:(a + 1) * P], onesd[:, 0:1],
                              start=(ch == 0 and a == 0), stop=(ch == DC - 1), **kw)
            last.then_inc(ms_mm, 1)


PAR_DMAS = (9, 8, 2, 1, 1)
EXPERT_LINKS = 9
DVE_CHUNKS, POOL_CHUNKS, PE_CHUNK = (0, 1, 3, 5, 6), (2, 4), 7
PRODUCTS = 10
GLU_EVERY, GLU_AHEAD = 18, 3
ADA_DVE = (4, 7, 9, 10, 11, 12)
ASIDE = (2, 4)
ADA_ALT = (1, 3, 11)
ADA_BUF = tuple(part for part in range(14) if part not in ADA_ALT)
DMA_SCRATCH = 1024


_INS = ["x", "c", "ada_w", "ada_b", "norm1_g", "norm2_g", "cm_w1", "cm_b1", "cm_dw", "cm_dwb", "cm_ln_g",
        "cm_ln_b", "cm_w2", "cm_b2", "rg_wy", "rg_by", "rg_wx", "rg_bx", "rg_cw", "rg_cb", "rg_wa", "rg_ba",
        "rg_wi", "rg_bi", "rg_lambda", "rg_wo", "rg_bo", "moe_wg", "moe_bg", "moe_wr", "moe_br", "moe_w_gate",
        "moe_w_up", "moe_w_down", "fin_ada_w", "fin_ada_b", "fin_g"]


def kernel(**inputs):
    import numpy as _np
    import concourse.bacc as _bacc
    from concourse import mybir as _mybir
    from concourse.bass_utils import run_bass_kernel_spmd as _run

    nc = _bacc.Bacc("TRN2", target_bir_lowering=False, num_devices=1, dynamic_dma_scratch_size=DMA_SCRATCH)
    arrays, args = {}, []
    for name in _INS:
        a = _np.ascontiguousarray(inputs[name])
        arrays[f"in_{name}"] = a
        args.append(nc.dram_tensor(f"in_{name}", a.shape, _mybir.dt.from_np(a.dtype), kind="ExternalInput").ap())
    args.append(nc.dram_tensor("out_0", (1, T, D), F32, kind="ExternalOutput").ap())
    trunk(nc, *args)
    r = _run(nc, [arrays], core_ids=[0])
    return r.results[0]["out_0"]
```
